# Optimizing a Trainium2 kernel written in Bass

```python
import math
import jax, jax.numpy as jnp
from jax import lax
import numpy as np

D_MODEL = 1024
BATCH = 1
SEQ = 256
DEPTH = 2

ATT_Q_HEADS = 8
ATT_KV_HEADS = 2
ATT_HEAD_DIM = 64
WINDOW = 128
ATT_BLOCK = 128
REL_BUCKETS = 32
REL_MAX_DIST = 128
HG_HEADS = 4
HG_DK = 128
HG_DV = 128
HG_CHUNK = 16
ATT_Q_W = ATT_Q_HEADS * ATT_HEAD_DIM
ATT_KV_W = ATT_KV_HEADS * ATT_HEAD_DIM
HG_K_W = HG_HEADS * HG_DK
HG_V_W = HG_HEADS * HG_DV
IN_SPLITS = (ATT_Q_W, ATT_KV_W, ATT_KV_W, HG_K_W, HG_K_W, HG_V_W, HG_V_W, D_MODEL, D_MODEL)
IN_WIDTH = sum(IN_SPLITS)
FFN_DENSE = 2816
N_EXPERTS = 8
TOP_K = 2
FFN_EXPERT = 3584
N_DENSE = (DEPTH + 1) // 2
N_MOE = DEPTH // 2
PLE_DIM = 256
EPS = 1e-6

kernel_name = 'hybrid_swa_hgrn2_moe_ple_trunk'

def _rmsnorm(x, g):
    xf = x.astype(jnp.float32)
    y = xf * lax.rsqrt(jnp.mean(xf * xf, axis=-1, keepdims=True) + EPS)
    return (y * g.astype(jnp.float32)).astype(x.dtype)

def _t5_bucket(dist):
    max_exact = REL_BUCKETS // 2
    d = jnp.maximum(dist, 0)
    large = max_exact + (jnp.log(jnp.maximum(d, 1).astype(jnp.float32) / max_exact)
                         / math.log(REL_MAX_DIST / max_exact)
                         * (REL_BUCKETS - max_exact)).astype(jnp.int32)
    large = jnp.minimum(large, REL_BUCKETS - 1)
    return jnp.where(d < max_exact, d, large)

def _split(z):
    outs = []
    off = 0
    for w in IN_SPLITS:
        outs.append(z[..., off:off + w])
        off += w
    return outs

def _sliding_window_attention(q, k, v, sinks, band_bias):
    B, S = q.shape[0], q.shape[1]
    nb = S // ATT_BLOCK
    G = ATT_Q_HEADS // ATT_KV_HEADS
    qb = q.reshape(B, nb, ATT_BLOCK, ATT_KV_HEADS, G, ATT_HEAD_DIM)

    def band(t):
        tp = jnp.pad(t, ((0, 0), (ATT_BLOCK, 0), (0, 0), (0, 0)))
        tb = tp.reshape(B, nb + 1, ATT_BLOCK, ATT_KV_HEADS, ATT_HEAD_DIM)
        return jnp.concatenate([tb[:, :-1], tb[:, 1:]], axis=2)

    kb, vb = band(k), band(v)
    s = jnp.einsum('bnqhgd,bnkhd->bnhgqk', qb, kb).astype(jnp.float32) * (ATT_HEAD_DIM ** -0.5)
    s = s + band_bias.astype(jnp.float32).reshape(ATT_KV_HEADS, G, ATT_BLOCK, 2 * ATT_BLOCK)
    qi = jnp.arange(ATT_BLOCK)[:, None]
    kj = jnp.arange(2 * ATT_BLOCK)[None, :]
    dist = qi + ATT_BLOCK - kj
    kpos = jnp.arange(nb)[:, None, None] * ATT_BLOCK - ATT_BLOCK + kj
    valid = (dist >= 0) & (dist < WINDOW) & (kpos >= 0)
    s = jnp.where(valid[None, :, None, None], s, -1e30)
    sink = sinks.astype(jnp.float32).reshape(ATT_KV_HEADS, G)[None, None, :, :, None, None]
    m = jnp.maximum(jnp.max(s, axis=-1, keepdims=True), sink)
    pr = jnp.exp(s - m)
    denom = jnp.sum(pr, axis=-1, keepdims=True) + jnp.exp(sink - m)
    pr = (pr / denom).astype(v.dtype)
    o = jnp.einsum('bnhgqk,bnkhd->bnqhgd', pr, vb)
    return o.reshape(B, S, ATT_Q_W)

def _hgrn2(q, f_logit, v, g, lb, norm_g):
    B, S = q.shape[0], q.shape[1]
    nc = S // HG_CHUNK
    dt = q.dtype
    lbh = lb.astype(jnp.float32).reshape(HG_HEADS, HG_DK)
    f = lbh + (1.0 - lbh) * jax.nn.sigmoid(f_logit.astype(jnp.float32))
    log_f = jnp.log(f)
    k = 1.0 - f

    def chunk(t):
        return t.reshape(B, nc, HG_CHUNK, HG_HEADS, t.shape[-1])

    qc, kc, vc = chunk(q.astype(jnp.float32)), chunk(k), chunk(v.astype(jnp.float32))
    A = jnp.cumsum(chunk(log_f), axis=2)
    A_last = A[:, :, -1:]
    q_dec = qc * jnp.exp(A)
    k_in = kc * jnp.exp(-A)
    k_end = kc * jnp.exp(A_last - A)
    causal = jnp.tril(jnp.ones((HG_CHUNK, HG_CHUNK), dtype=bool))
    P = jnp.where(causal, jnp.einsum('bnthd,bnshd->bnhts', q_dec, k_in), 0.0)
    o_intra = jnp.einsum('bnhts,bnshe->bnthe', P, vc)
    decay = jnp.exp(A_last[:, :, 0])

    def step(state, inp):
        qd, ke, vv, a = inp
        o_int = jnp.einsum('bthd,bhde->bthe', qd, state)
        state = a[..., None] * state + jnp.einsum('bshd,bshe->bhde', ke, vv)
        return state, o_int

    s0 = jnp.zeros((B, HG_HEADS, HG_DK, HG_DV), jnp.float32)
    xs = (jnp.moveaxis(q_dec, 1, 0), jnp.moveaxis(k_end, 1, 0),
          jnp.moveaxis(vc, 1, 0), jnp.moveaxis(decay, 1, 0))
    _, o_inter = lax.scan(step, s0, xs)
    o = (o_intra + jnp.moveaxis(o_inter, 0, 1)).reshape(B, S, HG_HEADS, HG_DV)
    o = o * lax.rsqrt(jnp.mean(o * o, axis=-1, keepdims=True) + EPS) * norm_g.astype(jnp.float32)
    o = o.reshape(B, S, HG_V_W) * jax.nn.silu(g.astype(jnp.float32))
    return o.astype(dt)

def _swiglu(u, w1, w3, w2):
    return (jax.nn.silu(u @ w1) * (u @ w3)) @ w2

def _moe(u, router_w, w1, w3, w2):
    logits = (u @ router_w).astype(jnp.float32)
    top_val, top_idx = lax.top_k(logits, TOP_K)
    wts = jax.nn.softmax(top_val, axis=-1)
    gate = jnp.sum(jax.nn.one_hot(top_idx, N_EXPERTS, dtype=jnp.float32) * wts[..., None], axis=-2)
    gate = gate.astype(u.dtype)
    out = jnp.zeros_like(u)
    for e in range(N_EXPERTS):
        out = out + gate[..., e:e + 1] * _swiglu(u, w1[e], w3[e], w2[e])
    return out

def setup_inputs(seed: int = 0) -> dict:
    key = jax.random.key(seed)
    ks = jax.random.split(key, 24)
    f32 = jnp.float32
    nrm = lambda k, shp, s: jax.random.normal(k, shp, f32) * s
    return {
        'x': nrm(ks[0], (BATCH, SEQ, D_MODEL), 1.0),
        'p': nrm(ks[1], (DEPTH, BATCH, SEQ, PLE_DIM), 1.0),
        'w_in': nrm(ks[2], (DEPTH, D_MODEL, IN_WIDTH), D_MODEL ** -0.5),
        'sinks': nrm(ks[3], (DEPTH, ATT_Q_HEADS), 0.5),
        'rel_bias': nrm(ks[4], (REL_BUCKETS, ATT_Q_HEADS), 0.5),
        'lb_logits': nrm(ks[5], (DEPTH, HG_K_W), 1.0),
        'hgrn_norm': 1.0 + nrm(ks[6], (DEPTH, HG_DV), 0.01),
        'w_branch_a': nrm(ks[7], (DEPTH, ATT_Q_W, D_MODEL), ATT_Q_W ** -0.5),
        'w_branch_b': nrm(ks[8], (DEPTH, HG_V_W, D_MODEL), HG_V_W ** -0.5),
        'w_out': nrm(ks[9], (DEPTH, D_MODEL, D_MODEL), D_MODEL ** -0.5),
        'norm_mix': 1.0 + nrm(ks[10], (DEPTH, D_MODEL), 0.01),
        'norm_ffn': 1.0 + nrm(ks[11], (DEPTH, D_MODEL), 0.01),
        'norm_ple': 1.0 + nrm(ks[12], (DEPTH, D_MODEL), 0.01),
        'dense_w1': nrm(ks[13], (N_DENSE, D_MODEL, FFN_DENSE), D_MODEL ** -0.5),
        'dense_w3': nrm(ks[14], (N_DENSE, D_MODEL, FFN_DENSE), D_MODEL ** -0.5),
        'dense_w2': nrm(ks[15], (N_DENSE, FFN_DENSE, D_MODEL), FFN_DENSE ** -0.5),
        'router_w': nrm(ks[16], (N_MOE, D_MODEL, N_EXPERTS), D_MODEL ** -0.5),
        'moe_w1': nrm(ks[17], (N_MOE, N_EXPERTS, D_MODEL, FFN_EXPERT), D_MODEL ** -0.5),
        'moe_w3': nrm(ks[18], (N_MOE, N_EXPERTS, D_MODEL, FFN_EXPERT), D_MODEL ** -0.5),
        'moe_w2': nrm(ks[19], (N_MOE, N_EXPERTS, FFN_EXPERT, D_MODEL), FFN_EXPERT ** -0.5),
        'ple_proj': nrm(ks[20], (DEPTH, PLE_DIM, D_MODEL), PLE_DIM ** -0.5),
        'ple_gate': nrm(ks[21], (DEPTH, D_MODEL, D_MODEL), D_MODEL ** -0.5),
        'final_norm': 1.0 + nrm(ks[22], (D_MODEL,), 0.01),
    }

def reference(x, p, w_in, sinks, rel_bias, lb_logits, hgrn_norm, w_branch_a, w_branch_b,
              w_out, norm_mix, norm_ffn, norm_ple, dense_w1, dense_w3, dense_w2, router_w,
              moe_w1, moe_w3, moe_w2, ple_proj, ple_gate, final_norm):
    B, S = x.shape[0], x.shape[1]
    qi = jnp.arange(ATT_BLOCK)[:, None]
    kj = jnp.arange(2 * ATT_BLOCK)[None, :]
    band_bias = jnp.transpose(rel_bias[_t5_bucket(qi + ATT_BLOCK - kj)], (2, 0, 1))
    sm = jax.nn.softmax(lb_logits.astype(jnp.float32), axis=0)
    lower_bounds = jnp.cumsum(sm, axis=0) - sm[0:1]

    h = x
    for l in range(DEPTH):
        u = _rmsnorm(h, norm_mix[l])
        aq, ak, av, hq, hf, hi, hg, ga, gb = _split(u @ w_in[l])
        ya = _sliding_window_attention(
            aq.reshape(B, S, ATT_Q_HEADS, ATT_HEAD_DIM),
            ak.reshape(B, S, ATT_KV_HEADS, ATT_HEAD_DIM),
            av.reshape(B, S, ATT_KV_HEADS, ATT_HEAD_DIM),
            sinks[l], band_bias) @ w_branch_a[l]
        yb = _hgrn2(
            hq.reshape(B, S, HG_HEADS, HG_DK),
            hf.reshape(B, S, HG_HEADS, HG_DK),
            hi.reshape(B, S, HG_HEADS, HG_DV),
            hg, lower_bounds[l], hgrn_norm[l]) @ w_branch_b[l]
        merged = jax.nn.sigmoid(ga) * ya + jax.nn.sigmoid(gb) * yb
        h = h + merged @ w_out[l]

        u = _rmsnorm(h, norm_ffn[l])
        if l % 2 == 0:
            h = h + _swiglu(u, dense_w1[l // 2], dense_w3[l // 2], dense_w2[l // 2])
        else:
            h = h + _moe(u, router_w[l // 2], moe_w1[l // 2], moe_w3[l // 2], moe_w2[l // 2])

        u = _rmsnorm(h, norm_ple[l])
        h = h + jax.nn.sigmoid(u @ ple_gate[l]) * (p[l] @ ple_proj[l])
    return _rmsnorm(h, final_norm)


_drawn_inputs = setup_inputs


def setup_inputs(seed=0):
    import zlib

    import numpy as np

    out = dict(_drawn_inputs(seed))
    spreads = {}
    factors = {'sinks': 12.106,
     'hgrn_norm': 15.551,
     'norm_mix': 2.757,
     'norm_ple': 55.888,
     'final_norm': 31.791,
     'norm_ffn': 8.0}
    for name, (base, spread) in spreads.items():
        noise = np.random.default_rng([zlib.crc32(name.encode()), seed]).standard_normal(out[name].shape)
        drawn = base * np.exp(spread * noise) if base else spread * noise
        out[name] = __import__('jax').numpy.asarray(drawn.astype(out[name].dtype))
    for name, factor in factors.items():
        out[name] = (out[name] * factor).astype(out[name].dtype)
    return out
```

```python
from contextlib import ExitStack

import numpy as np

import concourse.bass as bass
from concourse import mybir

F32 = mybir.dt.float32
I32 = mybir.dt.int32
U32 = mybir.dt.uint32
ALU = mybir.AluOpType
ACT = mybir.ActivationFunctionType
AX = mybir.AxisListType

P = 128
D = 1024
DT = D // P
S = 256
TT = S // P
DEPTH = 2
QH, KVH, HD = 8, 2, 64
GROUP = QH // KVH
BUCKETS = 32
MAX_DIST = 128
HH = 4
CHUNK = 16
NCH = S // CHUNK
CPT = P // CHUNK
FD = 2816
FE = 3584
NE = 8
PLE = 256
KP = PLE // P
EPS = 1e-6
IN_W = 4864
O_AQ, O_AK, O_AV, O_HQ, O_HF, O_HI, O_HG, O_GA, O_GB = 0, 512, 640, 768, 1280, 1792, 2304, 2816, 3840
CAP = 96
NEG = -1e30

SLOTS = 7
SLOT = 2048

G_MIX, G_FFN, G_PLE, G_HN, LB, OMLB = 0, 8, 16, 24, 25, 29
PCOLS = 33
VROWS = 25
R_LB = DEPTH * VROWS
R_FIN = R_LB + DEPTH * HH
NVEC = R_FIN + DT

C_ID, C_ONE, C_LT, C_HM, C_CM, C_IO, C_SC, C_I8 = 0, 128, 256, 384, 512, 520, 616, 1640
C_N = 1648

U_HF, U_HQ, U_HI, U_AQ, U_AK, U_AV, U_HG, U_GA, U_GB, U_YA, U_YB, U_WO, U_PG, U_PP = (
    0, 4, 8, 12, 16, 18, 20, 24, 32, 40, 48, 56, 64, 72)
UNITS = "A" * 4 + "D" * 4 + "D" * 4 + "A" * 4 + "D" * 2 + "D" * 2 + "D" * 4 + "A" * 16 + "D" * 24 + "A" * 8 + "D" * 8
NU = len(UNITS)
UA, UD = UNITS.count("A"), UNITS.count("D")

X_SSQ, X_KT, X_P, X_SC = 0, 1, 5, 9
X_O01 = 17
X_ATT = 19
X_ORDER = (["ssq"] + ["kt"] * 4 + ["p"] * 4 + ["sc"] * 8 + ["o"] * 2 + ["pt", "pt", "pv"] * 3 + ["o"] * 2
           + ["pt", "pt", "pv"] + ["osq"] * 2 + ["ssq"] * 2)
X_DRAIN = "".join("D" if k in ("p", "sc", "pv") else "A" for k in X_ORDER)
NX = len(X_ORDER)
XA, XD = X_DRAIN.count("A"), X_DRAIN.count("D")
X_FFN, X_PLE = NX - 2, NX - 1
RING = 3


def nth(kind, n):
    return [i for i, k in enumerate(X_ORDER) if k == kind][n]


def mixer_steps():
    s = [("hf", h) for h in range(4)] + [("hq", h) for h in range(4)] + [("gates", 0)]
    s += [("hi", i) for i in range(4)] + [("scan", 0)] + [("aq", i) for i in range(4)] + [("decay", 0)]
    s += [("ak", 0), ("ak", 1), ("av", 0), ("av", 1)]
    s += [("kt", h) for h in range(4)] + [("p", h) for h in range(4)]
    for h in range(8):
        s += [("sc", h), ("kv", h)]
    s += [("softmax", 0)]
    s += [("hg", 0), ("o", 0), ("hg", 1), ("o", 1), ("hg", 2), ("kv", 8), ("hg", 3), ("kv", 9)]
    s += [("ga", 0), ("kv", 10), ("ga", 1), ("kv", 11), ("ga", 2), ("pt", 0), ("pt", 1), ("pv", 0)]
    s += [("kv", 12), ("ga", 3), ("kv", 13), ("ga", 4), ("pt", 2), ("pt", 3), ("pv", 1)]
    s += [("kv", 14), ("ga", 5), ("kv", 15), ("ga", 6), ("pt", 4), ("pt", 5), ("pv", 2)]
    s += [("ga", 7), ("o", 2), ("gb", 0), ("o", 3), ("gb", 1), ("pt", 6), ("pt", 7), ("pv", 3), ("gb", 2)]
    s += [("osq", 0), ("osq", 1)] + [("gb", i) for i in range(3, 8)] + [("ynorm", 0)]
    s += [("ya", d) for d in range(8)] + [("yb", d) for d in range(8)] + [("wo", d) for d in range(8)]
    return s


STEPS = mixer_steps()


def ffn_chunks(tiles, halves):
    out = []
    pairs = tiles // 2
    for j in range(pairs):
        out += [("w1", 2 * j, 2), ("w3", 2 * j, 2)]
        out += [("w2", 2 * j, 1), ("w2", 2 * j + 1, 1)] if j >= pairs - halves else [("w2", 2 * j, 2)]
    return out


def chunk_of(chunks, matrix, f):
    for i, (m, f0, n) in enumerate(chunks):
        if m == matrix and f0 <= f < f0 + n:
            return i, f - f0


TD, TE = FD // P, FE // P
DENSE = ffn_chunks(TD, 2)
EXPERT = ffn_chunks(TE, 0)

MIXER = [("in", O_HF + P * i, P, U_HF + i) for i in range(4)]
for name_off, unit, n in ((O_HQ, U_HQ, 2), (O_HI, U_HI, 2), (O_AQ, U_AQ, 2), (O_AK, U_AK, 1), (O_HG, U_HG, 2),
                          (O_GA, U_GA, 4), (O_GB, U_GB, 4)):
    MIXER += [("in", name_off + 256 * i, 256, unit + (3 if name_off == O_AK else 2 * i + 1)) for i in range(n)]
MIXER += [("wa", 512 * i, 512, U_YA + 4 * i + 3) for i in range(2)]
MIXER += [("wb", 512 * i, 512, U_YB + 4 * i + 3) for i in range(2)]
MIXER += [("wo", 256 * i, 256, U_WO + 2 * i + 1) for i in range(4)]
EMBED = [("pg", 256 * i, 256, U_PG + 2 * i + 1) for i in range(4)] + [("pp", 512 * i, 512, U_PP + 4 * i + 3) for i in range(2)]
NM, ND, NX_E, NP = len(MIXER), len(DENSE), len(EXPERT), len(EMBED)
assert (NM + NP) % SLOTS == 0 and ND % SLOTS == 0 and NX_E % SLOTS == 0
LAYER_CHUNKS = NM + ND + NP


def trunk(nc, x, p, w_in, sinks, rel_bias, vectors, w_branch_a, w_branch_b, w_out, dense_w1, dense_w3,
          dense_w2, router_w, moe_w1, moe_w3, moe_w2, ple_proj, ple_gate, consts, buckets, outside, out):
    ctx = ExitStack()
    with ctx:
        def sb(name, shape, dt=F32):
            return ctx.enter_context(nc.sbuf_tensor(name, shape, dt))

        def sem(name):
            return ctx.enter_context(nc.semaphore(name))

        bias_rows_dram = nc.dram_tensor("bias_rows_dram", (QH, P, 384), F32, kind="Internal").ap()

        ring = sb("ring", [P, SLOTS, SLOT])
        hT = sb("hT", [P, DT, S])
        uT = sb("uT", [P, DT, S])
        rstd = sb("rstd", [P, S])
        consts_sb = sb("consts_sb", [P, C_N])
        ident, ones = consts_sb[:, C_ID:C_ID + P], consts_sb[:, C_ONE:C_ONE + P]
        before = consts_sb[:, C_LT:C_LT + P]
        hg_mask = consts_sb[:, C_HM:C_HM + P]
        chunk_mask = consts_sb[:, C_CM:C_CM + CPT]
        slot_iota = consts_sb[:, C_IO:C_IO + CAP]
        scan_mask = consts_sb[:, C_SC:C_SC + HH * S]
        expert_iota = consts_sb[:, C_I8:C_I8 + NE]
        eps = sb("eps", [P, 1])
        params = sb("params", [P, DEPTH, PCOLS])
        fin_gain = sb("fin_gain", [P, DT])
        gain = sb("gain", [P, PCOLS])
        vec_rows = sb("vec_rows", [P, P])
        lbt = sb("lbt", [P, 3, HH])
        sink = sb("sink", [P, DEPTH, QH])
        p_T = sb("p_T", [P, DEPTH, KP, S])
        rw = sb("rw", [P, DT, NE])
        bias = sb("bias", [P, QH, 384])
        hF = sb("hF", [P, HH, S])
        hK = sb("hK", [P, HH, S])
        hA = sb("hA", [P, HH, S])
        kend = sb("kend", [P, TT, HH * P])
        hE = sb("hE", [P, HH, S])
        hKi = sb("hKi", [P, HH, S])
        hQ = sb("hQ", [P, HH, S])
        hV = sb("hV", [P, TT, HH * P])
        hO = sb("hO", [P, HH, S])
        hG = sb("hG", [P, HH, S])
        dec = sb("dec", [P, HH * NCH])
        vx = sb("vx", [P, 2, CPT, P])
        state = sb("state", [P, 2, NCH - 1, P])
        pm = sb("pm", [P, HH, TT, P])
        aQ = sb("aQ", [P, QH // 2, S])
        aK = sb("aK", [P, KVH, S])
        aV = sb("aV", [P, TT, KVH * HD])
        sc = sb("sc", [P, QH, 384])
        pT = sb("pT", [P, 2, 384])
        aO = sb("aO", [P, QH // 2, S])
        smax = sb("smax", [P, 6, 2 * QH])
        gA = sb("gA", [P, DT, S])
        gB = sb("gB", [P, DT, S])
        x_in = gA[:].rearrange("p d s -> p (d s)").rearrange("p (t n) -> p t n", t=TT)
        p_in = hG[:].rearrange("p d s -> p (d s)").rearrange("p (l t n) -> p l t n", l=DEPTH, t=TT)
        out_rows = x_in
        onehot = sc[0:BUCKETS, 0, :]
        bias_out = sc[0:QH, 1, :]
        rel_sb = sc[0:BUCKETS, 2, 0:QH]
        mask_row = sc[0:QH, 3, :]
        ffn_silu = hF[:, 0:2, :]
        ffn_act = hF[:, 2:4, :]
        u_tok = x_in
        gbf = gB[:].rearrange("p d s -> p (d s)")
        u_slot = gbf[:, 0:DT * CAP].rearrange("p (d n) -> p d n", d=DT)
        y_slot = gbf[:, 768:768 + DT * CAP].rearrange("p (d n) -> p d n", d=DT)
        y_tok = hE[:].rearrange("p d s -> p (d s)")[0:CAP, :]
        sel_slot = hKi[:].rearrange("p d s -> p (d s)")[:, 0:TT * CAP].rearrange("p (t n) -> p t n", t=TT)
        gate_slot = hKi[:].rearrange("p d s -> p (d s)")[:, 512:512 + TT * CAP].rearrange("p (t n) -> p t n", t=TT)
        comb = hQ[0:CAP, 0, :]
        gate_cols = hKi[:, 0, :].rearrange("p (t n) -> p t n", t=TT)
        gate_row = hQ[:, 1, :]
        rt = sb("rt", [P, 12, TT, NE])
        logit, top8, picked, gate, pos, ex, tmp8 = (rt[:, i] for i in range(7))
        idxf = rt[:, 7]
        den = rt[:, 8]
        idx8 = sb("idx8", [P, TT, NE], U32)
        cnt = sb("cnt", [P, NE])
        flag = sb("flag", [P, 1], I32)

        bank = [ctx.enter_context(nc.psum_tensor(f"bank{i}", [P, 512], F32)) for i in range(8)]

        slot_loaded = [sem(f"slot_loaded{i}") for i in range(SLOTS)]
        consts_in, vec_in, x_loaded, small_in, p_loaded, sc_in = (
            sem(n) for n in ("consts_in", "vec_in", "x_loaded", "small_in", "p_loaded", "sc_in"))
        setup_pe, setup_dve, lb_exp, bias_row_ready, bias_rows_out, bias_in, set_const = (
            sem(n) for n in ("setup_pe", "setup_dve", "lb_exp", "bias_row_ready", "bias_rows_out", "bias_in", "set_const"))
        h_ready, h_mix, h_ffn = sem("h_ready"), sem("h_mix"), sem("h_ffn")
        sq_ready, rms_ready, u_ready = sem("sq_ready"), sem("rms_ready"), sem("u_ready")
        unit_done, unit_act, unit_dve = sem("unit_done"), sem("unit_act"), sem("unit_dve")
        aux_done, aux_act, aux_dve = sem("aux_done"), sem("aux_act"), sem("aux_dve")
        f_ready, logf_ready, scan_ready, exp_ready, diff_ready, kdec_ready, hgrn_ready = (
            sem(n) for n in ("f_ready", "logf_ready", "scan_ready", "exp_ready", "diff_ready", "kdec_ready", "hgrn_ready"))
        pm_ready, vx_ready, kv_done, state_ready = sem("pm_ready"), sem("vx_ready"), sem("kv_done"), sem("state_ready")
        gate_sig, max_ready, exp_done, prob_ready = sem("gate_sig"), sem("max_ready"), sem("exp_done"), sem("prob_ready")
        osq_ready, orms_ready, yb_ready, merged = sem("osq_ready"), sem("orms_ready"), sem("yb_ready"), sem("merged")
        d_up, d_silu, d_act, d_down = sem("d_up"), sem("d_silu"), sem("d_act"), sem("d_down")
        m_up, m_silu, m_act, m_down = sem("m_up"), sem("m_silu"), sem("m_act"), sem("m_down")
        r_pe, r_act, r_dve, route_ready = sem("r_pe"), sem("r_act"), sem("r_dve"), sem("route_ready")
        slots_ready, gathered, u_slot_ready = sem("slots_ready"), sem("gathered"), sem("u_slot_ready")
        y_ready, y_tr, y_tok_ready, comb_tr, comb_ready, comb_done = (
            sem(n) for n in ("y_ready", "y_tr", "y_tok_ready", "comb_tr", "comb_ready", "comb_done"))
        fin_ready, fin_tr, row_ready, out_done = sem("fin_ready"), sem("fin_tr"), sem("row_ready"), sem("out_done")

        def wview(i, tiles, cols):
            return ring[:, i % SLOTS, 0:tiles * cols].rearrange("p (k n) -> p k n", k=tiles)

        def await_unit_free(eng, u, l):
            if u >= RING:
                n = u - RING
                if UNITS[n] == "A":
                    eng.wait_ge(unit_act, UA * l + UNITS[:n + 1].count("A"))
                else:
                    eng.wait_ge(unit_dve, UD * l + UNITS[:n + 1].count("D"))

        def await_unit_read(eng, u, l):
            if UNITS[u] == "A":
                eng.wait_ge(unit_act, UA * l + UNITS[:u + 1].count("A"))
            else:
                eng.wait_ge(unit_dve, UD * l + UNITS[:u + 1].count("D"))

        def await_aux_free(eng, u, l):
            if u >= RING:
                await_aux_read(eng, u - RING, l)

        def await_aux_read(eng, u, l):
            if X_DRAIN[u] == "A":
                eng.wait_ge(aux_act, XA * l + X_DRAIN[:u + 1].count("A"))
            else:
                eng.wait_ge(aux_dve, XD * l + X_DRAIN[:u + 1].count("D"))

        def ubank(u):
            return bank[u % RING]

        def xbank(u):
            return bank[3 + u % RING]

        block = ctx.enter_context(nc.Block())

        @block.sync
        def _(sp):
            src = {"in": w_in, "wo": w_out, "pg": ple_gate, "wa": w_branch_a, "wb": w_branch_b, "pp": ple_proj}

            freed = []

            def load(n, dst, source):
                if n >= SLOTS:
                    s, v = freed[n - SLOTS]
                    sp.wait_ge(s, v)
                sp.dma_start(dst, source).then_inc(slot_loaded[n % SLOTS], 16)

            def by_columns(table, l):
                for matrix, c0, cols, unit in table:
                    w = src[matrix][l].rearrange("(k p) n -> p k n", p=P)
                    n = len(freed)
                    load(n, wview(n, w.shape[1], cols), w[:, :, c0:c0 + cols])
                    freed.append((unit_done, NU * l + unit + 1))

            def swiglu(chunk, w1, w3, w2, n):
                m, f0, tiles = chunk
                if m == "w2":
                    return wview(n, tiles, D), w2[f0 * P:(f0 + tiles) * P, :].rearrange("(k p) n -> p k n", p=P)
                w = {"w1": w1, "w3": w3}[m].rearrange("(k p) n -> p k n", p=P)
                return wview(n, DT, tiles * P), w[:, :, f0 * P:(f0 + tiles) * P]

            by_columns(MIXER, 0)
            for chunk in DENSE:
                n = len(freed)
                load(n, *swiglu(chunk, dense_w1[0], dense_w3[0], dense_w2[0], n))
                freed.append((d_down if chunk[0] == "w2" else d_up, chunk[1] + chunk[2]))
            by_columns(EMBED, 0)
            by_columns(MIXER, 1)
            first = len(freed)
            for chunk in EXPERT:
                n = len(freed)
                load(n, *swiglu(chunk, moe_w1[0, 0], moe_w3[0, 0], moe_w2[0, 0], n))
                freed.append((m_down if chunk[0] == "w2" else m_up, chunk[1] + chunk[2]))
            used = [(m_down if m == "w2" else m_up, f0 + n) for m, f0, n in EXPERT]
            with sp.Fori(1, NE) as e:
                for i, chunk in enumerate(EXPERT):
                    s, v = used[(i - SLOTS) % NX_E]
                    sp.wait_ge(s, TE * e + (v - TE if i < SLOTS else v))
                    dst, source = swiglu(chunk, moe_w1[0, e], moe_w3[0, e], moe_w2[0, e], first + i)
                    sp.dma_start(dst, source).then_inc(slot_loaded[(first + i) % SLOTS], 16)
            freed += [(s, v + TE * (NE - 1)) for s, v in used] * (NE - 1)
            by_columns(EMBED, 1)

        at_mixer = lambda i, l: (i, LAYER_CHUNKS // SLOTS * l)
        at_embed = lambda i, l: (NM + ND + i, (LAYER_CHUNKS + NE * NX_E - ND) // SLOTS * l)

        def await_chunk(pe, n, rounds=0):
            pe.wait_ge(slot_loaded[n % SLOTS], 16 * (n // SLOTS + 1) + 16 * rounds)

        @block.tensor
        def _(pe):
            mm = nc.tensor.matmul

            def product(dst, w, rhs, tiles, await_k=None):
                for k in range(tiles):
                    if await_k:
                        await_k(k)
                    last = mm(dst, w[:, k, :], rhs[:, k, :], start=(k == 0), stop=(k == tiles - 1))
                return last

            def transpose(dst, a, parts=P):
                return nc.tensor.transpose(dst, a, consts_sb[0:parts, C_ID:C_ID + parts])

            def sum_of_squares(norm, unit, l):
                await_aux_free(pe, unit, l)
                for k in range(DT):
                    if k % 4 == 0:
                        pe.wait_ge(sq_ready, 6 * l + 2 * norm + k // 4 + 1)
                    last = mm(xbank(unit)[:, 0:S], ones, uT[:, k, :], start=(k == 0), stop=(k == DT - 1))
                last.then_inc(aux_done, 1)

            def unit_product(u, l, w, rhs, tiles, dst=None, await_k=None):
                await_unit_free(pe, u, l)
                dst = ubank(u)[:, 0:S] if dst is None else dst
                product(dst, w, rhs, tiles, await_k).then_inc(unit_done, 1)

            pe.wait_ge(consts_in, 16)
            pe.wait_ge(vec_in, 16)
            transpose(bank[0][:, 0:NVEC], vec_rows[0:NVEC, :], NVEC).then_inc(setup_pe, 1)
            pe.wait_ge(sc_in, 48)
            mm(bank[7][0:QH, 0:384], rel_sb, onehot, start=True, stop=True).then_inc(setup_pe, 1)
            pe.wait_ge(x_loaded, 16)
            for j in range(DT // 2):
                for k in (2 * j, 2 * j + 1):
                    for t in range(TT):
                        c = (k % 2) * S + t * P
                        last = transpose(bank[1 + j][:, c:c + P], x_in[:, t, k * P:(k + 1) * P])
                last.then_inc(setup_pe, 1)
            pe.wait_ge(p_loaded, 16)
            for l in range(DEPTH):
                for k in range(KP):
                    for t in range(TT):
                        c = k * S + t * P
                        last = transpose(bank[5 + l][:, c:c + P], p_in[:, l, t, k * P:(k + 1) * P])
                last.then_inc(setup_pe, 1)

            def mixer(l):
                for stage, i in STEPS:
                    if stage in ("hf", "hq", "aq", "hg", "ga", "gb"):
                        u = {"hf": U_HF, "hq": U_HQ, "aq": U_AQ, "hg": U_HG, "ga": U_GA, "gb": U_GB}[stage] + i
                        if stage == "hf":
                            c, off, cols = i, 0, P
                        else:
                            c = {"hq": 4, "aq": 8, "hg": 11, "ga": 13, "gb": 17}[stage] + i // 2
                            off, cols = (i % 2) * P, 256
                        await_chunk(pe, *at_mixer(c, l))
                        w = wview(c, DT, cols)[:, :, off:off + P]
                        wait_u = (lambda k: pe.wait_ge(u_ready, 24 * l + k + 1)) if u == 0 else None
                        unit_product(u, l, w, uT, DT, await_k=wait_u)
                    elif stage == "hi":
                        half, t = i // 2, i % 2
                        await_chunk(pe, *at_mixer(6 + half, l))
                        unit_product(U_HI + i, l, uT[:, :, t * P:(t + 1) * P], wview(6 + half, DT, 256), DT)
                    elif stage == "ak":
                        await_chunk(pe, *at_mixer(10, l))
                        w = wview(10, DT, 256)
                        await_unit_free(pe, U_AK + i, l)
                        for half in range(2):
                            last = product(ubank(U_AK + i)[half * HD:(half + 1) * HD, 0:S],
                                           w[:, :, i * HD:(i + 1) * HD], uT, DT)
                        last.then_inc(unit_done, 1)
                    elif stage == "av":
                        unit_product(U_AV + i, l, uT[:, :, i * P:(i + 1) * P], wview(10, DT, 256)[:, :, P:2 * P], DT,
                                     dst=ubank(U_AV + i)[:, 0:P])
                    elif stage == "kt":
                        u = nth("kt", i)
                        pe.wait_ge(kdec_ready, l + 1)
                        await_aux_free(pe, u, l)
                        for t in range(TT):
                            last = transpose(xbank(u)[:, t * P:(t + 1) * P], hF[:, i, t * P:(t + 1) * P])
                        last.then_inc(aux_done, 1)
                    elif stage == "p":
                        u = nth("p", i)
                        pe.wait_ge(hgrn_ready, l + 1)
                        await_aux_free(pe, u, l)
                        for t in range(TT):
                            last = mm(xbank(u)[:, t * P:(t + 1) * P], hKi[:, i, t * P:(t + 1) * P],
                                      hQ[:, i, t * P:(t + 1) * P], start=True, stop=True)
                        last.then_inc(aux_done, 1)
                    elif stage == "kv":
                        h, t, half = i // 4, i // 2 % 2, i % 2
                        n = P * (3 if t == 1 and half == 1 else 4)
                        pe.wait_ge(vx_ready, 8 * l + i // 2 + 1)
                        await_aux_read(pe, nth("kt", h), l)
                        if i >= 2:
                            pe.wait_ge(state_ready, 16 * l + i - 1)
                        rhs = vx[:, (i // 2) % 2, 4 * half:4 * half + 4, :].rearrange("p c n -> p (c n)")
                        mm(bank[6 + i % 2][:, 0:n], kend[:, t, h * P:(h + 1) * P], rhs[:, 0:n],
                           start=True, stop=True).then_inc(kv_done, 1)
                    elif stage == "sc":
                        u = nth("sc", i)
                        await_unit_read(pe, U_AQ + 3, l)
                        await_unit_read(pe, U_AV + 1, l)
                        await_aux_free(pe, u, l)
                        r = slice((i % 2) * HD, (i % 2 + 1) * HD)
                        q, k = aQ[r, i // 2, :], aK[r, i // GROUP, :]
                        mm(xbank(u)[:, 0:P], q[:, 0:P], k[:, 0:P], start=True, stop=True)
                        mm(xbank(u)[:, P:P + S], q[:, P:S], k, start=True, stop=True).then_inc(aux_done, 1)
                    elif stage == "pt":
                        u = nth("pt", i)
                        pe.wait_ge(prob_ready, l + 1)
                        await_aux_free(pe, u, l)
                        for b in range(3):
                            last = transpose(xbank(u)[:, b * P:(b + 1) * P], sc[:, i, b * P:(b + 1) * P])
                        last.then_inc(aux_done, 1)
                    elif stage == "pv":
                        u = nth("pv", i)
                        await_aux_free(pe, u, l)
                        for h in (2 * i, 2 * i + 1):
                            await_aux_read(pe, nth("pt", h), l)
                            dst = xbank(u)[(h % 2) * HD:(h % 2 + 1) * HD, 0:S]
                            g = slice(h // GROUP * HD, (h // GROUP + 1) * HD)
                            mm(dst[:, 0:P], aV[:, 0, g], pT[:, h % 2, 0:P], start=True, stop=True)
                            mm(dst[:, P:S], aV[:, 0, g], pT[:, h % 2, P:2 * P], start=True, stop=False)
                            last = mm(dst[:, P:S], aV[:, 1, g], pT[:, h % 2, 2 * P:3 * P], start=False, stop=True)
                        last.then_inc(aux_done, 1)
                    elif stage == "o":
                        u = nth("o", i)
                        pe.wait_ge(pm_ready, 4 * l + i + 1)
                        pe.wait_ge(state_ready, 16 * l + 4 * i + 4)
                        await_aux_free(pe, u, l)
                        for t in range(TT):
                            mm(xbank(u)[:, t * P:(t + 1) * P], hV[:, t, i * P:(i + 1) * P], pm[:, i, t, :],
                               start=True, stop=False, skip_group_check=True)
                            for c in range(t * CPT + (t == 0), (t + 1) * CPT):
                                cols = slice(c * CHUNK, (c + 1) * CHUNK)
                                last = mm(xbank(u)[:, cols], state[:, i % 2, c - 1, :], hQ[:, i, cols],
                                          start=False, stop=True, skip_group_check=True)
                        last.then_inc(aux_done, 1)
                    elif stage == "osq":
                        u = nth("osq", i)
                        pe.wait_ge(osq_ready, 4 * l + 2 * i + 2)
                        await_aux_free(pe, u, l)
                        mm(xbank(u)[:], ones, hK[:, 2 * i:2 * i + 2, :].rearrange("p h s -> p (h s)"),
                           start=True, stop=True).then_inc(aux_done, 1)
                    elif stage == "ya":
                        c = 21 + i // 4
                        await_chunk(pe, *at_mixer(c, l))
                        await_aux_read(pe, nth("pv", 3), l)
                        unit_product(U_YA + i, l, wview(c, 4, 512)[:, :, (i % 4) * P:(i % 4 + 1) * P], aO, 4)
                    elif stage == "yb":
                        c = 23 + i // 4
                        await_chunk(pe, *at_mixer(c, l))
                        pe.wait_ge(yb_ready, l + 1)
                        unit_product(U_YB + i, l, wview(c, 4, 512)[:, :, (i % 4) * P:(i % 4 + 1) * P], hO, 4)
                    elif stage == "wo":
                        c = 25 + i // 2
                        await_chunk(pe, *at_mixer(c, l))
                        pe.wait_ge(merged, 8 * l + 8)
                        unit_product(U_WO + i, l, wview(c, DT, 256)[:, :, (i % 2) * P:(i % 2 + 1) * P], uT, DT)

            def up(f, n, rhs, table, chunk, up_sem):
                for j, m in enumerate(("w1", "w3")):
                    c, at = chunk_of(table, m, f)
                    chunk(c)
                    tiles = table[c][2]
                    w = wview(chunk.base + c, DT, tiles * P)[:, :, at * P:(at + 1) * P]
                    last = product(bank[f % 4][:, j * n:(j + 1) * n], w, rhs, DT)
                last.then_inc(up_sem, 1)

            def down(f, n, act, table, chunk, down_sem, tiles, per_bank):
                c, at = chunk_of(table, "w2", f)
                chunk(c)
                w = wview(chunk.base + c, table[c][2], D)
                for d in range(DT):
                    col = (d % per_bank) * n
                    last = mm(bank[4 + d // per_bank][:, col:col + n], w[:, at, d * P:(d + 1) * P], act[:, f % 2, 0:n],
                              start=(f == 0 and d % per_bank == 0), stop=(f == tiles - 1), skip_group_check=True)
                last.then_inc(down_sem, 1)

            def dense(l):
                def chunk(c):
                    await_chunk(pe, NM + c)
                chunk.base = NM
                for k in range(DT):
                    pe.wait_ge(u_ready, 8 + k + 1)
                for f in range(TD):
                    if f >= 4:
                        pe.wait_ge(d_act, f - 3)
                    up(f, S, uT, DENSE, chunk, d_up)
                    if f:
                        pe.wait_ge(d_act, f)
                        down(f - 1, S, ffn_act, DENSE, chunk, d_down, TD, 2)
                pe.wait_ge(d_act, TD)
                down(TD - 1, S, ffn_act, DENSE, chunk, d_down, TD, 2)

            def experts(e, n, rhs):
                base = LAYER_CHUNKS + NM

                def chunk(c):
                    await_chunk(pe, base + c, NX_E // SLOTS * e)
                chunk.base = base
                for f in range(TE):
                    if f >= 4:
                        pe.wait_ge(m_act, TE * e + f - 3)
                    up(f, n, rhs, EXPERT, chunk, m_up)
                    if f:
                        pe.wait_ge(m_act, TE * e + f)
                        down(f - 1, n, ffn_act, EXPERT, chunk, m_down, TE, 4 if n == CAP else 2)
                pe.wait_ge(m_act, TE * e + TE)
                down(TE - 1, n, ffn_act, EXPERT, chunk, m_down, TE, 4 if n == CAP else 2)

            def moe():
                for k in range(DT):
                    pe.wait_ge(u_ready, 32 + k + 1)
                for t in range(TT):
                    product(bank[4][:, t * NE:(t + 1) * NE], uT[:, :, t * P:(t + 1) * P], rw, DT)
                transpose(bank[0][:, 0:P], uT[:, 0, 0:P]).then_inc(r_pe, 1)
                for t in range(TT):
                    for half in range(2):
                        for j in range(4):
                            last = transpose(bank[2 * t + half][:, j * P:(j + 1) * P],
                                             uT[:, 4 * half + j, t * P:(t + 1) * P])
                        last.then_inc(r_pe, 1)
                pe.wait_ge(r_dve, 1)
                mm(bank[5][:, 0:8], before, picked[:, 0, :], start=True, stop=True)
                mm(bank[5][:, 8:16], ones, picked[:, 0, :], start=True, stop=False)
                mm(bank[5][:, 8:16], before, picked[:, 1, :], start=False, stop=True)
                mm(bank[5][:, 16:24], ones, picked[:, 0, :], start=True, stop=False)
                mm(bank[5][:, 16:24], ones, picked[:, 1, :], start=False, stop=True).then_inc(r_pe, 1)
                pe.wait_ge(r_act, 4)
                pe.wait_ge(route_ready, 1)
                fullest = pe.value_load(flag[0:1, 0:1], min_val=0, max_val=S)
                with pe.If(fullest <= CAP):
                    with pe.Fori(0, NE) as e:
                        pe.wait_ge(slots_ready, e + 1)
                        for d in range(DT):
                            for t in range(TT):
                                last = mm(bank[6 + d // 4][:, (d % 4) * CAP:(d % 4 + 1) * CAP],
                                          u_tok[:, t, d * P:(d + 1) * P], sel_slot[:, t, :],
                                          start=(t == 0), stop=(t == TT - 1))
                            if d % 4 == 3:
                                last.then_inc(gathered, 1)
                        pe.wait_ge(u_slot_ready, 2 * e + 2)
                        experts(e, CAP, u_slot)
                        for t in range(TT):
                            last = transpose(bank[0][0:CAP, t * P:(t + 1) * P], gate_slot[:, t, :])
                        last.then_inc(comb_tr, 1)
                        for half in range(2):
                            pe.wait_ge(y_ready, 2 * e + half + 1)
                            for j in range(4):
                                last = transpose(bank[6 + half][0:CAP, j * P:(j + 1) * P], y_slot[:, 4 * half + j, :])
                            last.then_inc(y_tr, 1)
                        pe.wait_ge(comb_ready, e + 1)
                        pe.wait_ge(y_tok_ready, 2 * e + 2)
                        for d in range(DT):
                            last = mm(bank[4 + d // 2][:, (d % 2) * S:(d % 2 + 1) * S], y_tok[:, d * P:(d + 1) * P], comb,
                                      start=True, stop=True)
                            if d % 2:
                                last.then_inc(comb_done, 1)
                with pe.Else():
                    with pe.Fori(0, NE) as e:
                        pe.wait_ge(slots_ready, e + 1)
                        for t in range(TT):
                            last = mm(bank[3][:, t * P:(t + 1) * P], gate_cols[:, t, :], ident, start=True, stop=True)
                        last.then_inc(gathered, 1)
                        pe.wait_ge(u_slot_ready, e + 1)
                        experts(e, S, uT)
                return fullest

            with pe.Fori(0, DEPTH) as l:
                sum_of_squares(0, X_SSQ, l)
                mixer(l)
                sum_of_squares(1, X_FFN, l)
                with pe.If(l < 1):
                    dense(l)
                with pe.Else():
                    moe()
                    pe.drain()
                sum_of_squares(2, X_PLE, l)
                for i in range(DT):
                    c = i // 2
                    n, more = at_embed(c, l)
                    await_chunk(pe, n, more)
                    wait_u = (lambda k: pe.wait_ge(u_ready, 24 * l + 16 + k + 1)) if i == 0 else None
                    unit_product(U_PG + i, l, wview(n, DT, 256)[:, :, (i % 2) * P:(i % 2 + 1) * P], uT, DT, await_k=wait_u)
                for i in range(DT):
                    n, more = at_embed(4 + i // 4, l)
                    await_chunk(pe, n, more)
                    await_unit_free(pe, U_PP + i, l)
                    w = wview(n, KP, 512)
                    for k in range(KP):
                        last = mm(ubank(U_PP + i)[:, 0:S], w[:, k, (i % 4) * P:(i % 4 + 1) * P],
                                  p_T[:, bass.ds(l, 1), k, :].rearrange("p a s -> p (a s)"),
                                  start=(k == 0), stop=(k == KP - 1))
                    last.then_inc(unit_done, 1)

            sum_of_squares(0, 0, DEPTH)
            for k in range(DT):
                pe.wait_ge(fin_ready, k + 1)
                for t in range(TT):
                    last = transpose(bank[4 + 2 * t + k // 4 if t == 0 else 6 + k // 4][:, (k % 4) * P:(k % 4 + 1) * P],
                                     uT[:, k, t * P:(t + 1) * P])
            last.then_inc(fin_tr, 1)

        @block.scalar
        def _(act):
            fn = nc.scalar.activation

            act.dma_start(consts_sb[:], consts).then_inc(consts_in, 16)
            act.dma_start(vec_rows[0:NVEC, :], vectors).then_inc(vec_in, 16)
            act.dma_start(x_in, x.rearrange("(t p) n -> p t n", p=P)).then_inc(x_loaded, 16)
            act.dma_start(onehot, buckets).then_inc(sc_in, 16)
            act.dma_start(rel_sb, rel_bias).then_inc(sc_in, 16)
            act.dma_start(mask_row, outside).then_inc(sc_in, 16)
            act.dma_start(p_in, p.rearrange("l (t p) n -> p l t n", p=P)).then_inc(p_loaded, 16)
            act.dma_start(sink[:].rearrange("p l h -> p (l h)"),
                          sinks.rearrange("l h -> (l h)").partition_broadcast(P)).then_inc(small_in, 16)
            act.dma_start(rw[:], router_w[0].rearrange("(k p) e -> p k e", p=P)).then_inc(small_in, 16)
            act.wait_ge(set_const, 1)
            act.wait_ge(setup_dve, 1)
            fn(lbt[:, 0:2, :], lbt[:, 0:2, :], ACT.Exp).then_inc(lb_exp, 1)

            def rms(src_bank, unit, l, norm, norm_sem_value):
                act.wait_ge(aux_done, NX * l + unit + 1)
                fn(rstd[:], src_bank[:, 0:S], ACT.Ln, scale=1.0 / D, bias=eps[:]).then_inc(aux_act, 1)
                act.drain()
                fn(rstd[:], rstd[:], ACT.Exp, scale=-0.5).then_inc(rms_ready, 1)

            def squares():
                for half in range(2):
                    fn(uT[:, 4 * half:4 * half + 4, :], hT[:, 4 * half:4 * half + 4, :], ACT.Square).then_inc(sq_ready, 1)

            def unit_wait(u, l):
                act.wait_ge(unit_done, NU * l + u + 1)

            def aux_wait(u, l):
                act.wait_ge(aux_done, NX * l + u + 1)

            def mixer(l):
                for stage, i in STEPS:
                    if stage == "hf":
                        unit_wait(U_HF + i, l)
                        fn(hF[:, i, :], ubank(U_HF + i)[:, 0:S], ACT.Sigmoid).then_inc(unit_act, 1)
                    elif stage == "gates":
                        act.wait_ge(f_ready, l + 1)
                        fn(hF[:], hF[:], ACT.Ln).then_inc(logf_ready, 1)
                    elif stage == "scan":
                        act.wait_ge(scan_ready, l + 1)
                        fn(hE[:], hA[:], ACT.Exp).then_inc(exp_ready, 1)
                        fn(hKi[:], hA[:], ACT.Exp, scale=-1.0).then_inc(exp_ready, 1)
                        act.wait_ge(diff_ready, l + 1)
                        fn(hF[:], hF[:], ACT.Exp).then_inc(exp_ready, 1)
                    elif stage == "aq":
                        unit_wait(U_AQ + i, l)
                        fn(aQ[:, i, :], ubank(U_AQ + i)[:, 0:S], ACT.Copy, scale=HD ** -0.5).then_inc(unit_act, 1)
                    elif stage == "kt":
                        u = nth("kt", i)
                        aux_wait(u, l)
                        fn(kend[:, :, i * P:(i + 1) * P], xbank(u)[:, 0:S].rearrange("p (t n) -> p t n", t=TT),
                           ACT.Copy).then_inc(aux_act, 1)
                    elif stage == "softmax":
                        act.wait_ge(max_ready, l + 1)
                        for b in range(2):
                            for h in range(QH):
                                s = sc[:, h, 0:P] if b == 0 else sc[:, h, P:P + S]
                                j = b * QH + h
                                fn(s, s, ACT.Exp, bias=smax[:, 1, j:j + 1], accum_out=smax[:, 2, j:j + 1])
                        fn(smax[:, 3, :], smax[:, 3, :], ACT.Exp).then_inc(exp_done, 1)
                    elif stage == "hg":
                        unit_wait(U_HG + i, l)
                        fn(hG[:, i, :], ubank(U_HG + i)[:, 0:S], ACT.Sigmoid).then_inc(gate_sig, 1)
                    elif stage in ("ga", "gb"):
                        u, dst = (U_GA + i, gA) if stage == "ga" else (U_GB + i, gB)
                        unit_wait(u, l)
                        fn(dst[:, i, :], ubank(u)[:, 0:S], ACT.Sigmoid).then_inc(unit_act, 1)
                    elif stage == "pt":
                        u = nth("pt", i)
                        aux_wait(u, l)
                        if i >= 2:
                            aux_wait(nth("pv", i // 2 - 1), l)
                        fn(pT[:, i % 2, :], xbank(u)[:, 0:384], ACT.Copy).then_inc(aux_act, 1)
                    elif stage == "o":
                        u = nth("o", i)
                        aux_wait(u, l)
                        fn(hK[:, i, :], xbank(u)[:, 0:S], ACT.Square).then_inc(osq_ready, 1)
                        fn(hO[:, i, :], xbank(u)[:, 0:S], ACT.Copy).then_inc(aux_act, 1)
                    elif stage == "osq":
                        u = nth("osq", i)
                        aux_wait(u, l)
                        r = hE[:, 2 * i:2 * i + 2, :].rearrange("p h s -> p (h s)")
                        fn(r, xbank(u)[:], ACT.Ln, scale=1.0 / P, bias=eps[:]).then_inc(aux_act, 1)
                        act.drain()
                        fn(r, r, ACT.Exp, scale=-0.5).then_inc(orms_ready, 1)

            def silu(f, n, up_v, free_v, up_sem, act_sem, silu_sem):
                if free_v is not None:
                    act.wait_ge(act_sem, free_v)
                act.wait_ge(up_sem, up_v)
                fn(ffn_silu[:, f % 2, 0:n], bank[f % 4][:, 0:n], ACT.Silu).then_inc(silu_sem, 1)

            def moe():
                for t in range(TT):
                    for half in range(2):
                        act.wait_ge(r_pe, 2 + 2 * t + half)
                        fn(u_tok[:, t, 512 * half:512 * half + 512], bank[2 * t + half][:], ACT.Copy).then_inc(r_act, 1)
                act.wait_ge(r_dve, 2)
                fn(ex, ex, ACT.Exp).then_inc(r_act, 1)
                act.wait_ge(route_ready, 1)
                fullest = act.value_load(flag[0:1, 0:1], min_val=0, max_val=S)
                with act.If(fullest <= CAP):
                    with act.Fori(0, NE) as e:
                        for f in range(TE):
                            silu(f, CAP, TE * e + f + 1, TE * e + f - 1 if f >= 2 else None, m_up, m_act, m_silu)
                        act.wait_ge(m_down, TE * e + TE)
                        for half in range(2):
                            fn(y_slot[:, 4 * half:4 * half + 4, :],
                               bank[4 + half][:, 0:4 * CAP].rearrange("p (d n) -> p d n", d=4), ACT.Copy).then_inc(y_ready, 1)
                        for half in range(2):
                            act.wait_ge(y_tr, 2 * e + half + 1)
                            fn(y_tok[:, 512 * half:512 * half + 512], bank[6 + half][0:CAP, :], ACT.Copy).then_inc(y_tok_ready, 1)
                with act.Else():
                    with act.Fori(0, NE) as e:
                        for f in range(TE):
                            silu(f, S, TE * e + f + 1, TE * e + f - 1 if f >= 2 else None, m_up, m_act, m_silu)
                act.drain()

            with act.Fori(0, DEPTH) as l:
                act.wait_ge(h_ready, 8 * l + 8)
                squares()
                rms(xbank(X_SSQ), X_SSQ, l, 0, None)
                mixer(l)
                act.wait_ge(h_mix, 8 * l + 8)
                squares()
                rms(xbank(X_FFN), X_FFN, l, 1, None)
                with act.If(l < 1):
                    for f in range(TD):
                        silu(f, S, f + 1, f - 1 if f >= 2 else None, d_up, d_act, d_silu)
                with act.Else():
                    moe()
                act.wait_ge(h_ffn, 4 * NE * l + 4)
                squares()
                rms(xbank(X_PLE), X_PLE, l, 2, None)
                for i in range(DT):
                    unit_wait(U_PG + i, l)
                    fn(gA[:, i, :], ubank(U_PG + i)[:, 0:S], ACT.Sigmoid).then_inc(unit_act, 1)
            act.wait_ge(h_ready, 8 * DEPTH + 8)
            squares()
            rms(xbank(0), 0, DEPTH, 0, None)
            act.wait_ge(row_ready, 4)
            act.dma_start(out.rearrange("(t p) n -> p t n", p=P), out_rows).then_inc(out_done, 16)
            act.wait_ge(out_done, 16)

        @block.gpsimd
        def _(pool):
            pool.memset(eps[:], EPS).then_inc(set_const, 1)
            pool.memset(pm[:], 0.0).then_inc(set_const, 1)
            pool.wait_ge(bias_row_ready, 1)
            pool.dma_start(bias_rows_dram, bias_out.unsqueeze(1).to_broadcast([QH, P, 384])).then_inc(bias_rows_out, 16)
            pool.wait_ge(bias_rows_out, 16)
            both = bass.AP(tensor=bias_rows_dram.tensor, offset=P - 1, ap=[[383, P], [384 * P, QH], [1, 2 * P]])
            own = bass.AP(tensor=bias_rows_dram.tensor, offset=2 * P - 1, ap=[[383, P], [384 * P, QH], [1, P]])
            pool.dma_start(bias[:, :, P:3 * P], both).then_inc(bias_in, 16)
            pool.dma_start(bias[:, :, 0:P], own).then_inc(bias_in, 16)
            with pool.Fori(0, DEPTH) as l:
                pool.wait_ge(consts_in, 16)
                await_unit_read(pool, U_HI + 3, l)
                for i in range(HH * TT):
                    h, t = i // 2, i % 2
                    if i >= 2:
                        pool.wait_ge(kv_done, 16 * l + 2 * (i - 1))
                    v = hV[:, t, h * P:(h + 1) * P].unsqueeze(1).to_broadcast([P, CPT, P])
                    m = chunk_mask.unsqueeze(2).to_broadcast([P, CPT, P])
                    pool.tensor_tensor(vx[:, i % 2], v, m, ALU.mult).then_inc(vx_ready, 1)

        @block.vector
        def _(dve):
            v = nc.vector

            dve.wait_ge(setup_pe, 1)
            raw = bank[0]
            v.tensor_copy(params[:, :, 0:VROWS], raw[:, 0:R_LB].rearrange("p (l n) -> p l n", l=DEPTH))
            v.tensor_copy(fin_gain[:], raw[:, R_FIN:R_FIN + DT])
            v.tensor_copy(lbt[:, 0:2, :], raw[:, R_LB:R_FIN].rearrange("p (l n) -> p l n", l=DEPTH))
            dve.drain()
            v.tensor_tensor(lbt[:, 2, :], lbt[:, 0, :], lbt[:, 1, :], ALU.max)
            dve.drain()
            for l in range(DEPTH):
                last = v.tensor_tensor(lbt[:, l, :], lbt[:, l, :], lbt[:, 2, :], ALU.subtract)
            last.then_inc(setup_dve, 1)
            dve.wait_ge(setup_pe, 2)
            dve.wait_ge(sc_in, 48)
            v.tensor_tensor(bias_out, bank[7][0:QH, 0:384], mask_row, ALU.add).then_inc(bias_row_ready, 1)
            for j in range(DT // 2):
                dve.wait_ge(setup_pe, 3 + j)
                v.tensor_copy(hT[:, 2 * j:2 * j + 2, :], bank[1 + j][:].rearrange("p (k s) -> p k s", k=2)).then_inc(h_ready, 2)
            for l in range(DEPTH):
                dve.wait_ge(setup_pe, 3 + DT // 2 + l)
                v.tensor_copy(p_T[:, l], bank[5 + l][:].rearrange("p (k s) -> p k s", k=KP))
            dve.wait_ge(lb_exp, 1)
            v.tensor_tensor(lbt[:, 2, :], lbt[:, 0, :], lbt[:, 1, :], ALU.add)
            dve.drain()
            v.reciprocal(lbt[:, 2, :], lbt[:, 2, :])
            dve.drain()
            for l in range(DEPTH):
                v.tensor_tensor(lbt[:, l, :], lbt[:, l, :], lbt[:, 2, :], ALU.mult)
            dve.drain()
            v.tensor_tensor(lbt[:, 2, :], lbt[:, 0, :], lbt[:, 1, :], ALU.add)
            v.tensor_tensor(params[:, 0, LB:LB + HH], lbt[:, 0, :], lbt[:, 0, :], ALU.subtract)
            dve.drain()
            v.tensor_tensor(params[:, 1, LB:LB + HH], lbt[:, 2, :], lbt[:, 0, :], ALU.subtract)
            dve.drain()
            v.tensor_scalar(params[:, :, OMLB:OMLB + HH], params[:, :, LB:LB + HH], -1.0, 1.0, ALU.mult, ALU.add)
            dve.drain()
            dve.wait_ge(small_in, 32)
            dve.wait_ge(set_const, 2)
            dve.wait_ge(bias_in, 32)

            def normed(dst, gains, n, sem_):
                dve.wait_ge(rms_ready, n)
                for k in range(DT):
                    v.scalar_tensor_tensor(dst[:, k, :], hT[:, k, :], gains[:, k:k + 1], rstd[:], ALU.mult,
                                           ALU.mult).then_inc(sem_, 1)

            def unit_wait(u, l):
                dve.wait_ge(unit_done, NU * l + u + 1)

            def aux_wait(u, l):
                dve.wait_ge(aux_done, NX * l + u + 1)

            def mixer(l):
                for stage, i in STEPS:
                    if stage == "hq":
                        unit_wait(U_HQ + i, l)
                        v.tensor_copy(hQ[:, i, :], ubank(U_HQ + i)[:, 0:S]).then_inc(unit_dve, 1)
                    elif stage == "gates":
                        await_unit_read(dve, U_HF + 3, l)
                        for h in range(HH):
                            v.tensor_scalar(hF[:, h, :], hF[:, h, :], gain[:, OMLB + h:OMLB + h + 1],
                                            gain[:, LB + h:LB + h + 1], ALU.mult, ALU.add)
                        dve.drain()
                        v.tensor_scalar(hK[:], hF[:], -1.0, 1.0, ALU.mult, ALU.add).then_inc(f_ready, 1)
                    elif stage == "hi":
                        unit_wait(U_HI + i, l)
                        half, t = i // 2, i % 2
                        v.tensor_copy(hV[:, t, half * 256:half * 256 + 256], ubank(U_HI + i)[:, 0:S]).then_inc(unit_dve, 1)
                    elif stage == "scan":
                        dve.wait_ge(logf_ready, l + 1)
                        v.tensor_tensor_scan(hA[:].rearrange("p h s -> p (h s)"), scan_mask,
                                             hF[:].rearrange("p h s -> p (h s)"), 0.0, ALU.mult, ALU.add).then_inc(scan_ready, 1)
                        dve.drain()
                        a = hA[:].rearrange("p h (c t) -> p (h c) t", t=CHUNK)
                        v.tensor_tensor(hF[:].rearrange("p h (c t) -> p (h c) t", t=CHUNK),
                                        a[:, :, CHUNK - 1:CHUNK].to_broadcast([P, HH * NCH, CHUNK]), a,
                                        ALU.subtract).then_inc(diff_ready, 1)
                    elif stage == "decay":
                        dve.wait_ge(exp_ready, 3 * l + 3)
                        v.tensor_tensor(hF[:], hF[:], hK[:], ALU.mult).then_inc(kdec_ready, 1)
                        v.tensor_tensor(hKi[:], hKi[:], hK[:], ALU.mult)
                        v.tensor_copy(dec[:], hE[:].rearrange("p h (c t) -> p (h c) t", t=CHUNK)[:, :, CHUNK - 1])
                        v.tensor_tensor(hQ[:], hQ[:], hE[:], ALU.mult).then_inc(hgrn_ready, 1)
                    elif stage == "ak":
                        unit_wait(U_AK + i, l)
                        v.tensor_copy(aK[:, i, :], ubank(U_AK + i)[:, 0:S]).then_inc(unit_dve, 1)
                    elif stage == "av":
                        unit_wait(U_AV + i, l)
                        v.tensor_copy(aV[:, i, :], ubank(U_AV + i)[:, 0:P]).then_inc(unit_dve, 1)
                    elif stage == "p":
                        u = nth("p", i)
                        dve.drain()
                        aux_wait(u, l)
                        v.tensor_copy(rstd[:], xbank(u)[:, 0:S]).then_inc(aux_dve, 1)
                        dve.drain()
                        v.copy_predicated(pm[:, i], hg_mask.bitcast(U32).unsqueeze(1).to_broadcast([P, TT, P]),
                                          rstd[:].rearrange("p (t n) -> p t n", t=TT)).then_inc(pm_ready, 1)
                    elif stage == "kv":
                        h, t, half = i // 4, i // 2 % 2, i % 2
                        dve.drain()
                        dve.wait_ge(kv_done, 16 * l + i + 1)
                        if i % 4 == 0 and h >= 2:
                            aux_wait(nth("o", h - 2), l)
                        for j in range(4):
                            c = t * CPT + half * 4 + j
                            if c == NCH - 1:
                                continue
                            src = bank[6 + i % 2][:, j * P:(j + 1) * P]
                            if c == 0:
                                last = v.tensor_copy(state[:, h % 2, 0, :], src)
                            else:
                                if j:
                                    dve.drain()
                                last = v.scalar_tensor_tensor(
                                    state[:, h % 2, c, :], state[:, h % 2, c - 1, :],
                                    dec[:, h * NCH + c:h * NCH + c + 1], src, ALU.mult, ALU.add)
                        last.then_inc(state_ready, 1)
                    elif stage == "sc":
                        u = nth("sc", i)
                        aux_wait(u, l)
                        v.tensor_tensor(sc[:, i, :], xbank(u)[:, 0:384], bias[:, i, :], ALU.add).then_inc(aux_dve, 1)
                    elif stage == "softmax":
                        dve.drain()
                        v.tensor_reduce(smax[:, 0, 0:QH], sc[:, :, 0:P], AX.X, ALU.max)
                        v.tensor_reduce(smax[:, 0, QH:2 * QH], sc[:, :, P:P + S], AX.X, ALU.max)
                        dve.drain()
                        own_sink = sink[:, bass.ds(l, 1), :].to_broadcast([P, 2, QH])
                        top = smax[:, 0, :].rearrange("p (b h) -> p b h", b=2)
                        v.tensor_tensor(top, top, own_sink, ALU.max)
                        dve.drain()
                        v.tensor_scalar(smax[:, 1, :], smax[:, 0, :], -1.0, None, ALU.mult)
                        v.tensor_tensor(smax[:, 3, :].rearrange("p (b h) -> p b h", b=2), own_sink, top, ALU.subtract)
                        dve.drain()
                        v.tensor_copy(smax[:, 5, :], smax[:, 1, :]).then_inc(max_ready, 1)
                        dve.wait_ge(exp_done, l + 1)
                        v.tensor_tensor(smax[:, 4, :], smax[:, 2, :], smax[:, 3, :], ALU.add)
                        dve.drain()
                        v.reciprocal(smax[:, 4, :], smax[:, 4, :])
                        dve.drain()
                        v.tensor_tensor(sc[:, :, 0:P], sc[:, :, 0:P],
                                        smax[:, 4, 0:QH].unsqueeze(2).to_broadcast([P, QH, P]), ALU.mult)
                        v.tensor_tensor(sc[:, :, P:P + S], sc[:, :, P:P + S],
                                        smax[:, 4, QH:2 * QH].unsqueeze(2).to_broadcast([P, QH, S]),
                                        ALU.mult).then_inc(prob_ready, 1)
                    elif stage == "hg":
                        dve.wait_ge(gate_sig, 4 * l + i + 1)
                        v.tensor_tensor(hG[:, i, :], hG[:, i, :], ubank(U_HG + i)[:, 0:S], ALU.mult).then_inc(unit_dve, 1)
                    elif stage == "pv":
                        u = nth("pv", i)
                        aux_wait(u, l)
                        v.tensor_copy(aO[:, i, :], xbank(u)[:, 0:S]).then_inc(aux_dve, 1)
                    elif stage == "ynorm":
                        dve.wait_ge(orms_ready, 2 * l + 2)
                        v.tensor_tensor(hO[:], hO[:], hE[:], ALU.mult)
                        dve.drain()
                        v.scalar_tensor_tensor(hO[:], hO[:], gain[:, G_HN:G_HN + 1], hG[:], ALU.mult,
                                               ALU.mult).then_inc(yb_ready, 1)
                    elif stage == "ya":
                        await_unit_read(dve, U_GA + i, l)
                        unit_wait(U_YA + i, l)
                        v.tensor_tensor(gA[:, i, :], gA[:, i, :], ubank(U_YA + i)[:, 0:S], ALU.mult).then_inc(unit_dve, 1)
                    elif stage == "yb":
                        await_unit_read(dve, U_GB + i, l)
                        unit_wait(U_YB + i, l)
                        v.tensor_tensor(gB[:, i, :], gB[:, i, :], ubank(U_YB + i)[:, 0:S], ALU.mult).then_inc(unit_dve, 1)
                        dve.drain()
                        v.tensor_tensor(uT[:, i, :], gA[:, i, :], gB[:, i, :], ALU.add).then_inc(merged, 1)
                    elif stage == "wo":
                        unit_wait(U_WO + i, l)
                        v.tensor_tensor(hT[:, i, :], hT[:, i, :], ubank(U_WO + i)[:, 0:S], ALU.add).then_inc(unit_dve, 1)
                dve.drain()
                v.tensor_copy(smax[:, 5, 0:1], smax[:, 1, 0:1]).then_inc(h_mix, 8)

            def gated(f, n, silu_v, free_v, silu_sem, down_sem, act_sem, by_row=False):
                if free_v is not None:
                    dve.wait_ge(down_sem, free_v)
                dve.wait_ge(silu_sem, silu_v)
                last = v.tensor_tensor(ffn_act[:, f % 2, 0:n], ffn_silu[:, f % 2, 0:n], bank[f % 4][:, n:2 * n], ALU.mult)
                if by_row:
                    dve.drain()
                    last = v.tensor_tensor(ffn_act[:, f % 2, 0:n], ffn_act[:, f % 2, 0:n], gate_row, ALU.mult)
                last.then_inc(act_sem, 1)

            def add_to_h(j):
                v.tensor_tensor(hT[:, 2 * j:2 * j + 2, :], hT[:, 2 * j:2 * j + 2, :],
                                bank[4 + j][:].rearrange("p (k s) -> p k s", k=2), ALU.add).then_inc(h_ffn, 1)

            def moe():
                dve.wait_ge(r_pe, 1)
                v.tensor_copy(logit, bank[4][:, 0:TT * NE].rearrange("p (t e) -> p t e", t=TT))
                dve.drain()
                for t in range(TT):
                    v.max(top8[:, t, :], logit[:, t, :])
                dve.drain()
                for t in range(TT):
                    v.max_index(idx8[:, t, :], top8[:, t, :], logit[:, t, :])
                dve.drain()
                v.tensor_copy(idxf, idx8[:])
                dve.drain()
                for t in range(TT):
                    v.tensor_scalar(tmp8[:, t, :], expert_iota, idxf[:, t, 0:1], None, ALU.is_equal)
                    v.tensor_scalar(picked[:, t, :], expert_iota, idxf[:, t, 1:2], None, ALU.is_equal)
                    v.tensor_scalar(ex[:, t, :], logit[:, t, :], top8[:, t, 0:1], None, ALU.subtract)
                dve.drain()
                v.tensor_tensor(picked, picked, tmp8, ALU.add).then_inc(r_dve, 1)
                dve.drain()
                v.tensor_tensor(ex, ex, picked, ALU.mult).then_inc(r_dve, 1)
                dve.wait_ge(r_act, 5)
                v.tensor_tensor(gate, ex, picked, ALU.mult)
                dve.drain()
                v.tensor_reduce(den[:, :, 0], gate, AX.X, ALU.add)
                dve.drain()
                v.reciprocal(den[:, :, 0], den[:, :, 0])
                dve.drain()
                for t in range(TT):
                    v.tensor_scalar(gate[:, t, :], gate[:, t, :], den[:, t, 0:1], None, ALU.mult)
                dve.wait_ge(r_pe, 6)
                v.tensor_copy(pos, bank[5][:, 0:16].rearrange("p (t e) -> p t e", t=TT))
                v.tensor_copy(cnt[:], bank[5][:, 16:24])
                dve.drain()
                v.tensor_reduce(flag[:], cnt[:], AX.X, ALU.max).then_inc(route_ready, 1)
                dve.wait_ge(route_ready, 1)
                fullest = dve.value_load(flag[0:1, 0:1], min_val=0, max_val=S)
                with dve.If(fullest <= CAP):
                    with dve.Fori(0, NE) as e:
                        for t in range(TT):
                            v.tensor_scalar(sel_slot[:, t, :], slot_iota, pos[:, t, bass.ds(e, 1)],
                                            picked[:, t, bass.ds(e, 1)], ALU.is_equal, ALU.mult)
                        dve.drain()
                        for t in range(TT):
                            last = v.tensor_scalar(gate_slot[:, t, :], sel_slot[:, t, :], gate[:, t, bass.ds(e, 1)],
                                                   None, ALU.mult)
                        last.then_inc(slots_ready, 1)
                        for half in range(2):
                            dve.wait_ge(gathered, 2 * e + half + 1)
                            v.tensor_copy(u_slot[:, 4 * half:4 * half + 4, :],
                                          bank[6 + half][:, 0:4 * CAP].rearrange("p (d n) -> p d n", d=4)
                                          ).then_inc(u_slot_ready, 1)
                        for f in range(TE):
                            gated(f, CAP, TE * e + f + 1, TE * e + f - 1 if f >= 2 else None, m_silu, m_down, m_act)
                        dve.wait_ge(comb_tr, e + 1)
                        v.tensor_copy(comb, bank[0][0:CAP, 0:S]).then_inc(comb_ready, 1)
                        for j in range(4):
                            dve.wait_ge(comb_done, 4 * e + j + 1)
                            add_to_h(j)
                        dve.drain()
                with dve.Else():
                    with dve.Fori(0, NE) as e:
                        for t in range(TT):
                            last = v.tensor_scalar(gate_cols[:, t, :], ones, gate[:, t, bass.ds(e, 1)], None, ALU.mult)
                        last.then_inc(slots_ready, 1)
                        dve.wait_ge(gathered, e + 1)
                        v.tensor_copy(gate_row, bank[3][:, 0:S]).then_inc(u_slot_ready, 1)
                        dve.drain()
                        for f in range(TE):
                            gated(f, S, TE * e + f + 1, TE * e + f - 1 if f >= 2 else None, m_silu, m_down, m_act, True)
                        dve.wait_ge(m_down, TE * e + TE)
                        for j in range(4):
                            add_to_h(j)
                        dve.drain()
                dve.drain()

            with dve.Fori(0, DEPTH) as l:
                v.tensor_copy(gain[:], params[:, bass.ds(l, 1), :].rearrange("p a n -> p (a n)"))
                dve.drain()
                normed(uT, gain[:, G_MIX:G_MIX + DT], 3 * l + 1, u_ready)
                mixer(l)
                normed(uT, gain[:, G_FFN:G_FFN + DT], 3 * l + 2, u_ready)
                with dve.If(l < 1):
                    for f in range(TD):
                        gated(f, S, f + 1, f - 1 if f >= 2 else None, d_silu, d_down, d_act)
                    dve.wait_ge(d_down, TD)
                    for j in range(4):
                        add_to_h(j)
                with dve.Else():
                    moe()
                normed(uT, gain[:, G_PLE:G_PLE + DT], 3 * l + 3, u_ready)
                for i in range(DT):
                    await_unit_read(dve, U_PG + i, l)
                    unit_wait(U_PP + i, l)
                    v.tensor_tensor(gA[:, i, :], gA[:, i, :], ubank(U_PP + i)[:, 0:S], ALU.mult).then_inc(unit_dve, 1)
                    dve.drain()
                    v.tensor_tensor(hT[:, i, :], hT[:, i, :], gA[:, i, :], ALU.add).then_inc(h_ready, 1)
                dve.drain()
            normed(uT, fin_gain[:], 3 * DEPTH + 1, fin_ready)
            dve.wait_ge(fin_tr, 1)
            for t in range(TT):
                for half in range(2):
                    b = bank[4 + half] if t == 0 else bank[6 + half]
                    v.tensor_copy(out_rows[:, t, 512 * half:512 * half + 512], b[:]).then_inc(row_ready, 1)


def constants():
    c = np.zeros((P, C_N), np.float32)
    i = np.arange(P)
    c[:, C_ID:C_ID + P] = np.eye(P)
    c[:, C_ONE:C_ONE + P] = 1
    c[:, C_LT:C_LT + P] = i[:, None] < i[None, :]
    c[:, C_HM:C_HM + P] = (i[:, None] // CHUNK == i[None, :] // CHUNK) & (i[:, None] <= i[None, :])
    c[:, C_CM:C_CM + CPT] = i[:, None] // CHUNK == np.arange(CPT)
    c[:, C_IO:C_IO + CAP] = np.arange(CAP)
    c[:, C_SC:C_SC + HH * S] = np.arange(HH * S) % CHUNK != 0
    c[:, C_I8:C_I8 + NE] = np.arange(NE)
    return c


def bias_tables():
    dist = 2 * P - 1 - np.arange(384)
    exact = BUCKETS // 2
    d = np.maximum(dist, 0)
    large = exact + (np.log(np.maximum(d, 1).astype(np.float32) / np.float32(exact)) / np.float32(np.log(MAX_DIST / exact))
                     * np.float32(BUCKETS - exact)).astype(np.int32)
    bucket = np.where(d < exact, d, np.minimum(large, BUCKETS - 1))
    inside = (dist >= 0) & (dist < P)
    onehot = ((np.arange(BUCKETS)[:, None] == bucket) & inside).astype(np.float32)
    outside = np.broadcast_to(np.where(inside, 0, NEG).astype(np.float32), (QH, 384))
    return onehot, np.ascontiguousarray(outside)


def kernel(**inputs):
    import concourse.bacc as bacc
    from concourse.bass_utils import run_bass_kernel_spmd

    a = {k: np.asarray(v) for k, v in inputs.items()}
    rows = []
    for l in range(DEPTH):
        for n in ("norm_mix", "norm_ffn", "norm_ple", "hgrn_norm"):
            rows.append(a[n][l].reshape(-1, P))
    rows += [a["lb_logits"].reshape(-1, P), a["final_norm"].reshape(-1, P)]
    onehot, outside = bias_tables()
    arrays = {
        "x": a["x"][0], "p": a["p"][:, 0], "w_in": a["w_in"], "sinks": a["sinks"], "rel_bias": a["rel_bias"],
        "vectors": np.concatenate(rows), "w_branch_a": a["w_branch_a"], "w_branch_b": a["w_branch_b"],
        "w_out": a["w_out"], "dense_w1": a["dense_w1"], "dense_w3": a["dense_w3"], "dense_w2": a["dense_w2"],
        "router_w": a["router_w"], "moe_w1": a["moe_w1"], "moe_w3": a["moe_w3"], "moe_w2": a["moe_w2"],
        "ple_proj": a["ple_proj"], "ple_gate": a["ple_gate"], "consts": constants(), "buckets": onehot,
        "outside": outside,
    }
    nc = bacc.Bacc("TRN2", target_bir_lowering=False, num_devices=1)
    handles = {n: nc.dram_tensor(n, v.shape, F32, kind="ExternalInput").ap() for n, v in arrays.items()}
    out = nc.dram_tensor("out", (S, D), F32, kind="ExternalOutput").ap()
    trunk(nc, *handles.values(), out)
    r = run_bass_kernel_spmd(nc, [{n: np.ascontiguousarray(v) for n, v in arrays.items()}], core_ids=[0])
    return r.results[0]["out"].reshape(1, S, D)
```

```python
from contextlib import ExitStack

import numpy as np

import concourse.bass as bass
from concourse import mybir

F32 = mybir.dt.float32
F32R = mybir.dt.float32r
I32 = mybir.dt.int32
U32 = mybir.dt.uint32
ALU = mybir.AluOpType
ACT = mybir.ActivationFunctionType
AX = mybir.AxisListType

P = 128
D = 1024
DT = D // P
S = 256
TT = S // P
DEPTH = 2
QH, KVH, HD = 8, 2, 64
GROUP = QH // KVH
BUCKETS = 32
MAX_DIST = 128
HH = 4
CHUNK = 16
NCH = S // CHUNK
CPT = P // CHUNK
FD = 2816
FE = 3584
NE = 8
PLE = 256
KP = PLE // P
EPS = 1e-6
IN_W = 4864
O_AQ, O_AK, O_AV, O_HQ, O_HF, O_HI, O_HG, O_GA, O_GB = 0, 512, 640, 768, 1280, 1792, 2304, 2816, 3840
CAP = 128
NEG = -1e30

CHUNK_N = 2048
HALF = CHUNK_N // 2
RAW = 6
SPLIT = 3

G_MIX, G_FFN, G_PLE, G_HN, LB, OMLB = 0, 8, 16, 24, 25, 29
PCOLS = 33
VROWS = 25
R_LB = DEPTH * VROWS
R_FIN = R_LB + DEPTH * HH
NVEC = R_FIN + DT

C_ID, C_ONE, C_LT, C_HM, C_CM, C_IO, C_SC, C_I8 = 0, 128, 256, 384, 512, 520, 648, 664
C_N = 672

U_HF, U_HQ, U_HI, U_AQ, U_AK, U_AV, U_SW, U_HG, U_GA, U_GB, U_YA, U_YB, U_WO, U_PG, U_PP = (
    0, 4, 8, 12, 16, 17, 19, 20, 24, 32, 40, 48, 56, 64, 72)
UNITS = "A" * 4 + "D" * 4 + "D" * 4 + "A" * 4 + "D" * 2 + "D" * 2 + "D" * 4 + "A" * 16 + "D" * 24 + "A" * 8 + "D" * 8
NU = len(UNITS)
UA, UD = UNITS.count("A"), UNITS.count("D")

X_SSQ, X_KT, X_P, X_SC = 0, 1, 5, 9
X_O01 = 17
X_ATT = 19
X_ORDER = (["ssq"] + ["kt"] * 4 + ["p"] * 4 + ["sc"] * 8 + ["o"] * 2 + ["pt", "pt", "pv"] * 3 + ["o"] * 2
           + ["pt", "pt", "pv"] + ["osq"] * 2 + ["ssq"] * 2)
X_DRAIN = "".join("D" if k in ("p", "sc", "pv") else "A" for k in X_ORDER)
NX = len(X_ORDER)
XA, XD = X_DRAIN.count("A"), X_DRAIN.count("D")
X_FFN, X_PLE = NX - 2, NX - 1
RING = 3


def nth(kind, n):
    return [i for i, k in enumerate(X_ORDER) if k == kind][n]


def mixer_steps():
    s = [("hf", h) for h in range(4)] + [("hq", h) for h in range(4)] + [("gates", 0)]
    s += [("hi", i) for i in range(4)] + [("scan", 0)] + [("aq", i) for i in range(4)] + [("decay", 0)]
    s += [("ak", 0), ("av", 0), ("av", 1), ("swap", 0)]
    s += [("kt", h) for h in range(4)] + [("p", h) for h in range(4)]
    for h in range(8):
        s += [("sc", h), ("kv", h)]
    s += [("softmax", 0)]
    s += [("hg", 0), ("o", 0), ("hg", 1), ("o", 1), ("hg", 2), ("kv", 8), ("hg", 3), ("kv", 9)]
    s += [("ga", 0), ("kv", 10), ("ga", 1), ("kv", 11), ("ga", 2), ("pt", 0), ("pt", 1), ("pv", 0)]
    s += [("kv", 12), ("ga", 3), ("kv", 13), ("ga", 4), ("pt", 2), ("pt", 3), ("pv", 1)]
    s += [("kv", 14), ("ga", 5), ("kv", 15), ("ga", 6), ("pt", 4), ("pt", 5), ("pv", 2)]
    s += [("ga", 7), ("o", 2), ("gb", 0), ("o", 3), ("gb", 1), ("pt", 6), ("pt", 7), ("pv", 3), ("gb", 2)]
    s += [("osq", 0), ("osq", 1)] + [("gb", i) for i in range(3, 8)] + [("branch", 0), ("ynorm", 0), ("branch", 1)]
    s += [("ya", d) for d in range(8)] + [("yb", d) for d in range(4)] + [("merge", 0)]
    s += [("yb", d) for d in range(4, 8)] + [("merge", 1)] + [("wo", d) for d in range(8)]
    return s


STEPS = mixer_steps()


def ffn_order(pairs):
    out = []
    for j in range(pairs + 2):
        out += [("w1", j)] * (j < pairs) + [("w2", j - 2)] * (j >= 2) + [("w3", j)] * (j < pairs)
    return out


DENSE, EXPERT = ffn_order(FD // P // 2), ffn_order(FE // P // 2)
PD, PE_ = FD // P // 2, FE // P // 2

MIXER = []
for first_col, unit, n in ((O_HF, U_HF, 2), (O_HQ, U_HQ, 2), (O_HI, U_HI, 2), (O_AQ, U_AQ, 2), (O_AK, U_AV, 1),
                           (O_HG, U_HG, 2), (O_GA, U_GA, 4), (O_GB, U_GB, 4)):
    MIXER += [("in", first_col + 256 * i, 256, unit + 2 * i + 1) for i in range(n)]
K_YA = len(MIXER)
MIXER += [("wa", 512 * i, 512, U_YA + 4 * i + 3) for i in range(2)]
K_YB = len(MIXER)
MIXER += [("wb", 512 * i, 512, U_YB + 4 * i + 3) for i in range(2)]
K_WO = len(MIXER)
MIXER += [("wo", 256 * i, 256, U_WO + 2 * i + 1) for i in range(4)]
EMBED = [("pg", 256 * i, 256, U_PG + 2 * i + 1) for i in range(4)] + [("pp", 512 * i, 512, U_PP + 4 * i + 3) for i in range(2)]
K_HF, K_HQ, K_HI, K_AQ, K_AK, K_HG, K_GA, K_GB = (
    [c for m, c, _, _ in MIXER if m == "in"].index(o) for o in (O_HF, O_HQ, O_HI, O_AQ, O_AK, O_HG, O_GA, O_GB))
NM, ND, NX_E, NP = len(MIXER), len(DENSE), len(EXPERT), len(EMBED)
assert all(n % SPLIT == 0 and 2 * n % RAW == 0 for n in (NM, ND, NX_E, NP))
LAYER_CHUNKS = NM + ND + NP
K_DENSE, K_EMBED = NM, NM + ND
K_EXPERTS = LAYER_CHUNKS + NM
EMBED_STEP = LAYER_CHUNKS + NE * NX_E - ND

UNIT_OF = {"hf": U_HF, "hq": U_HQ, "hi": U_HI, "aq": U_AQ, "ak": U_AK, "av": U_AV, "swap": U_SW, "hg": U_HG,
           "ga": U_GA, "gb": U_GB, "ya": U_YA, "yb": U_YB, "wo": U_WO}
LAST_OF = {unit: n for n, (_, _, _, unit) in enumerate(MIXER + EMBED)}


def trunk(nc, x, p, w_in, sinks, rel_bias, vectors, w_branch_a, w_branch_b, w_out, dense_w1, dense_w3,
          dense_w2, router_w, moe_w1, moe_w3, moe_w2, ple_proj, ple_gate, consts, buckets, outside, out):
    ctx = ExitStack()
    with ctx:
        def sb(name, shape, dt=F32):
            return ctx.enter_context(nc.sbuf_tensor(name, shape, dt))

        def sem(name):
            return ctx.enter_context(nc.semaphore(name))

        bias_rows_dram = nc.dram_tensor("bias_rows_dram", (QH, P, 384), F32, kind="Internal").ap()

        raw_ring = sb("raw_ring", [P, RAW, HALF])
        w_hi = sb("w_hi", [P, SPLIT, CHUNK_N], F32R)
        w_lo = sb("w_lo", [P, SPLIT, CHUNK_N], F32R)
        hT = sb("hT", [P, DT, S])
        u_hi = sb("u_hi", [P, DT, S], F32R)
        u_lo = sb("u_lo", [P, DT, S], F32R)
        rstd = sb("rstd", [P, S])
        consts_sb = sb("consts_sb", [P, C_N])
        ident, ones = consts_sb[:, C_ID:C_ID + P], consts_sb[:, C_ONE:C_ONE + P]
        before = consts_sb[:, C_LT:C_LT + P]
        hg_mask = consts_sb[:, C_HM:C_HM + P]
        chunk_mask = consts_sb[:, C_CM:C_CM + CPT]
        slot_iota = consts_sb[:, C_IO:C_IO + CAP]
        scan_mask = consts_sb[:, C_SC:C_SC + CHUNK]
        expert_iota = consts_sb[:, C_I8:C_I8 + NE]
        eps = sb("eps", [P, 1])
        params = sb("params", [P, DEPTH, PCOLS])
        fin_gain = sb("fin_gain", [P, DT])
        gain = sb("gain", [P, PCOLS])
        vec_rows = sb("vec_rows", [P, P])
        lbt = sb("lbt", [P, 3, HH])
        sink = sb("sink", [P, DEPTH, QH])
        p_T = sb("p_T", [P, DEPTH, KP, S])
        rw = sb("rw", [P, DT, NE])
        bias = sb("bias", [P, QH, 384])
        pm = sb("pm", [P, HH, TT, P])
        smax = sb("smax", [P, 6, 2 * QH])
        gA = sb("gA", [P, DT, S])
        gB = sb("gB", [P, DT, S])
        rt = sb("rt", [P, 8, TT, NE + 1])
        idx8 = sb("idx8", [P, TT, NE], U32)
        cnt = sb("cnt", [P, NE])
        flag = sb("flag", [P, 1], I32)

        mixer_memory = ExitStack()

        def msb(name, shape, dt=F32):
            return mixer_memory.enter_context(nc.sbuf_tensor(name, shape, dt))

        hF = msb("hF", [P, HH, S])
        hK = msb("hK", [P, HH, S])
        hA = msb("hA", [P, HH, S])
        hE = msb("hE", [P, HH, S])
        hKi = msb("hKi", [P, HH, S])
        hQ = msb("hQ", [P, HH, S])
        hV = msb("hV", [P, TT, HH * P])
        hG = msb("hG", [P, HH, S])
        kend = hA[:].rearrange("p h s -> p (h s)").rearrange("p (t n) -> p t n", t=TT)
        hO = hF
        chunk_starts = hG[:].rearrange("p h s -> p (h s)")
        dec = msb("dec", [P, HH * NCH])
        vx = msb("vx", [P, 2, 4, P])
        state = msb("state", [P, 2, NCH - 1, P])
        aQ = hG
        aK = msb("aK", [P, KVH, S])
        aV = msb("aV", [P, TT, KVH * HD])
        sc = msb("sc", [P, QH, 384])
        pT = msb("pT", [P, 2, 384])
        aO = hKi
        mixer_memory.close()
        act2 = sb("act2", [P, 2, 2, S])
        act_hi = sb("act_hi", [P, 2, 2, S], F32R)
        act_lo = sb("act_lo", [P, 2, 2, S], F32R)
        gate_cols = sb("gate_cols", [P, TT, P])
        gate_row = sb("gate_row", [P, S])
        p_hi = sb("p_hi", [P, KP, S], F32R)
        p_lo = sb("p_lo", [P, KP, S], F32R)
        us = sb("us", [P, DT, CAP])
        us_hi = sb("us_hi", [P, DT, CAP], F32R)
        us_lo = sb("us_lo", [P, DT, CAP], F32R)
        slot_act = sb("slot_act", [P, 2, 2 * P])
        y_tok = sb("y_tok", [P, D])
        comb = sb("comb", [P, S])
        sel_slot = sb("sel_slot", [P, TT, CAP])
        gate_slot = sb("gate_slot", [P, TT, CAP])
        x_in = gA[:].rearrange("p d s -> p (d s)").rearrange("p (t n) -> p t n", t=TT)
        p_in = hG[:].rearrange("p d s -> p (d s)").rearrange("p (l t n) -> p l t n", l=DEPTH, t=TT)
        out_rows = x_in
        onehot = sc[0:BUCKETS, 0, :]
        bias_out = sc[0:QH, 1, :]
        rel_sb = sc[0:BUCKETS, 2, 0:QH]
        mask_row = sc[0:QH, 3, :]
        u_tok = x_in
        logit, top8, picked, gate, pos, ex, tmp8 = (rt[:, i, :, 0:NE] for i in range(7))
        picked_wide, pos_wide = rt[:, 2], rt[:, 4]
        idxf = rt[:, 7, :, 0:NE]
        den = sb("den", [P, TT])

        bank = [ctx.enter_context(nc.psum_tensor(f"bank{i}", [P, 512], F32)) for i in range(8)]

        raw_loaded = [sem(f"raw_loaded{i}") for i in range(RAW)]
        hi_done, lo_done = sem("hi_done"), sem("lo_done")
        consts_in, vec_in, x_loaded, small_in, p_loaded, sc_in = (
            sem(n) for n in ("consts_in", "vec_in", "x_loaded", "small_in", "p_loaded", "sc_in"))
        setup_pe, setup_dve, lb_exp, bias_row_ready, bias_rows_out, bias_in, set_const = (
            sem(n) for n in ("setup_pe", "setup_dve", "lb_exp", "bias_row_ready", "bias_rows_out", "bias_in", "set_const"))
        h_ready, h_mix, h_ffn = sem("h_ready"), sem("h_mix"), sem("h_ffn")
        sq_ready, rms_ready, u_ready = sem("sq_ready"), sem("rms_ready"), sem("u_ready")
        u_normed, u_hi_ready = sem("u_normed"), sem("u_hi_ready")
        branch_hi, branch_ready, merge_hi, merge_ready = (
            sem(n) for n in ("branch_hi", "branch_ready", "merge_hi", "merge_ready"))
        unit_done, unit_act, unit_dve = sem("unit_done"), sem("unit_act"), sem("unit_dve")
        aux_done, aux_act, aux_dve = sem("aux_done"), sem("aux_act"), sem("aux_dve")
        f_ready, logf_ready, scan_ready, exp_ready, diff_ready, kdec_ready, hgrn_ready = (
            sem(n) for n in ("f_ready", "logf_ready", "scan_ready", "exp_ready", "diff_ready", "kdec_ready", "hgrn_ready"))
        pm_ready, vx_ready, kv_done, state_ready = sem("pm_ready"), sem("vx_ready"), sem("kv_done"), sem("state_ready")
        gate_sig, max_ready, exp_done, prob_ready = sem("gate_sig"), sem("max_ready"), sem("exp_done"), sem("prob_ready")
        osq_ready, orms_ready, yb_ready, merged = sem("osq_ready"), sem("orms_ready"), sem("yb_ready"), sem("merged")
        d_used, d_silu, d_mul, d_hi, d_act = (sem(n) for n in ("d_used", "d_silu", "d_mul", "d_hi", "d_act"))
        m_used, m_silu, m_mul, m_hi, m_act = (sem(n) for n in ("m_used", "m_silu", "m_mul", "m_hi", "m_act"))
        act_turned, starts_ready = sem("act_turned"), sem("starts_ready")
        p_hi_ready, p_split = sem("p_hi_ready"), sem("p_split")
        r_pe, r_act, r_dve, route_ready = sem("r_pe"), sem("r_act"), sem("r_dve"), sem("route_ready")
        slots_ready, gathered, us_copied, us_hi_ready, us_ready = (
            sem(n) for n in ("slots_ready", "gathered", "us_copied", "us_hi_ready", "us_ready"))
        y_act, y_dve, comb_tr, comb_ready, comb_done = (
            sem(n) for n in ("y_act", "y_dve", "comb_tr", "comb_ready", "comb_done"))
        fin_ready, fin_tr, row_ready, out_done = sem("fin_ready"), sem("fin_tr"), sem("row_ready"), sem("out_done")

        def wview(n, tiles, cols):
            return [w[:, n % SPLIT, 0:tiles * cols].rearrange("p (k n) -> p k n", k=tiles) for w in (w_hi, w_lo)]

        def columns(w, c0, n):
            return [part[:, :, c0:c0 + n] for part in w]

        def await_chunk(eng, n, turns):
            eng.wait_ge(lo_done, 2 * (n + 1) + RAW * turns)

        def half_views(n, half, size):
            at = slice(half * size, (half + 1) * size)
            return raw_ring[:, (2 * n + half) % RAW, 0:size], w_hi[:, n % SPLIT, at], w_lo[:, n % SPLIT, at]

        def await_unit_free(eng, u, l):
            if u >= RING:
                n = u - RING
                if UNITS[n] == "A":
                    eng.wait_ge(unit_act, UA * l + UNITS[:n + 1].count("A"))
                else:
                    eng.wait_ge(unit_dve, UD * l + UNITS[:n + 1].count("D"))

        def await_unit_read(eng, u, l):
            if UNITS[u] == "A":
                eng.wait_ge(unit_act, UA * l + UNITS[:u + 1].count("A"))
            else:
                eng.wait_ge(unit_dve, UD * l + UNITS[:u + 1].count("D"))

        def await_aux_free(eng, u, l):
            if u >= RING:
                await_aux_read(eng, u - RING, l)

        def await_aux_read(eng, u, l):
            if X_DRAIN[u] == "A":
                eng.wait_ge(aux_act, XA * l + X_DRAIN[:u + 1].count("A"))
            else:
                eng.wait_ge(aux_dve, XD * l + X_DRAIN[:u + 1].count("D"))

        def ubank(u):
            return bank[u % RING]

        def xbank(u):
            return bank[3 + u % RING]

        block = ctx.enter_context(nc.Block())

        @block.sync
        def _(sp):
            src = {"in": w_in, "wo": w_out, "pg": ple_gate, "wa": w_branch_a, "wb": w_branch_b, "pp": ple_proj}

            def load(n, turns, chunk_dst_k, source, cols):
                for half in range(2):
                    i = 2 * n + half
                    if i >= RAW:
                        sp.wait_ge(lo_done, i - RAW + 1 + RAW * turns)
                    k = chunk_dst_k // 2
                    dst = raw_ring[:, i % RAW, 0:k * cols].rearrange("p (k n) -> p k n", k=k)
                    sp.dma_start(dst, source[:, half * k:(half + 1) * k, :]).then_inc(raw_loaded[i % RAW], 16)

            def by_columns(table, l, n0):
                for i, (matrix, c0, cols, _) in enumerate(table):
                    w = src[matrix][l].rearrange("(k p) n -> p k n", p=P)
                    load(n0 + i, 0, w.shape[1], w[:, :, c0:c0 + cols], cols)

            def swiglu(order, n0, turns, w1, w3, w2):
                for i, (m, j) in enumerate(order):
                    if m == "w2":
                        source = w2[2 * j * P:(2 * j + 2) * P, :].rearrange("(k p) n -> p k n", p=P)
                        load(n0 + i, turns, 2, source, D)
                    else:
                        w = {"w1": w1, "w3": w3}[m].rearrange("(k p) n -> p k n", p=P)
                        load(n0 + i, turns, DT, w[:, :, 2 * j * P:(2 * j + 2) * P], 2 * P)

            by_columns(MIXER, 0, 0)
            swiglu(DENSE, K_DENSE, 0, dense_w1[0], dense_w3[0], dense_w2[0])
            by_columns(EMBED, 0, K_EMBED)
            by_columns(MIXER, 1, LAYER_CHUNKS)
            with sp.Fori(0, NE) as e:
                swiglu(EXPERT, K_EXPERTS, NX_E // SPLIT * e, moe_w1[0, e], moe_w3[0, e], moe_w2[0, e])
            by_columns(EMBED, 1, K_EMBED + EMBED_STEP)

        mixer_turns = lambda l: LAYER_CHUNKS // SPLIT * l
        embed_turns = lambda l: EMBED_STEP // SPLIT * l

        @block.tensor
        def _(pe):
            mm = nc.tensor.matmul

            def product(dst, stationary, moving, tiles, await_k=None, start=True, stop=True):
                (s_hi, s_lo), (m_hi_part, m_lo_part) = stationary, moving
                for k in range(tiles):
                    if await_k:
                        await_k(k)
                    mm(dst, s_hi[:, k, :], m_hi_part[:, k, :], start=start and k == 0, stop=False, skip_group_check=True)
                    mm(dst, s_hi[:, k, :], m_lo_part[:, k, :], start=False, stop=False, skip_group_check=True)
                    last = mm(dst, s_lo[:, k, :], m_hi_part[:, k, :], start=False, stop=stop and k == tiles - 1,
                              skip_group_check=True)
                return last

            stream = [u_hi, u_lo]

            def transpose(dst, a, parts=P):
                return nc.tensor.transpose(dst, a, consts_sb[0:parts, C_ID:C_ID + parts])

            def sum_of_squares(norm, unit, l):
                await_aux_free(pe, unit, l)
                for k in range(DT):
                    if k % 4 == 0:
                        pe.wait_ge(sq_ready, 6 * l + 2 * norm + k // 4 + 1)
                    last = mm(xbank(unit)[:, 0:S], ones, gA[:, k, :], start=(k == 0), stop=(k == DT - 1))
                last.then_inc(aux_done, 1)

            def unit_product(n, l, stationary, moving, tiles, await_k=None):
                await_unit_free(pe, n, l)
                product(ubank(n)[:, 0:S], stationary, moving, tiles, await_k).then_inc(unit_done, 1)

            def await_u(norm, l):
                def wait(k):
                    if k % 2 == 0:
                        pe.wait_ge(u_ready, 12 * l + 4 * norm + k // 2 + 1)
                return wait

            pe.wait_ge(consts_in, 16)
            pe.wait_ge(vec_in, 16)
            transpose(bank[0][:, 0:NVEC], vec_rows[0:NVEC, :], NVEC).then_inc(setup_pe, 1)
            pe.wait_ge(sc_in, 48)
            mm(bank[7][0:QH, 0:384], rel_sb, onehot, start=True, stop=True).then_inc(setup_pe, 1)
            pe.wait_ge(x_loaded, 16)
            for j in range(DT // 2):
                for k in (2 * j, 2 * j + 1):
                    for t in range(TT):
                        c = (k % 2) * S + t * P
                        last = transpose(bank[1 + j][:, c:c + P], x_in[:, t, k * P:(k + 1) * P])
                last.then_inc(setup_pe, 1)
            pe.wait_ge(p_loaded, 16)
            for l in range(DEPTH):
                for k in range(KP):
                    for t in range(TT):
                        c = k * S + t * P
                        last = transpose(bank[5 + l][:, c:c + P], p_in[:, l, t, k * P:(k + 1) * P])
                last.then_inc(setup_pe, 1)

            def mixer(l):
                for stage, i in STEPS:
                    if stage in ("hf", "hq", "aq", "hg", "ga", "gb"):
                        c = {"hf": K_HF, "hq": K_HQ, "aq": K_AQ, "hg": K_HG, "ga": K_GA, "gb": K_GB}[stage] + i // 2
                        await_chunk(pe, c, mixer_turns(l))
                        unit_product(UNIT_OF[stage] + i, l, columns(wview(c, DT, 256), (i % 2) * P, P), stream, DT,
                                     await_k=await_u(0, l) if stage == "hf" and i == 0 else None)
                    elif stage == "hi":
                        half, t = i // 2, i % 2
                        await_chunk(pe, K_HI + half, mixer_turns(l))
                        unit_product(U_HI + i, l, columns(stream, t * P, P), wview(K_HI + half, DT, 256), DT)
                    elif stage == "ak":
                        await_chunk(pe, K_AK, mixer_turns(l))
                        unit_product(U_AK, l, columns(wview(K_AK, DT, 256), 0, P), stream, DT)
                    elif stage == "av":
                        unit_product(U_AV + i, l, columns(stream, i * P, P), wview(K_AK, DT, 256), DT)
                    elif stage == "swap":
                        await_unit_read(pe, U_AK, l)
                        await_unit_free(pe, U_SW, l)
                        mm(ubank(U_SW)[0:HD, 0:S], ident[:, HD:P], aK[:, 0, :], start=True, stop=True)
                        mm(ubank(U_SW)[HD:P, 0:S], ident[:, 0:HD], aK[:, 0, :], start=True, stop=True).then_inc(unit_done, 1)
                    elif stage == "kt":
                        u = nth("kt", i)
                        pe.wait_ge(kdec_ready, l + 1)
                        await_aux_free(pe, u, l)
                        for t in range(TT):
                            last = transpose(xbank(u)[:, t * P:(t + 1) * P], hF[:, i, t * P:(t + 1) * P])
                        last.then_inc(aux_done, 1)
                    elif stage == "p":
                        u = nth("p", i)
                        pe.wait_ge(hgrn_ready, l + 1)
                        await_aux_free(pe, u, l)
                        for t in range(TT):
                            last = mm(xbank(u)[:, t * P:(t + 1) * P], hKi[:, i, t * P:(t + 1) * P],
                                      hQ[:, i, t * P:(t + 1) * P], start=True, stop=True)
                        last.then_inc(aux_done, 1)
                    elif stage == "kv":
                        h, t, half = i // 4, i // 2 % 2, i % 2
                        n = P * (3 if t == 1 and half == 1 else 4)
                        pe.wait_ge(vx_ready, 16 * l + i + 1)
                        await_aux_read(pe, nth("kt", h), l)
                        if i >= 2:
                            pe.wait_ge(state_ready, 16 * l + i - 1)
                        rhs = vx[:, i % 2].rearrange("p c n -> p (c n)")
                        mm(bank[6 + i % 2][:, 0:n], kend[:, t, h * P:(h + 1) * P], rhs[:, 0:n],
                           start=True, stop=True).then_inc(kv_done, 1)
                    elif stage == "sc":
                        u = nth("sc", i)
                        await_unit_read(pe, U_AQ + 3, l)
                        await_unit_read(pe, U_SW, l)
                        await_aux_free(pe, u, l)
                        r = slice((i % 2) * HD, (i % 2 + 1) * HD)
                        q, k = aQ[r, i // 2, :], aK[r, int(i % 2 != i // GROUP), :]
                        mm(xbank(u)[:, 0:P], q[:, 0:P], k[:, 0:P], start=True, stop=True)
                        mm(xbank(u)[:, P:P + S], q[:, P:S], k, start=True, stop=True).then_inc(aux_done, 1)
                    elif stage == "pt":
                        u = nth("pt", i)
                        pe.wait_ge(prob_ready, l + 1)
                        await_aux_free(pe, u, l)
                        for b in range(3):
                            last = transpose(xbank(u)[:, b * P:(b + 1) * P], sc[:, i, b * P:(b + 1) * P])
                        last.then_inc(aux_done, 1)
                    elif stage == "pv":
                        u = nth("pv", i)
                        await_aux_free(pe, u, l)
                        for h in (2 * i, 2 * i + 1):
                            await_aux_read(pe, nth("pt", h), l)
                            dst = xbank(u)[(h % 2) * HD:(h % 2 + 1) * HD, 0:S]
                            g = slice(h // GROUP * HD, (h // GROUP + 1) * HD)
                            mm(dst[:, 0:P], aV[:, 0, g], pT[:, h % 2, 0:P], start=True, stop=True)
                            mm(dst[:, P:S], aV[:, 0, g], pT[:, h % 2, P:2 * P], start=True, stop=False)
                            last = mm(dst[:, P:S], aV[:, 1, g], pT[:, h % 2, 2 * P:3 * P], start=False, stop=True)
                        last.then_inc(aux_done, 1)
                    elif stage == "o":
                        u = nth("o", i)
                        pe.wait_ge(pm_ready, 4 * l + i + 1)
                        pe.wait_ge(state_ready, 16 * l + 4 * i + 4)
                        await_aux_free(pe, u, l)
                        for t in range(TT):
                            mm(xbank(u)[:, t * P:(t + 1) * P], hV[:, t, i * P:(i + 1) * P], pm[:, i, t, :],
                               start=True, stop=False, skip_group_check=True)
                            for c in range(t * CPT + (t == 0), (t + 1) * CPT):
                                cols = slice(c * CHUNK, (c + 1) * CHUNK)
                                last = mm(xbank(u)[:, cols], state[:, i % 2, c - 1, :], hQ[:, i, cols],
                                          start=False, stop=True, skip_group_check=True)
                        last.then_inc(aux_done, 1)
                    elif stage == "osq":
                        u = nth("osq", i)
                        pe.wait_ge(osq_ready, 4 * l + 2 * i + 2)
                        await_aux_free(pe, u, l)
                        mm(xbank(u)[:], ones, hK[:, 2 * i:2 * i + 2, :].rearrange("p h s -> p (h s)"),
                           start=True, stop=True).then_inc(aux_done, 1)
                    elif stage in ("ya", "yb"):
                        c = (K_YA if stage == "ya" else K_YB) + i // 4
                        await_chunk(pe, c, mixer_turns(l))
                        pe.wait_ge(branch_ready, 2 * l + (1 if stage == "ya" else 2))
                        first = 0 if stage == "ya" else 4
                        unit_product(UNIT_OF[stage] + i, l, columns(wview(c, 4, 512), (i % 4) * P, P),
                                     [part[:, first:first + 4, :] for part in stream], 4)
                    elif stage == "wo":
                        c = K_WO + i // 2
                        await_chunk(pe, c, mixer_turns(l))
                        merged_k = lambda k: pe.wait_ge(merge_ready, 2 * l + 1 + k // 4) if k % 4 == 0 else None
                        unit_product(U_WO + i, l, columns(wview(c, DT, 256), (i % 2) * P, P), stream, DT,
                                     await_k=merged_k if i == 0 else None)

            def swiglu_all(order, n0, turns, pairs0, used, act_ready):
                last_pair = len(order) // 3 - 1
                for i, (m, j) in enumerate(order):
                    await_chunk(pe, n0 + i, turns)
                    if m == "w2":
                        pe.wait_ge(act_ready, pairs0 + j + 1)
                        w = wview(n0 + i, 2, D)
                        for d in range(DT):
                            last = product(bank[4 + d // 2][:, (d % 2) * S:(d % 2 + 1) * S], columns(w, d * P, P),
                                           [act_hi[:, j % 2], act_lo[:, j % 2]], 2, start=(j == 0 and d % 2 == 0),
                                           stop=(j == last_pair))
                    else:
                        if m == "w1" and j >= 2:
                            pe.wait_ge(act_ready, pairs0 + j - 1)
                        w = wview(n0 + i, DT, 2 * P)
                        for a in range(2):
                            last = product(bank[2 * (j % 2) + (m == "w3")][:, a * S:(a + 1) * S], columns(w, a * P, P), stream, DT)
                    last.then_inc(used, 1)

            def dense(l):
                pe.wait_ge(u_ready, 8)
                swiglu_all(DENSE, K_DENSE, 0, 0, d_used, d_act)

            def expert(e):
                def turn_act(j):
                    pe.wait_ge(m_mul, PE_ * e + j + 3)
                    for a in range(2):
                        last = transpose(bank[j % 2][:, a * P:(a + 1) * P], slot_act[:, j % 2, a * P:(a + 1) * P])
                    last.then_inc(act_turned, 1)

                pe.wait_ge(us_ready, e + 1)
                for i, (m, j) in enumerate(EXPERT):
                    n = K_EXPERTS + i
                    if m == "w2" and j == PE_ - 2:
                        turn_act(PE_ - 1)
                    await_chunk(pe, n, NX_E // SPLIT * e)
                    if m == "w2":
                        pe.wait_ge(m_act, PE_ * e + j + 3)
                        w = wview(n, 2, D)
                        for half in range(2):
                            last = product(bank[6 + half][:], [act_hi[:, j % 2, :, 0:P], act_lo[:, j % 2, :, 0:P]],
                                           columns(w, 512 * half, 512), 2, start=(j == 0), stop=(j == PE_ - 1))
                    else:
                        pe.wait_ge(m_act if m == "w1" else m_mul, PE_ * e + j + 1)
                        last = product(bank[j % 2 + 2 * (m == "w3")][:, 0:2 * P], [us_hi, us_lo], wview(n, DT, 2 * P), DT)
                    last.then_inc(m_used, 1)
                    if m == "w1" and j >= 1:
                        turn_act(j - 1)
                    if m == "w3" and j in (1, 2):
                        combine(e, j - 1)
                    if m == "w3" and j == 4:
                        pe.wait_ge(slots_ready, 2 * e + 2)
                        pe.wait_ge(h_ffn, 4 * e + 8)
                        for t in range(TT):
                            last = transpose(bank[4][:, t * P:(t + 1) * P], gate_slot[:, t, :])
                        last.then_inc(comb_tr, 1)
                    if m == "w3" and j == 7:
                        pe.wait_ge(comb_ready, e + 2)
                        pe.wait_ge(slots_ready, 2 * e + 3)
                        gather()

            def combine(e, part):
                if part == 0:
                    pe.wait_ge(y_act, e + 1)
                    pe.wait_ge(y_dve, e + 1)
                    pe.wait_ge(comb_ready, e + 1)
                for d in range(4 * part, 4 * part + 4):
                    if part == 1 and d % 2 == 0:
                        pe.wait_ge(h_ffn, 4 * e + 5 + (d - 4) // 2)
                    last = mm(bank[4 + d // 2 % 2][:, (d % 2) * S:(d % 2 + 1) * S], y_tok[:, d * P:(d + 1) * P], comb[:],
                              start=True, stop=True)
                    if d % 2:
                        last.then_inc(comb_done, 1)

            def gather():
                for d in range(DT):
                    for t in range(TT):
                        last = mm(bank[4 + d // 4][:, (d % 4) * CAP:(d % 4 + 1) * CAP], u_tok[:, t, d * P:(d + 1) * P],
                                  sel_slot[:, t, :], start=(t == 0), stop=(t == TT - 1))
                    if d % 4 == 3:
                        last.then_inc(gathered, 1)

            def moe():
                pe.wait_ge(u_ready, 20)
                for t in range(TT):
                    for k in range(DT):
                        mm(bank[4][:, t * NE:(t + 1) * NE], gB[:, k, t * P:(t + 1) * P], rw[:, k, :], start=(k == 0),
                           stop=(k == DT - 1))
                transpose(bank[0][:, 0:P], gB[:, 0, 0:P]).then_inc(r_pe, 1)
                for t in range(TT):
                    for half in range(2):
                        for j in range(4):
                            last = transpose(bank[2 * t + half][:, j * P:(j + 1) * P],
                                             gB[:, 4 * half + j, t * P:(t + 1) * P])
                        last.then_inc(r_pe, 1)
                pe.wait_ge(r_dve, 1)
                mm(bank[5][:, 0:8], before, picked[:, 0, :], start=True, stop=True)
                mm(bank[5][:, 8:16], ones, picked[:, 0, :], start=True, stop=False)
                mm(bank[5][:, 8:16], before, picked[:, 1, :], start=False, stop=True)
                mm(bank[5][:, 16:24], ones, picked[:, 0, :], start=True, stop=False)
                mm(bank[5][:, 16:24], ones, picked[:, 1, :], start=False, stop=True).then_inc(r_pe, 1)
                pe.wait_ge(r_act, 4)
                pe.wait_ge(route_ready, 1)
                fullest = pe.value_load(flag[0:1, 0:1], min_val=0, max_val=S)
                with pe.If(fullest <= CAP):
                    pe.wait_ge(slots_ready, 1)
                    gather()
                    with pe.Fori(0, NE) as e:
                        expert(e)
                    for part in range(2):
                        combine(NE, part)
                with pe.Else():
                    with pe.Fori(0, NE) as e:
                        pe.wait_ge(h_ffn, 4 * e + 4)
                        pe.wait_ge(slots_ready, e + 1)
                        for t in range(TT):
                            last = mm(bank[0][:, t * P:(t + 1) * P], gate_cols[:, t, :], ident, start=True, stop=True)
                        last.then_inc(gathered, 1)
                        pe.wait_ge(us_copied, e + 1)
                        swiglu_all(EXPERT, K_EXPERTS, NX_E // SPLIT * e, PE_ * e, m_used, m_act)

            with pe.Fori(0, DEPTH) as l:
                sum_of_squares(0, X_SSQ, l)
                mixer(l)
                sum_of_squares(1, X_FFN, l)
                with pe.If(l < 1):
                    dense(l)
                with pe.Else():
                    moe()
                    pe.drain()
                sum_of_squares(2, X_PLE, l)
                for i in range(DT):
                    c = K_EMBED + i // 2
                    await_chunk(pe, c, embed_turns(l))
                    unit_product(U_PG + i, l, columns(wview(c, DT, 256), (i % 2) * P, P), stream, DT,
                                 await_k=await_u(2, l) if i == 0 else None)
                for i in range(DT):
                    c = K_EMBED + 4 + i // 4
                    await_chunk(pe, c, embed_turns(l))
                    pe.wait_ge(p_split, l + 1)
                    unit_product(U_PP + i, l, columns(wview(c, KP, 512), (i % 4) * P, P), [p_hi, p_lo], KP)

            sum_of_squares(0, 0, DEPTH)
            for k in range(DT):
                pe.wait_ge(fin_ready, k + 1)
                for t in range(TT):
                    last = transpose(bank[4 + 2 * t + k // 4 if t == 0 else 6 + k // 4][:, (k % 4) * P:(k % 4 + 1) * P],
                                     gB[:, k, t * P:(t + 1) * P])
            last.then_inc(fin_tr, 1)

        @block.scalar
        def _(act):
            fn = nc.scalar.activation

            act.dma_start(consts_sb[:], consts).then_inc(consts_in, 16)
            act.dma_start(vec_rows[0:NVEC, :], vectors).then_inc(vec_in, 16)
            act.dma_start(x_in, x.rearrange("(t p) n -> p t n", p=P)).then_inc(x_loaded, 16)
            act.dma_start(onehot, buckets).then_inc(sc_in, 16)
            act.dma_start(rel_sb, rel_bias).then_inc(sc_in, 16)
            act.dma_start(mask_row, outside).then_inc(sc_in, 16)
            act.dma_start(p_in, p.rearrange("l (t p) n -> p l t n", p=P)).then_inc(p_loaded, 16)
            act.dma_start(sink[:].rearrange("p l h -> p (l h)"),
                          sinks.rearrange("l h -> (l h)").partition_broadcast(P)).then_inc(small_in, 16)
            act.dma_start(rw[:], router_w[0].rearrange("(k p) e -> p k e", p=P)).then_inc(small_in, 16)
            act.wait_ge(set_const, 1)
            act.wait_ge(setup_dve, 1)
            fn(lbt[:, 0:2, :], lbt[:, 0:2, :], ACT.Exp).then_inc(lb_exp, 1)

            def rms(src_bank, unit, l, norm, norm_sem_value):
                act.wait_ge(aux_done, NX * l + unit + 1)
                fn(rstd[:], src_bank[:, 0:S], ACT.Ln, scale=1.0 / D, bias=eps[:]).then_inc(aux_act, 1)
                act.drain()
                fn(rstd[:], rstd[:], ACT.Exp, scale=-0.5).then_inc(rms_ready, 1)

            def squares():
                for half in range(2):
                    fn(gA[:, 4 * half:4 * half + 4, :], hT[:, 4 * half:4 * half + 4, :], ACT.Square).then_inc(sq_ready, 1)

            def split_hi(n, turns, size=HALF):
                for half in range(2):
                    raw, hi, _ = half_views(n, half, size)
                    i = 2 * n + half
                    act.wait_ge(raw_loaded[i % RAW], 16 * (i // RAW + 1) + 16 * turns)
                    fn(hi, raw, ACT.Copy).then_inc(hi_done, 1)

            def u_parts(norm, l):
                for j in range(4):
                    act.wait_ge(u_normed, 12 * l + 4 * norm + j + 1)
                    fn(u_hi[:, 2 * j:2 * j + 2, :], gB[:, 2 * j:2 * j + 2, :], ACT.Copy).then_inc(u_hi_ready, 1)

            def unit_wait(u, l):
                act.wait_ge(unit_done, NU * l + u + 1)

            def aux_wait(u, l):
                act.wait_ge(aux_done, NX * l + u + 1)

            def mixer(l):
                for stage, i in STEPS:
                    stage_work(stage, i, l)
                    if stage in UNIT_OF and UNIT_OF[stage] + i in LAST_OF:
                        unit_wait(UNIT_OF[stage] + i, l)
                        split_hi(LAST_OF[UNIT_OF[stage] + i] + SPLIT, mixer_turns(l))

            def stage_work(stage, i, l):
                if True:
                    if stage == "hf":
                        unit_wait(U_HF + i, l)
                        fn(hF[:, i, :], ubank(U_HF + i)[:, 0:S], ACT.Sigmoid).then_inc(unit_act, 1)
                    elif stage == "gates":
                        act.wait_ge(f_ready, l + 1)
                        fn(hF[:], hF[:], ACT.Ln).then_inc(logf_ready, 1)
                    elif stage == "scan":
                        act.wait_ge(scan_ready, l + 1)
                        fn(hE[:], hA[:], ACT.Exp).then_inc(exp_ready, 1)
                        fn(hKi[:], hA[:], ACT.Exp, scale=-1.0).then_inc(exp_ready, 1)
                        act.wait_ge(diff_ready, l + 1)
                        fn(hF[:], hF[:], ACT.Exp).then_inc(exp_ready, 1)
                    elif stage == "aq":
                        unit_wait(U_AQ + i, l)
                        fn(aQ[:, i, :], ubank(U_AQ + i)[:, 0:S], ACT.Copy, scale=HD ** -0.5).then_inc(unit_act, 1)
                    elif stage == "kt":
                        u = nth("kt", i)
                        aux_wait(u, l)
                        fn(kend[:, :, i * P:(i + 1) * P], xbank(u)[:, 0:S].rearrange("p (t n) -> p t n", t=TT),
                           ACT.Copy).then_inc(aux_act, 1)
                    elif stage == "softmax":
                        act.wait_ge(max_ready, l + 1)
                        for b in range(2):
                            for h in range(QH):
                                s = sc[:, h, 0:P] if b == 0 else sc[:, h, P:P + S]
                                j = b * QH + h
                                fn(s, s, ACT.Exp, bias=smax[:, 1, j:j + 1], accum_out=smax[:, 2, j:j + 1])
                        fn(smax[:, 3, :], smax[:, 3, :], ACT.Exp).then_inc(exp_done, 1)
                    elif stage == "hg":
                        unit_wait(U_HG + i, l)
                        fn(hG[:, i, :], ubank(U_HG + i)[:, 0:S], ACT.Sigmoid).then_inc(gate_sig, 1)
                    elif stage in ("ga", "gb"):
                        u, dst = (U_GA + i, gA) if stage == "ga" else (U_GB + i, gB)
                        unit_wait(u, l)
                        fn(dst[:, i, :], ubank(u)[:, 0:S], ACT.Sigmoid).then_inc(unit_act, 1)
                    elif stage == "pt":
                        u = nth("pt", i)
                        aux_wait(u, l)
                        if i >= 2:
                            aux_wait(nth("pv", i // 2 - 1), l)
                        fn(pT[:, i % 2, :], xbank(u)[:, 0:384], ACT.Copy).then_inc(aux_act, 1)
                    elif stage == "o":
                        u = nth("o", i)
                        aux_wait(u, l)
                        fn(hK[:, i, :], xbank(u)[:, 0:S], ACT.Square).then_inc(osq_ready, 1)
                        fn(hO[:, i, :], xbank(u)[:, 0:S], ACT.Copy).then_inc(aux_act, 1)
                    elif stage == "osq":
                        u = nth("osq", i)
                        aux_wait(u, l)
                        r = hE[:, 2 * i:2 * i + 2, :].rearrange("p h s -> p (h s)")
                        fn(r, xbank(u)[:], ACT.Ln, scale=1.0 / P, bias=eps[:]).then_inc(aux_act, 1)
                        act.drain()
                        fn(r, r, ACT.Exp, scale=-0.5).then_inc(orms_ready, 1)

                    elif stage == "branch":
                        unit_wait(U_GB + 7, l)
                        if i == 0:
                            await_aux_read(act, nth("pv", 3), l)
                            fn(u_hi[:, 0:4, :], aO[:], ACT.Copy).then_inc(branch_hi, 1)
                        else:
                            act.wait_ge(yb_ready, l + 1)
                            fn(u_hi[:, 4:8, :], hO[:], ACT.Copy).then_inc(branch_hi, 1)
                    elif stage == "merge":
                        unit_wait((U_YA if i == 0 else U_YB) + 7, l)
                        act.wait_ge(merged, 8 * l + 4 * i + 4)
                        fn(u_hi[:, 4 * i:4 * i + 4, :], gA[:, 4 * i:4 * i + 4, :], ACT.Copy).then_inc(merge_hi, 1)

            def swiglu_all(order, n0, turns, pairs0, chunks0, used, silu_sem, mul_sem, hi_sem, act_ready):
                for i, (m, j) in enumerate(order):
                    act.wait_ge(used, chunks0 + i + 1)
                    if m == "w1":
                        if j >= 2:
                            act.wait_ge(act_ready, pairs0 + j - 1)
                        fn(act2[:, j % 2], bank[2 * (j % 2)][:].rearrange("p (a s) -> p a s", a=2), ACT.Silu).then_inc(silu_sem, 1)
                    split_hi(n0 + i + SPLIT, turns)
                    if m == "w3":
                        act.wait_ge(mul_sem, pairs0 + j + 1)
                        fn(act_hi[:, j % 2], act2[:, j % 2], ACT.Copy).then_inc(hi_sem, 1)

            def expert(e):
                def hi_of_turned(j):
                    act.wait_ge(act_turned, PE_ * e + j + 1)
                    fn(act_hi[:, j % 2, :, 0:P], bank[j % 2][:, 0:2 * P].rearrange("p (a s) -> p a s", a=2),
                       ACT.Copy).then_inc(m_hi, 1)

                for i, (m, j) in enumerate(EXPERT):
                    act.wait_ge(m_used, NX_E * e + i + 1)
                    if m == "w1":
                        fn(slot_act[:, j % 2], bank[j % 2][:, 0:2 * P], ACT.Silu).then_inc(m_silu, 1)
                    if m == "w3" and j == PE_ - 1:
                        act.wait_ge(us_copied, e + 2)
                        fn(us_hi[:], us[:], ACT.Copy).then_inc(us_hi_ready, 1)
                    if m == "w2" and j == PE_ - 1:
                        fn(y_tok[:, 0:512], bank[6][:], ACT.Copy).then_inc(y_act, 1)
                    split_hi(K_EXPERTS + i + SPLIT, NX_E // SPLIT * e)
                    if m == "w1" and j >= 1:
                        hi_of_turned(j - 1)
                    if m == "w3" and j == PE_ - 1:
                        hi_of_turned(j)

            def moe():
                for t in range(TT):
                    for half in range(2):
                        act.wait_ge(r_pe, 2 + 2 * t + half)
                        fn(u_tok[:, t, 512 * half:512 * half + 512], bank[2 * t + half][:], ACT.Copy).then_inc(r_act, 1)
                act.wait_ge(r_dve, 2)
                fn(ex, ex, ACT.Exp).then_inc(r_act, 1)
                act.wait_ge(route_ready, 1)
                fullest = act.value_load(flag[0:1, 0:1], min_val=0, max_val=S)
                with act.If(fullest <= CAP):
                    act.wait_ge(us_copied, 1)
                    fn(us_hi[:], us[:], ACT.Copy).then_inc(us_hi_ready, 1)
                    fn(y_tok[:, 0:512], consts_sb[:, 0:512], ACT.Copy, scale=0.0).then_inc(y_act, 1)
                    with act.Fori(0, NE) as e:
                        expert(e)
                with act.Else():
                    with act.Fori(0, NE) as e:
                        swiglu_all(EXPERT, K_EXPERTS, NX_E // SPLIT * e, PE_ * e, NX_E * e, m_used, m_silu, m_mul, m_hi, m_act)
                act.drain()

            with act.Fori(0, DEPTH) as l:
                act.wait_ge(h_ready, 8 * l + 8)
                squares()
                for c in range(SPLIT):
                    split_hi(c, mixer_turns(l))
                    if c == 0:
                        rms(xbank(X_SSQ), X_SSQ, l, 0, None)
                        u_parts(0, l)
                mixer(l)
                act.wait_ge(h_mix, 8 * l + 8)
                squares()
                rms(xbank(X_FFN), X_FFN, l, 1, None)
                u_parts(1, l)
                with act.If(l < 1):
                    swiglu_all(DENSE, K_DENSE, 0, 0, 0, d_used, d_silu, d_mul, d_hi, d_act)
                with act.Else():
                    moe()
                act.wait_ge(h_ffn, (4 * NE + 4) * l + 4)
                squares()
                rms(xbank(X_PLE), X_PLE, l, 2, None)
                u_parts(2, l)
                act.drain()
                fn(p_hi[:], p_T[:, bass.ds(l, 1)].rearrange("p a k s -> p (a k) s"), ACT.Copy).then_inc(p_hi_ready, 1)
                for i in range(DT):
                    unit_wait(U_PG + i, l)
                    fn(gA[:, i, :], ubank(U_PG + i)[:, 0:S], ACT.Sigmoid).then_inc(unit_act, 1)
                    c = LAST_OF.get(U_PG + i)
                    if c is not None and c + SPLIT < NM + NP:
                        split_hi(K_EMBED + c - NM + SPLIT, embed_turns(l), HALF if c - NM + SPLIT < 4 else HALF // 2)
            act.wait_ge(h_ready, 8 * DEPTH + 8)
            squares()
            rms(xbank(0), 0, DEPTH, 0, None)
            act.wait_ge(row_ready, 4)
            act.dma_start(out.rearrange("(t p) n -> p t n", p=P), out_rows).then_inc(out_done, 16)
            act.wait_ge(out_done, 16)

        @block.gpsimd
        def _(pool):
            pool.memset(eps[:], EPS).then_inc(set_const, 1)
            pool.memset(pm[:], 0.0).then_inc(set_const, 1)
            pool.wait_ge(bias_row_ready, 1)
            pool.dma_start(bias_rows_dram, bias_out.unsqueeze(1).to_broadcast([QH, P, 384])).then_inc(bias_rows_out, 16)
            pool.wait_ge(bias_rows_out, 16)
            both = bass.AP(tensor=bias_rows_dram.tensor, offset=P - 1, ap=[[383, P], [384 * P, QH], [1, 2 * P]])
            own = bass.AP(tensor=bias_rows_dram.tensor, offset=2 * P - 1, ap=[[383, P], [384 * P, QH], [1, P]])
            pool.dma_start(bias[:, :, P:3 * P], both).then_inc(bias_in, 16)
            pool.dma_start(bias[:, :, 0:P], own).then_inc(bias_in, 16)
            with pool.Fori(0, DEPTH) as l:
                pool.wait_ge(consts_in, 16)
                pool.wait_ge(setup_pe, 4 + DT // 2)
                pool.wait_ge(h_ready, 8 * l + 8)
                starts = scan_mask.unsqueeze(1).to_broadcast([P, HH * NCH, CHUNK])
                pool.tensor_tensor(chunk_starts.rearrange("p (c t) -> p c t", t=CHUNK), starts, starts,
                                   ALU.mult).then_inc(starts_ready, 1)
                await_unit_read(pool, U_HI + 3, l)
                for i in range(2 * HH * TT):
                    h, t, half = i // 4, i // 2 % 2, i % 2
                    if i >= 2:
                        pool.wait_ge(kv_done, 16 * l + i - 1)
                    v = hV[:, t, h * P:(h + 1) * P].unsqueeze(1).to_broadcast([P, 4, P])
                    m = chunk_mask[:, 4 * half:4 * half + 4].unsqueeze(2).to_broadcast([P, 4, P])
                    pool.tensor_tensor(vx[:, i % 2], v, m, ALU.mult).then_inc(vx_ready, 1)

        @block.vector
        def _(dve):
            v = nc.vector

            dve.wait_ge(setup_pe, 1)
            raw = bank[0]
            v.tensor_copy(params[:, :, 0:VROWS], raw[:, 0:R_LB].rearrange("p (l n) -> p l n", l=DEPTH))
            v.tensor_copy(fin_gain[:], raw[:, R_FIN:R_FIN + DT])
            v.tensor_copy(lbt[:, 0:2, :], raw[:, R_LB:R_FIN].rearrange("p (l n) -> p l n", l=DEPTH))
            dve.drain()
            v.tensor_tensor(lbt[:, 2, :], lbt[:, 0, :], lbt[:, 1, :], ALU.max)
            dve.drain()
            for l in range(DEPTH):
                last = v.tensor_tensor(lbt[:, l, :], lbt[:, l, :], lbt[:, 2, :], ALU.subtract)
            last.then_inc(setup_dve, 1)
            dve.wait_ge(setup_pe, 2)
            dve.wait_ge(sc_in, 48)
            v.tensor_tensor(bias_out, bank[7][0:QH, 0:384], mask_row, ALU.add).then_inc(bias_row_ready, 1)
            for j in range(DT // 2):
                dve.wait_ge(setup_pe, 3 + j)
                v.tensor_copy(hT[:, 2 * j:2 * j + 2, :], bank[1 + j][:].rearrange("p (k s) -> p k s", k=2)).then_inc(h_ready, 2)
            for l in range(DEPTH):
                dve.wait_ge(setup_pe, 3 + DT // 2 + l)
                v.tensor_copy(p_T[:, l], bank[5 + l][:].rearrange("p (k s) -> p k s", k=KP))
            dve.wait_ge(lb_exp, 1)
            v.tensor_tensor(lbt[:, 2, :], lbt[:, 0, :], lbt[:, 1, :], ALU.add)
            dve.drain()
            v.reciprocal(lbt[:, 2, :], lbt[:, 2, :])
            dve.drain()
            for l in range(DEPTH):
                v.tensor_tensor(lbt[:, l, :], lbt[:, l, :], lbt[:, 2, :], ALU.mult)
            dve.drain()
            v.tensor_tensor(lbt[:, 2, :], lbt[:, 0, :], lbt[:, 1, :], ALU.add)
            v.tensor_tensor(params[:, 0, LB:LB + HH], lbt[:, 0, :], lbt[:, 0, :], ALU.subtract)
            dve.drain()
            v.tensor_tensor(params[:, 1, LB:LB + HH], lbt[:, 2, :], lbt[:, 0, :], ALU.subtract)
            dve.drain()
            v.tensor_scalar(params[:, :, OMLB:OMLB + HH], params[:, :, LB:LB + HH], -1.0, 1.0, ALU.mult, ALU.add)
            dve.drain()
            dve.wait_ge(small_in, 32)
            dve.wait_ge(set_const, 2)
            dve.wait_ge(bias_in, 32)

            def norm_tile(k, gains):
                return v.scalar_tensor_tensor(gB[:, k, :], hT[:, k, :], gains[:, k:k + 1], rstd[:], ALU.mult, ALU.mult)

            def normed(norm, l, gains):
                def lo(j):
                    dve.wait_ge(u_hi_ready, 12 * l + 4 * norm + j + 1)
                    two = slice(2 * j, 2 * j + 2)
                    v.tensor_tensor(u_lo[:, two, :], gB[:, two, :], u_hi[:, two, :].bitcast(F32),
                                    ALU.subtract).then_inc(u_ready, 1)

                dve.wait_ge(rms_ready, 3 * l + norm + 1)
                for j in range(4):
                    norm_tile(2 * j, gains)
                    norm_tile(2 * j + 1, gains).then_inc(u_normed, 1)
                    if j:
                        lo(j - 1)
                lo(3)

            def split_lo(n, turns, size=HALF):
                for half in range(2):
                    raw, hi, lo = half_views(n, half, size)
                    dve.wait_ge(hi_done, 2 * n + half + 1 + RAW * turns)
                    v.tensor_tensor(lo, raw, hi.bitcast(F32), ALU.subtract).then_inc(lo_done, 1)

            def unit_wait(u, l):
                dve.wait_ge(unit_done, NU * l + u + 1)

            def aux_wait(u, l):
                dve.wait_ge(aux_done, NX * l + u + 1)

            def mixer(l):
                for stage, i in STEPS:
                    stage_work(stage, i, l)
                    if stage in UNIT_OF and UNIT_OF[stage] + i in LAST_OF:
                        split_lo(LAST_OF[UNIT_OF[stage] + i] + SPLIT, mixer_turns(l))
                dve.drain()
                v.tensor_copy(smax[:, 5, 0:1], smax[:, 1, 0:1]).then_inc(h_mix, 8)

            def stage_work(stage, i, l):
                if True:
                    if stage == "hq":
                        unit_wait(U_HQ + i, l)
                        v.tensor_copy(hQ[:, i, :], ubank(U_HQ + i)[:, 0:S]).then_inc(unit_dve, 1)
                    elif stage == "gates":
                        await_unit_read(dve, U_HF + 3, l)
                        for h in range(HH):
                            v.tensor_scalar(hF[:, h, :], hF[:, h, :], gain[:, OMLB + h:OMLB + h + 1],
                                            gain[:, LB + h:LB + h + 1], ALU.mult, ALU.add)
                        dve.drain()
                        v.tensor_scalar(hK[:], hF[:], -1.0, 1.0, ALU.mult, ALU.add).then_inc(f_ready, 1)
                    elif stage == "hi":
                        unit_wait(U_HI + i, l)
                        half, t = i // 2, i % 2
                        v.tensor_copy(hV[:, t, half * 256:half * 256 + 256], ubank(U_HI + i)[:, 0:S]).then_inc(unit_dve, 1)
                    elif stage == "scan":
                        dve.wait_ge(logf_ready, l + 1)
                        dve.wait_ge(starts_ready, l + 1)
                        v.tensor_tensor_scan(hA[:].rearrange("p h s -> p (h s)"), chunk_starts,
                                             hF[:].rearrange("p h s -> p (h s)"), 0.0, ALU.mult, ALU.add).then_inc(scan_ready, 1)
                        dve.drain()
                        a = hA[:].rearrange("p h (c t) -> p (h c) t", t=CHUNK)
                        v.tensor_tensor(hF[:].rearrange("p h (c t) -> p (h c) t", t=CHUNK),
                                        a[:, :, CHUNK - 1:CHUNK].to_broadcast([P, HH * NCH, CHUNK]), a,
                                        ALU.subtract).then_inc(diff_ready, 1)
                    elif stage == "decay":
                        dve.wait_ge(exp_ready, 3 * l + 3)
                        v.tensor_tensor(hF[:], hF[:], hK[:], ALU.mult).then_inc(kdec_ready, 1)
                        v.tensor_tensor(hKi[:], hKi[:], hK[:], ALU.mult)
                        v.tensor_copy(dec[:], hE[:].rearrange("p h (c t) -> p (h c) t", t=CHUNK)[:, :, CHUNK - 1])
                        v.tensor_tensor(hQ[:], hQ[:], hE[:], ALU.mult).then_inc(hgrn_ready, 1)
                    elif stage in ("ak", "swap"):
                        n = UNIT_OF[stage]
                        unit_wait(n, l)
                        v.tensor_copy(aK[:, int(stage == "swap"), :], ubank(n)[:, 0:S]).then_inc(unit_dve, 1)
                    elif stage == "av":
                        unit_wait(U_AV + i, l)
                        v.tensor_copy(aV[:, i, :], ubank(U_AV + i)[:, P:2 * P]).then_inc(unit_dve, 1)
                    elif stage == "p":
                        u = nth("p", i)
                        dve.drain()
                        aux_wait(u, l)
                        v.tensor_copy(rstd[:], xbank(u)[:, 0:S]).then_inc(aux_dve, 1)
                        dve.drain()
                        v.copy_predicated(pm[:, i], hg_mask.bitcast(U32).unsqueeze(1).to_broadcast([P, TT, P]),
                                          rstd[:].rearrange("p (t n) -> p t n", t=TT)).then_inc(pm_ready, 1)
                    elif stage == "kv":
                        h, t, half = i // 4, i // 2 % 2, i % 2
                        dve.drain()
                        dve.wait_ge(kv_done, 16 * l + i + 1)
                        if i % 4 == 0 and h >= 2:
                            aux_wait(nth("o", h - 2), l)
                        for j in range(4):
                            c = t * CPT + half * 4 + j
                            if c == NCH - 1:
                                continue
                            src = bank[6 + i % 2][:, j * P:(j + 1) * P]
                            if c == 0:
                                last = v.tensor_copy(state[:, h % 2, 0, :], src)
                            else:
                                if j:
                                    dve.drain()
                                last = v.scalar_tensor_tensor(
                                    state[:, h % 2, c, :], state[:, h % 2, c - 1, :],
                                    dec[:, h * NCH + c:h * NCH + c + 1], src, ALU.mult, ALU.add)
                        last.then_inc(state_ready, 1)
                    elif stage == "sc":
                        u = nth("sc", i)
                        aux_wait(u, l)
                        v.tensor_tensor(sc[:, i, :], xbank(u)[:, 0:384], bias[:, i, :], ALU.add).then_inc(aux_dve, 1)
                    elif stage == "softmax":
                        dve.drain()
                        v.tensor_reduce(smax[:, 0, 0:QH], sc[:, :, 0:P], AX.X, ALU.max)
                        v.tensor_reduce(smax[:, 0, QH:2 * QH], sc[:, :, P:P + S], AX.X, ALU.max)
                        dve.drain()
                        own_sink = sink[:, bass.ds(l, 1), :].to_broadcast([P, 2, QH])
                        top = smax[:, 0, :].rearrange("p (b h) -> p b h", b=2)
                        v.tensor_tensor(top, top, own_sink, ALU.max)
                        dve.drain()
                        v.tensor_scalar(smax[:, 1, :], smax[:, 0, :], -1.0, None, ALU.mult)
                        v.tensor_tensor(smax[:, 3, :].rearrange("p (b h) -> p b h", b=2), own_sink, top, ALU.subtract)
                        dve.drain()
                        v.tensor_copy(smax[:, 5, :], smax[:, 1, :]).then_inc(max_ready, 1)
                        dve.wait_ge(exp_done, l + 1)
                        v.tensor_tensor(smax[:, 4, :], smax[:, 2, :], smax[:, 3, :], ALU.add)
                        dve.drain()
                        v.reciprocal(smax[:, 4, :], smax[:, 4, :])
                        dve.drain()
                        v.tensor_tensor(sc[:, :, 0:P], sc[:, :, 0:P],
                                        smax[:, 4, 0:QH].unsqueeze(2).to_broadcast([P, QH, P]), ALU.mult)
                        v.tensor_tensor(sc[:, :, P:P + S], sc[:, :, P:P + S],
                                        smax[:, 4, QH:2 * QH].unsqueeze(2).to_broadcast([P, QH, S]),
                                        ALU.mult).then_inc(prob_ready, 1)
                    elif stage == "hg":
                        dve.wait_ge(gate_sig, 4 * l + i + 1)
                        v.tensor_tensor(hG[:, i, :], hG[:, i, :], ubank(U_HG + i)[:, 0:S], ALU.mult).then_inc(unit_dve, 1)
                    elif stage == "pv":
                        u = nth("pv", i)
                        aux_wait(u, l)
                        v.tensor_copy(aO[:, i, :], xbank(u)[:, 0:S]).then_inc(aux_dve, 1)
                    elif stage == "ynorm":
                        dve.wait_ge(orms_ready, 2 * l + 2)
                        v.tensor_tensor(hO[:], hO[:], hE[:], ALU.mult)
                        dve.drain()
                        v.scalar_tensor_tensor(hO[:], hO[:], gain[:, G_HN:G_HN + 1], hG[:], ALU.mult,
                                               ALU.mult).then_inc(yb_ready, 1)
                    elif stage == "ya":
                        await_unit_read(dve, U_GA + i, l)
                        unit_wait(U_YA + i, l)
                        v.tensor_tensor(gA[:, i, :], gA[:, i, :], ubank(U_YA + i)[:, 0:S], ALU.mult).then_inc(unit_dve, 1)
                    elif stage == "yb":
                        await_unit_read(dve, U_GB + i, l)
                        unit_wait(U_YB + i, l)
                        v.tensor_tensor(gB[:, i, :], gB[:, i, :], ubank(U_YB + i)[:, 0:S], ALU.mult).then_inc(unit_dve, 1)
                        dve.drain()
                        v.tensor_tensor(gA[:, i, :], gA[:, i, :], gB[:, i, :], ALU.add).then_inc(merged, 1)
                    elif stage == "branch":
                        dve.wait_ge(branch_hi, 2 * l + i + 1)
                        part = slice(4 * i, 4 * i + 4)
                        v.tensor_tensor(u_lo[:, part, :], (aO if i == 0 else hO)[:], u_hi[:, part, :].bitcast(F32),
                                        ALU.subtract).then_inc(branch_ready, 1)
                    elif stage == "merge":
                        dve.wait_ge(merge_hi, 2 * l + i + 1)
                        part = slice(4 * i, 4 * i + 4)
                        v.tensor_tensor(u_lo[:, part, :], gA[:, part, :], u_hi[:, part, :].bitcast(F32),
                                        ALU.subtract).then_inc(merge_ready, 1)
                    elif stage == "wo":
                        unit_wait(U_WO + i, l)
                        v.tensor_tensor(hT[:, i, :], hT[:, i, :], ubank(U_WO + i)[:, 0:S], ALU.add).then_inc(unit_dve, 1)

            def swiglu_all(order, n0, turns, pairs0, chunks0, used, silu_sem, mul_sem, hi_sem, act_ready, by_gate):
                for i, (m, j) in enumerate(order):
                    if m == "w3":
                        dve.wait_ge(used, chunks0 + i + 1)
                        dve.wait_ge(silu_sem, pairs0 + j + 1)
                        w3u = bank[2 * (j % 2) + 1][:].rearrange("p (a s) -> p a s", a=2)
                        last = v.tensor_tensor(act2[:, j % 2], act2[:, j % 2], w3u, ALU.mult)
                        if by_gate:
                            dve.drain()
                            last = v.tensor_tensor(act2[:, j % 2], act2[:, j % 2],
                                                   gate_row[:].unsqueeze(1).to_broadcast([P, 2, S]), ALU.mult)
                        last.then_inc(mul_sem, 1)
                    split_lo(n0 + i + SPLIT, turns)
                    if m == "w3":
                        dve.wait_ge(hi_sem, pairs0 + j + 1)
                        v.tensor_tensor(act_lo[:, j % 2], act2[:, j % 2], act_hi[:, j % 2].bitcast(F32),
                                        ALU.subtract).then_inc(act_ready, 1)

            def gate_slots(e):
                for t in range(TT):
                    last = v.tensor_scalar(gate_slot[:, t, :], slot_iota, pos[:, t, bass.ds(e, 1)],
                                           gate[:, t, bass.ds(e, 1)], ALU.is_equal, ALU.mult)
                last.then_inc(slots_ready, 1)

            def sel_slots(at):
                for t in range(TT):
                    last = v.tensor_scalar(sel_slot[:, t, :], slot_iota, pos_wide[:, t, at], picked_wide[:, t, at],
                                           ALU.is_equal, ALU.mult)
                last.then_inc(slots_ready, 1)

            def copy_slots(n):
                for half in range(2):
                    dve.wait_ge(gathered, 2 * n + half + 1)
                    last = v.tensor_copy(us[:, 4 * half:4 * half + 4, :], bank[4 + half][:].rearrange("p (d n) -> p d n", d=4))
                last.then_inc(us_copied, 1)

            def slots_lo(n):
                dve.wait_ge(us_hi_ready, n + 1)
                v.tensor_tensor(us_lo[:], us[:], us_hi[:].bitcast(F32), ALU.subtract).then_inc(us_ready, 1)

            def combined(e, part):
                for j in (2 * part, 2 * part + 1):
                    dve.wait_ge(comb_done, 4 * e + j + 1)
                    v.tensor_tensor(hT[:, 2 * j:2 * j + 2, :], hT[:, 2 * j:2 * j + 2, :],
                                    bank[4 + j % 2][:].rearrange("p (k s) -> p k s", k=2), ALU.add).then_inc(h_ffn, 1)

            def expert(e):
                def lo_of_turned(j):
                    dve.wait_ge(m_hi, PE_ * e + j + 1)
                    v.tensor_tensor(act_lo[:, j % 2, :, 0:P], bank[j % 2][:, 0:2 * P].rearrange("p (a s) -> p a s", a=2),
                                    act_hi[:, j % 2, :, 0:P].bitcast(F32), ALU.subtract).then_inc(m_act, 1)

                for i, (m, j) in enumerate(EXPERT):
                    if m == "w3":
                        dve.wait_ge(m_used, NX_E * e + i + 1)
                        dve.wait_ge(m_silu, PE_ * e + j + 1)
                        v.tensor_tensor(slot_act[:, j % 2], slot_act[:, j % 2], bank[2 + j % 2][:, 0:2 * P],
                                        ALU.mult).then_inc(m_mul, 1)
                    if m == "w3" and j == PE_ - 1:
                        slots_lo(e + 1)
                    if m == "w2" and j == PE_ - 1:
                        dve.wait_ge(m_used, NX_E * e + i + 1)
                        v.tensor_copy(y_tok[:, 512:1024], bank[7][:]).then_inc(y_dve, 1)
                    split_lo(K_EXPERTS + i + SPLIT, NX_E // SPLIT * e)
                    if m == "w1" and j in (2, 3):
                        combined(e, j - 2)
                    if m == "w1" and j == 4:
                        gate_slots(e)
                    if m == "w1" and j == 5:
                        dve.wait_ge(comb_tr, e + 1)
                        v.tensor_copy(comb[:], bank[4][:, 0:S]).then_inc(comb_ready, 1)
                    if m == "w1" and j == 6:
                        sel_slots(bass.ds(e + 1, 1))
                    if m == "w1" and j == 8:
                        copy_slots(e + 1)
                    if m == "w1" and j >= 1:
                        lo_of_turned(j - 1)
                    if m == "w3" and j == PE_ - 1:
                        lo_of_turned(j)

            def add_to_h(j):
                v.tensor_tensor(hT[:, 2 * j:2 * j + 2, :], hT[:, 2 * j:2 * j + 2, :],
                                bank[4 + j][:].rearrange("p (k s) -> p k s", k=2), ALU.add).then_inc(h_ffn, 1)

            def moe():
                v.memset(rt[:], 0.0)
                dve.drain()
                dve.wait_ge(r_pe, 1)
                v.tensor_copy(logit, bank[4][:, 0:TT * NE].rearrange("p (t e) -> p t e", t=TT))
                dve.drain()
                for t in range(TT):
                    v.max(top8[:, t, :], logit[:, t, :])
                dve.drain()
                for t in range(TT):
                    v.max_index(idx8[:, t, :], top8[:, t, :], logit[:, t, :])
                dve.drain()
                v.tensor_copy(idxf, idx8[:])
                dve.drain()
                for t in range(TT):
                    v.tensor_scalar(tmp8[:, t, :], expert_iota, idxf[:, t, 0:1], None, ALU.is_equal)
                    v.tensor_scalar(picked[:, t, :], expert_iota, idxf[:, t, 1:2], None, ALU.is_equal)
                    v.tensor_scalar(ex[:, t, :], logit[:, t, :], top8[:, t, 0:1], None, ALU.subtract)
                dve.drain()
                v.tensor_tensor(picked, picked, tmp8, ALU.add).then_inc(r_dve, 1)
                dve.drain()
                v.tensor_tensor(ex, ex, picked, ALU.mult).then_inc(r_dve, 1)
                dve.wait_ge(r_act, 5)
                v.tensor_tensor(gate, ex, picked, ALU.mult)
                dve.drain()
                v.tensor_reduce(den[:], gate, AX.X, ALU.add)
                dve.drain()
                v.reciprocal(den[:], den[:])
                dve.drain()
                for t in range(TT):
                    v.tensor_scalar(gate[:, t, :], gate[:, t, :], den[:, t:t + 1], None, ALU.mult)
                dve.wait_ge(r_pe, 6)
                v.tensor_copy(pos, bank[5][:, 0:16].rearrange("p (t e) -> p t e", t=TT))
                v.tensor_copy(cnt[:], bank[5][:, 16:24])
                dve.drain()
                v.tensor_reduce(flag[:], cnt[:], AX.X, ALU.max).then_inc(route_ready, 1)
                dve.wait_ge(route_ready, 1)
                fullest = dve.value_load(flag[0:1, 0:1], min_val=0, max_val=S)
                with dve.If(fullest <= CAP):
                    v.memset(y_tok[:, 512:1024], 0.0).then_inc(y_dve, 1)
                    v.memset(comb[:], 0.0).then_inc(comb_ready, 1)
                    v.memset(slot_act[:, 0], 0.0).then_inc(m_mul, 2)
                    v.memset(slot_act[:, 1], 0.0).then_inc(m_act, 2)
                    sel_slots(slice(0, 1))
                    copy_slots(0)
                    slots_lo(0)
                    with dve.Fori(0, NE) as e:
                        expert(e)
                    for part in range(2):
                        combined(NE, part)
                with dve.Else():
                    with dve.Fori(0, NE) as e:
                        for t in range(TT):
                            last = v.tensor_scalar(gate_cols[:, t, :], ones, gate[:, t, bass.ds(e, 1)], None, ALU.mult)
                        last.then_inc(slots_ready, 1)
                        dve.wait_ge(gathered, e + 1)
                        v.tensor_copy(gate_row[:], bank[0][:, 0:S]).then_inc(us_copied, 1)
                        dve.drain()
                        swiglu_all(EXPERT, K_EXPERTS, NX_E // SPLIT * e, PE_ * e, NX_E * e, m_used, m_silu, m_mul, m_hi,
                                   m_act, True)
                        dve.wait_ge(m_used, NX_E * e + NX_E)
                        for j in range(4):
                            add_to_h(j)
                        dve.drain()
                    v.memset(y_tok[:, 0:1], 0.0).then_inc(h_ffn, 4)
                dve.drain()

            with dve.Fori(0, DEPTH) as l:
                v.tensor_copy(gain[:], params[:, bass.ds(l, 1), :].rearrange("p a n -> p (a n)"))
                dve.drain()
                split_lo(0, mixer_turns(l))
                normed(0, l, gain[:, G_MIX:G_MIX + DT])
                for c in range(1, SPLIT):
                    split_lo(c, mixer_turns(l))
                mixer(l)
                normed(1, l, gain[:, G_FFN:G_FFN + DT])
                with dve.If(l < 1):
                    swiglu_all(DENSE, K_DENSE, 0, 0, 0, d_used, d_silu, d_mul, d_hi, d_act, False)
                    dve.wait_ge(d_used, ND)
                    for j in range(4):
                        add_to_h(j)
                with dve.Else():
                    moe()
                normed(2, l, gain[:, G_PLE:G_PLE + DT])
                dve.wait_ge(p_hi_ready, l + 1)
                v.tensor_tensor(p_lo[:], p_T[:, bass.ds(l, 1)].rearrange("p a k s -> p (a k) s"), p_hi[:].bitcast(F32),
                                ALU.subtract).then_inc(p_split, 1)
                for c in range(SPLIT, NP):
                    split_lo(K_EMBED + c, embed_turns(l), HALF if c < 4 else HALF // 2)
                for i in range(DT):
                    await_unit_read(dve, U_PG + i, l)
                    unit_wait(U_PP + i, l)
                    v.tensor_tensor(gA[:, i, :], gA[:, i, :], ubank(U_PP + i)[:, 0:S], ALU.mult).then_inc(unit_dve, 1)
                    dve.drain()
                    v.tensor_tensor(hT[:, i, :], hT[:, i, :], gA[:, i, :], ALU.add).then_inc(h_ready, 1)
                dve.drain()
            dve.wait_ge(rms_ready, 3 * DEPTH + 1)
            for k in range(DT):
                norm_tile(k, fin_gain[:]).then_inc(fin_ready, 1)
            dve.wait_ge(fin_tr, 1)
            for t in range(TT):
                for half in range(2):
                    b = bank[4 + half] if t == 0 else bank[6 + half]
                    v.tensor_copy(out_rows[:, t, 512 * half:512 * half + 512], b[:]).then_inc(row_ready, 1)


def constants():
    c = np.zeros((P, C_N), np.float32)
    i = np.arange(P)
    c[:, C_ID:C_ID + P] = np.eye(P)
    c[:, C_ONE:C_ONE + P] = 1
    c[:, C_LT:C_LT + P] = i[:, None] < i[None, :]
    c[:, C_HM:C_HM + P] = (i[:, None] // CHUNK == i[None, :] // CHUNK) & (i[:, None] <= i[None, :])
    c[:, C_CM:C_CM + CPT] = i[:, None] // CHUNK == np.arange(CPT)
    c[:, C_IO:C_IO + CAP] = np.arange(CAP)
    c[:, C_SC:C_SC + CHUNK] = np.arange(CHUNK) != 0
    c[:, C_I8:C_I8 + NE] = np.arange(NE)
    return c


def bias_tables():
    dist = 2 * P - 1 - np.arange(384)
    exact = BUCKETS // 2
    d = np.maximum(dist, 0)
    large = exact + (np.log(np.maximum(d, 1).astype(np.float32) / np.float32(exact)) / np.float32(np.log(MAX_DIST / exact))
                     * np.float32(BUCKETS - exact)).astype(np.int32)
    bucket = np.where(d < exact, d, np.minimum(large, BUCKETS - 1))
    inside = (dist >= 0) & (dist < P)
    onehot = ((np.arange(BUCKETS)[:, None] == bucket) & inside).astype(np.float32)
    outside = np.broadcast_to(np.where(inside, 0, NEG).astype(np.float32), (QH, 384))
    return onehot, np.ascontiguousarray(outside)


def kernel(**inputs):
    import concourse.bacc as bacc
    from concourse.bass_utils import run_bass_kernel_spmd

    a = {k: np.asarray(v) for k, v in inputs.items()}
    rows = []
    for l in range(DEPTH):
        for n in ("norm_mix", "norm_ffn", "norm_ple", "hgrn_norm"):
            rows.append(a[n][l].reshape(-1, P))
    rows += [a["lb_logits"].reshape(-1, P), a["final_norm"].reshape(-1, P)]
    onehot, outside = bias_tables()
    arrays = {
        "x": a["x"][0], "p": a["p"][:, 0], "w_in": a["w_in"], "sinks": a["sinks"], "rel_bias": a["rel_bias"],
        "vectors": np.concatenate(rows), "w_branch_a": a["w_branch_a"], "w_branch_b": a["w_branch_b"],
        "w_out": a["w_out"], "dense_w1": a["dense_w1"], "dense_w3": a["dense_w3"], "dense_w2": a["dense_w2"],
        "router_w": a["router_w"], "moe_w1": a["moe_w1"], "moe_w3": a["moe_w3"], "moe_w2": a["moe_w2"],
        "ple_proj": a["ple_proj"], "ple_gate": a["ple_gate"], "consts": constants(), "buckets": onehot,
        "outside": outside,
    }
    nc = bacc.Bacc("TRN2", target_bir_lowering=False, num_devices=1)
    handles = {n: nc.dram_tensor(n, v.shape, F32, kind="ExternalInput").ap() for n, v in arrays.items()}
    out = nc.dram_tensor("out", (S, D), F32, kind="ExternalOutput").ap()
    trunk(nc, *handles.values(), out)
    r = run_bass_kernel_spmd(nc, [{n: np.ascontiguousarray(v) for n, v in arrays.items()}], core_ids=[0])
    return r.results[0]["out"].reshape(1, S, D)
```

```python
from contextlib import ExitStack

import numpy as np

import concourse.bass as bass
from concourse import mybir

F32 = mybir.dt.float32
F32R = mybir.dt.float32r
I32 = mybir.dt.int32
U32 = mybir.dt.uint32
ALU = mybir.AluOpType
ACT = mybir.ActivationFunctionType
AX = mybir.AxisListType

P = 128
D = 1024
DT = D // P
S = 256
TT = S // P
DEPTH = 2
QH, KVH, HD = 8, 2, 64
GROUP = QH // KVH
BUCKETS = 32
MAX_DIST = 128
HH = 4
CHUNK = 16
NCH = S // CHUNK
LEVELS = 3
FD = 2816
FE = 3584
NE = 8
PLE = 256
KP = PLE // P
EPS = 1e-6
O_AQ, O_AK, O_AV, O_HQ, O_HF, O_HI, O_HG, O_GA, O_GB = 0, 512, 640, 768, 1280, 1792, 2304, 2816, 3840
CAP = 128
NEG = -1e30

CHUNK_N = 2048
HALF = CHUNK_N // 2
RAW = 6
SPLIT = 3

G_MIX, G_FFN, G_PLE, G_HN, LB, OMLB = 0, 8, 16, 24, 25, 29
PCOLS = 33
VROWS = 25
R_LB = DEPTH * VROWS
R_FIN = R_LB + DEPTH * HH
NVEC = R_FIN + DT

C_ID, C_ONE, C_LT, C_HM, C_PM, C_IO, C_SC, C_I8 = 0, 128, 256, 384, 512, 896, 1024, 1040
C_N = 1048

U_HF, U_HQ, U_HI, U_AQ, U_AK, U_AV, U_SW, U_HG, U_GA, U_GB, U_YA, U_YB, U_WO, U_PP, U_PG = (
    0, 4, 8, 12, 16, 17, 18, 20, 24, 32, 40, 48, 56, 64, 72)
UNITS = "A" * 4 + "D" * 8 + "A" * 4 + "ADAD" + "A" * 4 + "A" * 16 + "D" * 24 + "A" * 8 + "A" * 8
NU = len(UNITS)
UA, UD = UNITS.count("A"), UNITS.count("D")

X_SSQ = 0
X_ORDER = (["ssq"] + ["sc"] * 8 + ["p"] * 8 + ["kt", "st"] + ["o", "pt", "pt", "pv"] * 4 + ["osq"] * 2 + ["ssq"] * 2)
X_DRAIN = "".join("D" if k in ("p", "sc", "pv") else "A" for k in X_ORDER)
NX = len(X_ORDER)
XA, XD = X_DRAIN.count("A"), X_DRAIN.count("D")
X_FFN, X_PLE = NX - 2, NX - 1
RING, X_RING = 3, 5
N_KEEP = 14
POOLED = 6
X_BANKS, P_BANKS = (1, 2, 4, 5), (6, 7)


def nth(kind, n):
    return [i for i, k in enumerate(X_ORDER) if k == kind][n]


def mixer_steps():
    s = [("hf", h) for h in range(4)] + [("hq", h) for h in range(4)] + [("gates", 0)]
    s += [("hi", i) for i in range(4)] + [("scan", 0)] + [("aq", i) for i in range(4)] + [("decay", 0)]
    s += [("ak", 0), ("av", 0), ("swap", 0), ("av", 2)]
    s += [("sc", h) for h in range(4)] + [("levels", 0)] + [("sc", h) for h in range(4, 8)] + [("softmax", 0)] + [("p", i) for i in range(4)]
    s += [("hg", 0), ("p", 4), ("p", 5), ("hg", 1), ("probs", 0), ("p", 6), ("p", 7), ("hg", 2), ("kt", 0), ("hg", 3)]
    s += [("ga", 0), ("st", 0), ("ga", 1)]
    for i in range(4):
        s += [("o", i), ("ga", 2 * i + 2) if i < 3 else ("gb", 0), ("pt", 2 * i), ("pt", 2 * i + 1), ("pv", i)]
        s += [("ga", 2 * i + 3) if i < 3 else ("gb", 1)]
    s += [("osq", 0), ("gb", 2), ("osq", 1), ("gb", 3), ("branch", 0), ("gb", 4), ("ynorm", 0), ("gb", 5), ("gb", 6)]
    s += [("branch", 1), ("gb", 7)] + [("ya", d) for d in range(DT)]
    for d in range(DT):
        s += [("yb", d)] + [("merge", d // 2)] * (d % 2)
    for d in range(DT + 2):
        s += [("wo", d)] * (d < DT) + [("ssq", d - 2)] * (d >= 2)
    return s


STEPS = mixer_steps()


def ffn_order(pairs):
    out = []
    for j in range(pairs + 2):
        out += [("w1", j)] * (j < pairs) + [("w2", j - 2)] * (j >= 2) + [("w3", j)] * (j < pairs)
    return out


DENSE, EXPERT = ffn_order(FD // P // 2), ffn_order(FE // P // 2)
PAIRS = FE // P // 2

MIXER = []
for first_col, unit, n in ((O_HF, U_HF, 2), (O_HQ, U_HQ, 2), (O_HI, U_HI, 2), (O_AQ, U_AQ, 2), (O_AK, U_SW, 1),
                           (O_HG, U_HG, 2), (O_GA, U_GA, 4), (O_GB, U_GB, 4)):
    MIXER += [("in", first_col + 256 * i, 256, unit + 2 * i + 1) for i in range(n)]
K_YA = len(MIXER)
MIXER += [("wa", 512 * i, 512, U_YA + 4 * i + 3) for i in range(2)]
K_YB = len(MIXER)
MIXER += [("wb", 512 * i, 512, U_YB + 4 * i + 3) for i in range(2)]
K_WO = len(MIXER)
MIXER += [("wo", 256 * i, 256, U_WO + 2 * i + 1) for i in range(4)]
EMBED = [("pp", 512 * i, 512, U_PP + 4 * i + 3) for i in range(2)] + [("pg", 256 * i, 256, U_PG + 2 * i + 1) for i in range(4)]
K_HF, K_HQ, K_HI, K_AQ, K_AK, K_HG, K_GA, K_GB = (
    [c for m, c, _, _ in MIXER if m == "in"].index(o) for o in (O_HF, O_HQ, O_HI, O_AQ, O_AK, O_HG, O_GA, O_GB))
NM, ND, NX_E, NP = len(MIXER), len(DENSE), len(EXPERT), len(EMBED)
assert all(n % SPLIT == 0 and 2 * n % RAW == 0 for n in (NM, ND, NX_E, NP))
LAYER_CHUNKS = NM + ND + NP
K_DENSE, K_EMBED = NM, NM + ND
K_EXPERTS = LAYER_CHUNKS + NM
EMBED_STEP = LAYER_CHUNKS + NE * NX_E - ND

UNIT_OF = {"hf": U_HF, "hq": U_HQ, "hi": U_HI, "aq": U_AQ, "ak": U_AK, "av": U_AV, "swap": U_SW, "hg": U_HG,
           "ga": U_GA, "gb": U_GB, "ya": U_YA, "yb": U_YB, "wo": U_WO}
LAST_OF = {unit: n for n, (_, _, _, unit) in enumerate(MIXER + EMBED)}


def chunk_used(stage, i):
    if (stage, i) == ("merge", 3):
        return LAST_OF[U_YB + 7]
    if (stage, i) == ("ya", 2):
        return LAST_OF[U_GB + 7]
    if (stage, i) in (("wo", DT - 1), ("yb", DT - 1), ("gb", DT - 1)):
        return None
    return LAST_OF.get(UNIT_OF[stage] + i) if stage in UNIT_OF else None


def trunk(nc, x, p, w_in, sinks, rel_bias, vectors, w_branch_a, w_branch_b, w_out, dense_w1, dense_w3,
          dense_w2, router_w, moe_w1, moe_w3, moe_w2, ple_proj, ple_gate, consts, buckets, outside, out):
    ctx = ExitStack()
    with ctx:
        def sb(name, shape, dt=F32):
            return ctx.enter_context(nc.sbuf_tensor(name, shape, dt))

        def sem(name):
            return ctx.enter_context(nc.semaphore(name))

        bias_rows_dram = nc.dram_tensor("bias_rows_dram", (QH, P, 384), F32, kind="Internal").ap()

        raw_ring = sb("raw_ring", [P, RAW, HALF])
        w_hi = sb("w_hi", [P, SPLIT, CHUNK_N], F32R)
        w_lo = sb("w_lo", [P, SPLIT, CHUNK_N], F32R)
        hT = sb("hT", [P, DT, S])
        u_hi = sb("u_hi", [P, DT, S], F32R)
        u_lo = sb("u_lo", [P, DT, S], F32R)
        rstd = sb("rstd", [P, S])
        consts_sb = sb("consts_sb", [P, C_N])
        ident, ones = consts_sb[:, C_ID:C_ID + P], consts_sb[:, C_ONE:C_ONE + P]
        before = consts_sb[:, C_LT:C_LT + P]
        hg_mask = consts_sb[:, C_HM:C_HM + P]
        pair_masks = consts_sb[:, C_PM:C_PM + LEVELS * P].rearrange("p (g n) -> p g n", g=LEVELS)
        slot_iota = consts_sb[:, C_IO:C_IO + CAP]
        scan_mask = consts_sb[:, C_SC:C_SC + CHUNK]
        expert_iota = consts_sb[:, C_I8:C_I8 + NE]
        eps = sb("eps", [P, 1])
        params = sb("params", [P, DEPTH, PCOLS])
        fin_gain = sb("fin_gain", [P, DT])
        gain = sb("gain", [P, PCOLS])
        vec_rows = sb("vec_rows", [P, P])
        lbt = sb("lbt", [P, 3, HH])
        sink = sb("sink", [P, DEPTH, QH])
        p_T = sb("p_T", [P, DEPTH, KP, S])
        rw = sb("rw", [P, DT, NE])
        bias = sb("bias", [P, QH, 2 * P])
        q_factor, k_factor = ([sb(f"{n}_factor{g}", [P, HH * NCH >> g]) for g in range(LEVELS)] for n in "qk")
        smax = sb("smax", [P, 6, 2 * QH])
        gA = sb("gA", [P, DT, S])
        gB = sb("gB", [P, DT, S])
        rt = sb("rt", [P, 8, TT, NE + 1])
        idx8 = sb("idx8", [P, TT, NE], U32)
        cnt = sb("cnt", [P, NE])
        flag = sb("flag", [P, 1], I32)

        mixer_memory = ExitStack()

        def msb(name, shape, dt=F32):
            return mixer_memory.enter_context(nc.sbuf_tensor(name, shape, dt))

        hF = msb("hF", [P, HH, S])
        hK = msb("hK", [P, HH, S])
        hA = msb("hA", [P, HH, S])
        hE = msb("hE", [P, HH, S])
        hKi = msb("hKi", [P, HH, S])
        hQ = msb("hQ", [P, HH, S])
        hV = msb("hV", [P, TT, HH * P])
        hG = msb("hG", [P, HH, S])
        kend = hA[:].rearrange("p h s -> p (h s)")[:, 0:HH * P]
        hO = hF
        chunk_starts = hG[:].rearrange("p h s -> p (h s)")
        dec = [msb(f"dec{g}", [P, HH * NCH >> g]) for g in range(LEVELS)]
        state = msb("state", [P, HH * P])
        pm = msb("pm", [P, HH, TT, P])
        pm_part = gB[:, 0:2, :].rearrange("p g (t n) -> p g t n", t=TT)
        aQ = hG
        aK = msb("aK", [P, KVH, S])
        aV = msb("aV", [P, TT, KVH * HD])
        sc = msb("sc", [P, QH, 384])
        pT = gB[:, 4:7, :].rearrange("p d s -> p (d s)").rearrange("p (two n) -> p two n", two=2)
        aO = hKi
        level_memory = ExitStack()
        q_level, k_level = ([level_memory.enter_context(nc.sbuf_tensor(f"{n}_level{g}", [P, HH, S >> (g == 2)], F32))
                             for g in range(LEVELS)] for n in "qk")
        level_memory.close()
        br_hi = msb("br_hi", [P, DT, S], F32R)
        br_lo = msb("br_lo", [P, DT, S], F32R)
        mixer_memory.close()
        act2 = sb("act2", [P, 2, 2, S])
        act_hi = sb("act_hi", [P, 2, 2, S], F32R)
        act_lo = sb("act_lo", [P, 2, 2, S], F32R)
        gate_cols = sb("gate_cols", [P, TT, P])
        gate_row = sb("gate_row", [P, S])
        p_hi = sb("p_hi", [P, KP, S], F32R)
        p_lo = sb("p_lo", [P, KP, S], F32R)
        pp_out = sb("pp_out", [P, DT, S])
        logit_T = sb("logit_T", [NE, S])
        us = sb("us", [P, DT, CAP])
        us_hi = sb("us_hi", [P, DT, CAP], F32R)
        us_lo = sb("us_lo", [P, DT, CAP], F32R)
        slot_act = sb("slot_act", [P, 2, 2 * P])
        y_tok = sb("y_tok", [P, D])
        comb = sb("comb", [P, S])
        sel_slot = sb("sel_slot", [P, TT, CAP])
        gate_slot = sb("gate_slot", [P, TT, CAP])
        x_in, out_rows = (g[:].rearrange("p d s -> p (d s)").rearrange("p (t n) -> p t n", t=TT) for g in (gB, gA))
        p_in = hG[:].rearrange("p d s -> p (d s)").rearrange("p (l t n) -> p l t n", l=DEPTH, t=TT)
        onehot = sc[0:BUCKETS, 0, :]
        bias_out = sc[0:QH, 1, :]
        rel_sb = sc[0:BUCKETS, 2, 0:QH]
        mask_row = sc[0:QH, 3, :]
        u_tok = out_rows
        logit, top8, picked, gate, pos, ex, tmp8 = (rt[:, i, :, 0:NE] for i in range(7))
        picked_wide, pos_wide = rt[:, 2], rt[:, 4]
        idxf = rt[:, 7, :, 0:NE]
        den = sb("den", [P, TT])

        bank = [ctx.enter_context(nc.psum_tensor(f"bank{i}", [P, 512], F32)) for i in range(8)]

        raw_loaded = [sem(f"raw_loaded{i}") for i in range(RAW)]
        hi_done, lo_done = sem("hi_done"), sem("lo_done")
        consts_in, vec_in, x_loaded, small_in, p_loaded, sc_in = (
            sem(n) for n in ("consts_in", "vec_in", "x_loaded", "small_in", "p_loaded", "sc_in"))
        setup_pe, setup_dve, lb_exp, bias_row_ready, bias_rows_out, bias_in, set_const = (
            sem(n) for n in ("setup_pe", "setup_dve", "lb_exp", "bias_row_ready", "bias_rows_out", "bias_in", "set_const"))
        h_ready, h_ffn = sem("h_ready"), sem("h_ffn")
        sq_ready, rms_ready, u_ready, pooled = sem("sq_ready"), sem("rms_ready"), sem("u_ready"), sem("pooled")
        u_normed, u_hi_ready = sem("u_normed"), sem("u_hi_ready")
        branch_hi, branch_ready, merge_hi, merge_ready = (
            sem(n) for n in ("branch_hi", "branch_ready", "merge_hi", "merge_ready"))
        unit_done, unit_act, unit_dve = sem("unit_done"), sem("unit_act"), sem("unit_dve")
        aux_done, aux_act, aux_dve = sem("aux_done"), sem("aux_act"), sem("aux_dve")
        f_ready, logf_ready, scan_ready, exp_ready, diff_ready, hgrn_ready = (
            sem(n) for n in ("f_ready", "logf_ready", "scan_ready", "exp_ready", "diff_ready", "hgrn_ready"))
        pm_ready, factors_ready, q_ready, k_ready = sem("pm_ready"), sem("factors_ready"), sem("q_ready"), sem("k_ready")
        max_ready, exp_done, prob_ready = sem("max_ready"), sem("exp_done"), sem("prob_ready")
        osq_ready, orms_ready, yb_ready, merged = sem("osq_ready"), sem("orms_ready"), sem("yb_ready"), sem("merged")
        d_used, d_silu, d_mul, d_hi, d_act = (sem(n) for n in ("d_used", "d_silu", "d_mul", "d_hi", "d_act"))
        m_used, m_silu, m_mul, m_hi, m_act = (sem(n) for n in ("m_used", "m_silu", "m_mul", "m_hi", "m_act"))
        d_result = sem("d_result")
        act_turned, starts_ready = sem("act_turned"), sem("starts_ready")
        p_hi_ready, p_split = sem("p_hi_ready"), sem("p_split")
        r_pe, r_act, r_dve, route_ready = sem("r_pe"), sem("r_act"), sem("r_dve"), sem("route_ready")
        r_tok, logits_copied, p_turned = sem("r_tok"), sem("logits_copied"), sem("p_turned")
        slots_ready, gathered, us_copied, us_hi_ready, us_ready = (
            sem(n) for n in ("slots_ready", "gathered", "us_copied", "us_hi_ready", "us_ready"))
        y_act, y_dve, comb_tr, comb_ready, comb_done = (
            sem(n) for n in ("y_act", "y_dve", "comb_tr", "comb_ready", "comb_done"))
        fin_ready, fin_tr, row_ready, out_done = sem("fin_ready"), sem("fin_tr"), sem("row_ready"), sem("out_done")

        def wview(n, tiles, cols):
            return [w[:, n % SPLIT, 0:tiles * cols].rearrange("p (k n) -> p k n", k=tiles) for w in (w_hi, w_lo)]

        def columns(w, c0, n):
            return [part[:, :, c0:c0 + n] for part in w]

        def await_chunk(eng, n, turns):
            eng.wait_ge(lo_done, 2 * (n + 1) + RAW * turns)

        def half_views(n, half, size):
            at = slice(half * size, (half + 1) * size)
            return raw_ring[:, (2 * n + half) % RAW, 0:size], w_hi[:, n % SPLIT, at], w_lo[:, n % SPLIT, at]

        def await_unit_free(eng, u, l):
            if u >= RING:
                n = u - RING
                if UNITS[n] == "A":
                    eng.wait_ge(unit_act, UA * l + UNITS[:n + 1].count("A"))
                else:
                    eng.wait_ge(unit_dve, UD * l + UNITS[:n + 1].count("D"))

        def await_unit_read(eng, u, l):
            if UNITS[u] == "A":
                eng.wait_ge(unit_act, UA * l + UNITS[:u + 1].count("A"))
            else:
                eng.wait_ge(unit_dve, UD * l + UNITS[:u + 1].count("D"))

        def await_aux_free(eng, u, l):
            if u >= X_RING:
                await_aux_read(eng, u - X_RING, l)

        def await_aux_read(eng, u, l):
            if X_DRAIN[u] == "A":
                eng.wait_ge(aux_act, XA * l + X_DRAIN[:u + 1].count("A"))
            else:
                eng.wait_ge(aux_dve, XD * l + X_DRAIN[:u + 1].count("D"))

        def ubank(u):
            return bank[u % RING]

        def xbank(u):
            return bank[RING + u % X_RING]

        def ssq_bank(unit):
            return bank[3] if unit == X_PLE else xbank(unit)

        block = ctx.enter_context(nc.Block())

        @block.sync
        def _(sp):
            src = {"in": w_in, "wo": w_out, "pg": ple_gate, "wa": w_branch_a, "wb": w_branch_b, "pp": ple_proj}

            def load(n, turns, chunk_dst_k, source, cols):
                for half in range(2):
                    i = 2 * n + half
                    if i >= RAW:
                        sp.wait_ge(lo_done, i - RAW + 1 + RAW * turns)
                    k = chunk_dst_k // 2
                    dst = raw_ring[:, i % RAW, 0:k * cols].rearrange("p (k n) -> p k n", k=k)
                    sp.dma_start(dst, source[:, half * k:(half + 1) * k, :]).then_inc(raw_loaded[i % RAW], 16)

            def by_columns(table, l, n0):
                for i, (matrix, c0, cols, _) in enumerate(table):
                    w = src[matrix][l].rearrange("(k p) n -> p k n", p=P)
                    load(n0 + i, 0, w.shape[1], w[:, :, c0:c0 + cols], cols)

            def swiglu(order, n0, turns, w1, w3, w2):
                for i, (m, j) in enumerate(order):
                    if m == "w2":
                        source = w2[2 * j * P:(2 * j + 2) * P, :].rearrange("(k p) n -> p k n", p=P)
                        load(n0 + i, turns, 2, source, D)
                    else:
                        w = {"w1": w1, "w3": w3}[m].rearrange("(k p) n -> p k n", p=P)
                        load(n0 + i, turns, DT, w[:, :, 2 * j * P:(2 * j + 2) * P], 2 * P)

            sp.dma_start(consts_sb[:], consts).then_inc(consts_in, 16)
            by_columns(MIXER, 0, 0)
            swiglu(DENSE, K_DENSE, 0, dense_w1[0], dense_w3[0], dense_w2[0])
            by_columns(EMBED, 0, K_EMBED)
            by_columns(MIXER, 1, LAYER_CHUNKS)
            with sp.Fori(0, NE) as e:
                swiglu(EXPERT, K_EXPERTS, NX_E // SPLIT * e, moe_w1[0, e], moe_w3[0, e], moe_w2[0, e])
            by_columns(EMBED, 1, K_EMBED + EMBED_STEP)

        mixer_turns = lambda l: LAYER_CHUNKS // SPLIT * l
        embed_turns = lambda l: EMBED_STEP // SPLIT * l

        @block.tensor
        def _(pe):
            mm = nc.tensor.matmul

            def product(dst, stationary, moving, tiles, start=True, stop=True):
                (s_hi, s_lo), (m_hi_part, m_lo_part) = stationary, moving
                for k in range(tiles):
                    mm(dst, s_hi[:, k, :], m_hi_part[:, k, :], start=start and k == 0, stop=False, skip_group_check=True)
                    mm(dst, s_hi[:, k, :], m_lo_part[:, k, :], start=False, stop=False, skip_group_check=True)
                    last = mm(dst, s_lo[:, k, :], m_hi_part[:, k, :], start=False, stop=stop and k == tiles - 1,
                              skip_group_check=True)
                return last

            stream = [u_hi, u_lo]

            def transpose(dst, a, parts=P):
                return nc.tensor.transpose(dst, a, consts_sb[0:parts, C_ID:C_ID + parts])

            def sum_of_squares(norm, unit, l, k):
                if k < POOLED - 1:
                    return
                if k == POOLED - 1:
                    await_aux_free(pe, unit, l)
                    pe.wait_ge(pooled, 3 * l + norm + 1)
                else:
                    pe.wait_ge(sq_ready, 24 * l + 8 * norm + k + 1)
                tile = 0 if k < POOLED else k
                last = mm(ssq_bank(unit)[:, 0:S], ones, gA[:, tile, :], start=(k == POOLED - 1), stop=(k == DT - 1),
                          skip_group_check=True)
                if k == DT - 1:
                    last.then_inc(aux_done, 1)

            def keep_clock(n, spare):
                for _ in range(n):
                    mm(bank[spare][:, 0:P], ones, ident, start=True, stop=True)

            def first_products(hi_ready, lo_ready, earlier, targets):
                for n, (dst, w, begins, _) in enumerate(targets):
                    for k in range(DT):
                        if n == 0 and k % 2 == 0:
                            pe.wait_ge(hi_ready, earlier + k // 2 + 1)
                        mm(dst, w[0][:, k, :], u_hi[:, k, :], start=begins and k == 0, stop=False, skip_group_check=True)
                        mm(dst, w[1][:, k, :], u_hi[:, k, :], start=False, stop=False, skip_group_check=True)
                for n, (dst, w, _, sem_) in enumerate(targets):
                    for k in range(DT):
                        if n == 0 and k % 2 == 0:
                            pe.wait_ge(lo_ready, earlier + k // 2 + 1)
                        last = mm(dst, w[0][:, k, :], u_lo[:, k, :], start=False, stop=(k == DT - 1), skip_group_check=True)
                    if sem_:
                        last.then_inc(sem_, 1)

            def unit_product(n, l, stationary, moving, tiles):
                await_unit_free(pe, n, l)
                product(ubank(n)[:, 0:S], stationary, moving, tiles).then_inc(unit_done, 1)

            pe.wait_ge(consts_in, 16)
            pe.wait_ge(vec_in, 16)
            transpose(bank[0][:, 0:NVEC], vec_rows[0:NVEC, :], NVEC).then_inc(setup_pe, 1)
            keep_clock(N_KEEP // 2, 6)
            pe.wait_ge(x_loaded, 16)
            for j in range(DT // 2):
                for k in (2 * j, 2 * j + 1):
                    for t in range(TT):
                        c = (k % 2) * S + t * P
                        last = transpose(bank[X_BANKS[j]][:, c:c + P], x_in[:, t, k * P:(k + 1) * P])
                last.then_inc(setup_pe, 1)
            def mixer(l):
                for stage, i in STEPS:
                    if stage == "hf" and i < 2:
                        if i == 0:
                            keep_clock(N_KEEP, 5)
                            await_chunk(pe, K_HF, mixer_turns(l))
                            w = wview(K_HF, DT, 256)
                            first_products(u_hi_ready, u_ready, 12 * l, [(ubank(U_HF + n)[:, 0:S], columns(w, n * P, P), True, unit_done)
                                                  for n in range(2)])
                    elif stage in ("hf", "hq", "aq", "hg", "ga", "gb"):
                        c = {"hf": K_HF, "hq": K_HQ, "aq": K_AQ, "hg": K_HG, "ga": K_GA, "gb": K_GB}[stage] + i // 2
                        await_chunk(pe, c, mixer_turns(l))
                        unit_product(UNIT_OF[stage] + i, l, columns(wview(c, DT, 256), (i % 2) * P, P), stream, DT)
                    elif stage == "hi":
                        half, t = i // 2, i % 2
                        await_chunk(pe, K_HI + half, mixer_turns(l))
                        unit_product(U_HI + i, l, columns(stream, t * P, P), wview(K_HI + half, DT, 256), DT)
                    elif stage == "ak":
                        await_chunk(pe, K_AK, mixer_turns(l))
                        unit_product(U_AK, l, columns(wview(K_AK, DT, 256), 0, P), stream, DT)
                    elif stage == "av":
                        unit_product(U_AV + i, l, columns(stream, i // 2 * P, P), wview(K_AK, DT, 256), DT)
                    elif stage == "swap":
                        await_unit_read(pe, U_AK, l)
                        await_unit_free(pe, U_SW, l)
                        mm(ubank(U_SW)[0:HD, 0:S], ident[:, HD:P], aK[:, 0, :], start=True, stop=True)
                        mm(ubank(U_SW)[HD:P, 0:S], ident[:, 0:HD], aK[:, 0, :], start=True, stop=True).then_inc(unit_done, 1)
                    elif stage == "kt":
                        u = nth("kt", 0)
                        pe.wait_ge(k_ready, LEVELS * l + LEVELS)
                        await_aux_free(pe, u, l)
                        for h in range(HH):
                            last = transpose(xbank(u)[:, h * P:(h + 1) * P], k_level[2][:, h, :])
                        last.then_inc(aux_done, 1)
                    elif stage == "st":
                        u = nth("st", 0)
                        await_aux_read(pe, nth("kt", 0), l)
                        await_aux_free(pe, u, l)
                        for h in range(HH):
                            last = mm(xbank(u)[:, h * P:(h + 1) * P], kend[:, h * P:(h + 1) * P],
                                      hV[:, 0, h * P:(h + 1) * P], start=True, stop=True)
                        last.then_inc(aux_done, 1)
                    elif stage == "p":
                        h, part = i // 2, i % 2
                        u = nth("p", i)
                        pe.wait_ge(hgrn_ready, l + 1)
                        if part:
                            pe.wait_ge(q_ready, LEVELS * l + 2)
                            pe.wait_ge(k_ready, LEVELS * l + 2)
                        await_aux_free(pe, u, l)
                        pairs = ((k_level[0], q_level[0]), (k_level[1], q_level[1])) if part else ((hKi, hQ), (hF, hQ))
                        for g, (keys, queries) in enumerate(pairs):
                            for t in range(TT):
                                cols = slice(t * P, (t + 1) * P)
                                last = mm(xbank(u)[:, g * S + t * P:g * S + (t + 1) * P], keys[:, h, cols],
                                          queries[:, h, cols], start=True, stop=True)
                        last.then_inc(aux_done, 1)
                    elif stage == "sc":
                        u = nth("sc", i)
                        await_unit_read(pe, U_AQ + 3, l)
                        pe.wait_ge(p_turned, DEPTH)
                        await_unit_read(pe, U_SW, l)
                        await_aux_free(pe, u, l)
                        r = slice((i % 2) * HD, (i % 2 + 1) * HD)
                        q, k = aQ[r, i // 2, :], aK[r, int(i % 2 != i // GROUP), :]
                        mm(xbank(u)[:, 0:P], q[:, 0:P], k[:, 0:P], start=True, stop=True)
                        mm(xbank(u)[:, P:P + S], q[:, P:S], k, start=True, stop=True).then_inc(aux_done, 1)
                    elif stage == "pt":
                        u = nth("pt", i)
                        pe.wait_ge(prob_ready, l + 1)
                        await_aux_free(pe, u, l)
                        for b in range(3):
                            last = transpose(xbank(u)[:, b * P:(b + 1) * P], sc[:, i, b * P:(b + 1) * P])
                        last.then_inc(aux_done, 1)
                    elif stage == "pv":
                        u = nth("pv", i)
                        await_aux_free(pe, u, l)
                        for h in (2 * i, 2 * i + 1):
                            await_aux_read(pe, nth("pt", h), l)
                            dst = xbank(u)[(h % 2) * HD:(h % 2 + 1) * HD, 0:S]
                            g = slice(h // GROUP * HD, (h // GROUP + 1) * HD)
                            mm(dst[:, 0:P], aV[:, 0, g], pT[:, h % 2, 0:P], start=True, stop=True)
                            mm(dst[:, P:S], aV[:, 0, g], pT[:, h % 2, P:2 * P], start=True, stop=False)
                            last = mm(dst[:, P:S], aV[:, 1, g], pT[:, h % 2, 2 * P:3 * P], start=False, stop=True)
                        last.then_inc(aux_done, 1)
                    elif stage == "o":
                        u = nth("o", i)
                        pe.wait_ge(pm_ready, 4 * l + i + 1)
                        await_aux_read(pe, nth("st", 0), l)
                        pe.wait_ge(q_ready, LEVELS * l + LEVELS)
                        await_aux_free(pe, u, l)
                        cols = slice(i * P, (i + 1) * P)
                        mm(xbank(u)[:, 0:P], hV[:, 0, cols], pm[:, i, 0, :], start=True, stop=True)
                        mm(xbank(u)[:, P:S], hV[:, 1, cols], pm[:, i, 1, :], start=True, stop=False)
                        mm(xbank(u)[:, P:S], state[:, cols], q_level[2][:, i, :], start=False, stop=True).then_inc(aux_done, 1)
                    elif stage == "osq":
                        u = nth("osq", i)
                        pe.wait_ge(osq_ready, 4 * l + 2 * i + 2)
                        await_aux_free(pe, u, l)
                        mm(xbank(u)[:], ones, hK[:, 2 * i:2 * i + 2, :].rearrange("p h s -> p (h s)"),
                           start=True, stop=True).then_inc(aux_done, 1)
                    elif stage in ("ya", "yb"):
                        c = (K_YA if stage == "ya" else K_YB) + i // 4
                        await_chunk(pe, c, mixer_turns(l))
                        pe.wait_ge(branch_ready, 2 * l + (1 if stage == "ya" else 2))
                        first = 0 if stage == "ya" else 4
                        unit_product(UNIT_OF[stage] + i, l, columns(wview(c, 4, 512), (i % 4) * P, P),
                                     [part[:, first:first + 4, :] for part in (br_hi, br_lo)], 4)
                    elif stage == "ssq":
                        sum_of_squares(1, X_FFN, l, i)
                    elif stage == "wo":
                        c = K_WO + i // 2
                        await_chunk(pe, c, mixer_turns(l))
                        w = wview(c, DT, 256)
                        if i == 0:
                            for n in range(2):
                                await_unit_free(pe, U_WO + n, l)
                            first_products(merge_hi, merge_ready, 4 * l,
                                           [(ubank(U_WO + n)[:, 0:S], columns(w, n * P, P), True, unit_done) for n in range(2)])
                        elif i >= 2:
                            unit_product(U_WO + i, l, columns(w, (i % 2) * P, P), stream, DT)

            def swiglu_all(order, n0, turns, pairs0, used, act_ready, result=None):
                last_pair = len(order) // 3 - 1
                for i, (m, j) in enumerate(order):
                    await_chunk(pe, n0 + i, turns)
                    if m == "w2":
                        pe.wait_ge(act_ready, pairs0 + j + 1)
                        w = wview(n0 + i, 2, D)
                        for d in range(DT):
                            last = product(bank[4 + d // 2][:, (d % 2) * S:(d % 2 + 1) * S], columns(w, d * P, P),
                                           [act_hi[:, j % 2], act_lo[:, j % 2]], 2, start=(j == 0 and d % 2 == 0),
                                           stop=(j == last_pair))
                            if result and j == last_pair:
                                if d % 2:
                                    last.then_inc(result, 1)
                        if result and j == last_pair:
                            continue
                    else:
                        if m == "w1" and j >= 2:
                            pe.wait_ge(act_ready, pairs0 + j - 1)
                        w = wview(n0 + i, DT, 2 * P)
                        dst = [bank[2 * (j % 2) + (m == "w3")][:, a * S:(a + 1) * S] for a in range(2)]
                        if result and i == 0:
                            first_products(u_hi_ready, u_ready, 4, [(dst[a], columns(w, a * P, P), a == 0, used if a else None) for a in range(2)])
                            continue
                        for a in range(2):
                            last = product(dst[a], columns(w, a * P, P), stream, DT)
                    last.then_inc(used, 1)

            def embed_input(units, l):
                for i in units:
                    c = K_EMBED + i // 4
                    await_chunk(pe, c, embed_turns(l))
                    pe.wait_ge(p_split, l + 1)
                    unit_product(U_PP + i, l, columns(wview(c, KP, HALF), (i % 4) * P, P), [p_hi, p_lo], KP)

            def dense(l):
                keep_clock(N_KEEP, 6)
                swiglu_all(DENSE, K_DENSE, 0, 0, d_used, d_act, d_result)
                embed_input(range(RING), l)
                for k in range(DT):
                    sum_of_squares(2, X_PLE, 0, k)
                embed_input(range(RING, DT), l)

            def expert(e):
                def turn_act(j):
                    pe.wait_ge(m_mul, PAIRS * e + j + 3)
                    for a in range(2):
                        last = transpose(bank[j % 2][:, a * P:(a + 1) * P], slot_act[:, j % 2, a * P:(a + 1) * P])
                    last.then_inc(act_turned, 1)

                pe.wait_ge(us_ready, e + 1)
                for i, (m, j) in enumerate(EXPERT):
                    n = K_EXPERTS + i
                    if m == "w2" and j == PAIRS - 2:
                        turn_act(PAIRS - 1)
                    await_chunk(pe, n, NX_E // SPLIT * e)
                    if m == "w2":
                        pe.wait_ge(m_act, PAIRS * e + j + 3)
                        w = wview(n, 2, D)
                        for half in range(2):
                            last = product(bank[6 + half][:], [act_hi[:, j % 2, :, 0:P], act_lo[:, j % 2, :, 0:P]],
                                           columns(w, 512 * half, 512), 2, start=(j == 0), stop=(j == PAIRS - 1))
                    else:
                        pe.wait_ge(m_act if m == "w1" else m_mul, PAIRS * e + j + 1)
                        last = product(bank[j % 2 + 2 * (m == "w3")][:, 0:2 * P], [us_hi, us_lo], wview(n, DT, 2 * P), DT)
                    last.then_inc(m_used, 1)
                    if m == "w1" and j >= 1:
                        turn_act(j - 1)
                    if m == "w3" and j in (1, 2):
                        combine(e, j - 1)
                    if m == "w3" and j == 4:
                        pe.wait_ge(slots_ready, 2 * e + 2)
                        pe.wait_ge(h_ffn, 4 * e + 8)
                        for t in range(TT):
                            last = transpose(bank[4][:, t * P:(t + 1) * P], gate_slot[:, t, :])
                        last.then_inc(comb_tr, 1)
                    if m == "w3" and j == 7:
                        pe.wait_ge(comb_ready, e + 2)
                        pe.wait_ge(slots_ready, 2 * e + 3)
                        gather()

            def combine(e, part):
                if part == 0:
                    pe.wait_ge(y_act, e + 1)
                    pe.wait_ge(y_dve, e + 1)
                    pe.wait_ge(comb_ready, e + 1)
                for d in range(4 * part, 4 * part + 4):
                    if part == 1 and d % 2 == 0:
                        pe.wait_ge(h_ffn, 4 * e + 5 + (d - 4) // 2)
                    last = mm(bank[4 + d // 2 % 2][:, (d % 2) * S:(d % 2 + 1) * S], y_tok[:, d * P:(d + 1) * P], comb[:],
                              start=True, stop=True)
                    if d % 2:
                        last.then_inc(comb_done, 1)

            def gather():
                for d in range(DT):
                    for t in range(TT):
                        last = mm(bank[4 + d // 4][:, (d % 4) * CAP:(d % 4 + 1) * CAP], u_tok[:, t, d * P:(d + 1) * P],
                                  sel_slot[:, t, :], start=(t == 0), stop=(t == TT - 1))
                    if d % 4 == 3:
                        last.then_inc(gathered, 1)

            def moe():
                keep_clock(N_KEEP - 4, 6)
                for k in range(DT):
                    if k % 2 == 0:
                        pe.wait_ge(u_normed, 16 + k // 2 + 1)
                    last = mm(bank[4][0:NE, 0:S], rw[:, k, :], gB[:, k, :], start=(k == 0), stop=(k == DT - 1))
                last.then_inc(r_pe, 1)
                for t in range(TT):
                    for half in range(2):
                        for j in range(4):
                            last = transpose(bank[2 * (t == 1) + half][:, j * P:(j + 1) * P],
                                             gB[:, 4 * half + j, t * P:(t + 1) * P])
                        last.then_inc(r_tok, 1)
                        if t == 0 and half == 0:
                            pe.wait_ge(logits_copied, 1)
                            for t2 in range(TT):
                                last = transpose(bank[5][:, 32 + t2 * NE:32 + (t2 + 1) * NE], logit_T[:, t2 * P:(t2 + 1) * P], NE)
                            last.then_inc(r_pe, 1)
                pe.wait_ge(r_dve, 1)
                mm(bank[5][:, 0:8], before, picked[:, 0, :], start=True, stop=True)
                mm(bank[5][:, 8:16], ones, picked[:, 0, :], start=True, stop=False)
                mm(bank[5][:, 8:16], before, picked[:, 1, :], start=False, stop=True)
                mm(bank[5][:, 16:24], ones, picked[:, 0, :], start=True, stop=False)
                mm(bank[5][:, 16:24], ones, picked[:, 1, :], start=False, stop=True).then_inc(r_pe, 1)
                pe.wait_ge(r_act, 4)
                pe.wait_ge(route_ready, 1)
                fullest = pe.value_load(flag[0:1, 0:1], min_val=0, max_val=S)
                with pe.If(fullest <= CAP):
                    keep_clock(N_KEEP, 6)
                    pe.wait_ge(slots_ready, 1)
                    gather()
                    keep_clock(N_KEEP, 6)
                    with pe.Fori(0, NE) as e:
                        expert(e)
                    for part in range(2):
                        combine(NE, part)
                with pe.Else():
                    with pe.Fori(0, NE) as e:
                        pe.wait_ge(h_ffn, 4 * e + 4)
                        pe.wait_ge(slots_ready, e + 1)
                        for t in range(TT):
                            last = mm(bank[0][:, t * P:(t + 1) * P], gate_cols[:, t, :], ident, start=True, stop=True)
                        last.then_inc(gathered, 1)
                        pe.wait_ge(us_copied, e + 1)
                        swiglu_all(EXPERT, K_EXPERTS, NX_E // SPLIT * e, PAIRS * e, m_used, m_act)

            for k in range(DT):
                sum_of_squares(0, X_SSQ, 0, k)
            pe.wait_ge(sc_in, 48)
            mm(bank[4][0:QH, 0:384], rel_sb, onehot, start=True, stop=True).then_inc(setup_pe, 1)
            pe.wait_ge(p_loaded, 16)
            for l in range(DEPTH):
                for k in range(KP):
                    for t in range(TT):
                        c = k * S + t * P
                        last = transpose(bank[P_BANKS[l]][:, c:c + P], p_in[:, l, t, k * P:(k + 1) * P])
                last.then_inc(setup_pe, 1)
            with pe.Fori(0, DEPTH) as l:
                mixer(l)
                with pe.If(l < 1):
                    dense(l)
                with pe.Else():
                    moe()
                    embed_input(range(RING), l)
                    for k in range(DT):
                        sum_of_squares(2, X_PLE, 1, k)
                    embed_input(range(RING, DT), l)
                    pe.drain()
                for i in range(DT):
                    c = K_EMBED + 2 + i // 2
                    w = wview(c, DT, 256)
                    if i == 0:
                        keep_clock(4, 6)
                        await_chunk(pe, c, embed_turns(l))
                        for n in range(2):
                            await_unit_free(pe, U_PG + n, l)
                        first_products(u_hi_ready, u_ready, 12 * l + 8, [(ubank(U_PG + n)[:, 0:S], columns(w, n * P, P), True, unit_done)
                                              for n in range(2)])
                    elif i >= 2:
                        await_chunk(pe, c, embed_turns(l))
                        unit_product(U_PG + i, l, columns(w, (i % 2) * P, P), stream, DT)
                    if i >= 2:
                        sum_of_squares(3, 0, l, i - 2)
                for k in (DT - 2, DT - 1):
                    sum_of_squares(3, 0, l, k)

            keep_clock(N_KEEP - 4, 2)
            for k in range(DT):
                pe.wait_ge(fin_ready, k + 1)
                for t in range(TT):
                    last = transpose(bank[4 + 2 * t + k // 4 if t == 0 else 6 + k // 4][:, (k % 4) * P:(k % 4 + 1) * P],
                                     gB[:, k, t * P:(t + 1) * P])
            last.then_inc(fin_tr, 1)

        @block.scalar
        def _(act):
            fn = nc.scalar.activation

            act.dma_start(vec_rows[0:NVEC, :], vectors).then_inc(vec_in, 16)
            act.dma_start(x_in, x.rearrange("(t p) n -> p t n", p=P)).then_inc(x_loaded, 16)
            act.dma_start(onehot, buckets).then_inc(sc_in, 16)
            act.dma_start(rel_sb, rel_bias).then_inc(sc_in, 16)
            act.dma_start(mask_row, outside).then_inc(sc_in, 16)
            act.dma_start(p_in, p.rearrange("l (t p) n -> p l t n", p=P)).then_inc(p_loaded, 16)
            act.dma_start(sink[:].rearrange("p l h -> p (l h)"),
                          sinks.rearrange("l h -> (l h)").partition_broadcast(P)).then_inc(small_in, 16)
            act.dma_start(rw[:], router_w[0].rearrange("(k p) e -> p k e", p=P)).then_inc(small_in, 16)
            act.wait_ge(set_const, 1)
            act.wait_ge(setup_dve, 1)
            fn(lbt[:, 0:2, :], lbt[:, 0:2, :], ACT.Exp).then_inc(lb_exp, 1)

            def rms(unit, l):
                act.wait_ge(aux_done, NX * l + unit + 1)
                fn(rstd[:], ssq_bank(unit)[:, 0:S], ACT.Ln, scale=1.0 / D, bias=eps[:]).then_inc(aux_act, 1)
                act.drain()
                fn(rstd[:], rstd[:], ACT.Exp, scale=-0.5).then_inc(rms_ready, 1)

            def square(k0, n=1):
                fn(gA[:, k0:k0 + n, :], hT[:, k0:k0 + n, :], ACT.Square).then_inc(sq_ready, n)

            def split_hi(n, turns, size=HALF):
                for half in range(2):
                    raw, hi, _ = half_views(n, half, size)
                    i = 2 * n + half
                    act.wait_ge(raw_loaded[i % RAW], 16 * (i // RAW + 1) + 16 * turns)
                    fn(hi, raw, ACT.Copy).then_inc(hi_done, 1)

            def u_part(norm, l, j):
                act.wait_ge(u_normed, 12 * l + 4 * norm + j + 1)
                fn(u_hi[:, 2 * j:2 * j + 2, :], gB[:, 2 * j:2 * j + 2, :], ACT.Copy).then_inc(u_hi_ready, 1)

            def unit_wait(u, l):
                act.wait_ge(unit_done, NU * l + u + 1)

            def aux_wait(u, l):
                act.wait_ge(aux_done, NX * l + u + 1)

            def mixer(l):
                for stage, i in STEPS:
                    stage_work(stage, i, l)
                    used = chunk_used(stage, i)
                    if used is not None:
                        unit_wait(MIXER[used][3], l)
                        split_hi(used + SPLIT, mixer_turns(l))

            def stage_work(stage, i, l):
                if stage == "hf":
                    unit_wait(U_HF + i, l)
                    fn(hF[:, i, :], ubank(U_HF + i)[:, 0:S], ACT.Sigmoid).then_inc(unit_act, 1)
                elif stage == "gates":
                    act.wait_ge(f_ready, l + 1)
                    fn(hF[:], hF[:], ACT.Ln).then_inc(logf_ready, 1)
                elif stage == "scan":
                    act.wait_ge(scan_ready, l + 1)
                    fn(hE[:], hA[:], ACT.Exp).then_inc(exp_ready, 1)
                    fn(hKi[:], hA[:], ACT.Exp, scale=-1.0).then_inc(exp_ready, 1)
                    act.wait_ge(diff_ready, l + 1)
                    fn(hF[:], hF[:], ACT.Exp).then_inc(exp_ready, 1)
                elif stage == "aq":
                    unit_wait(U_AQ + i, l)
                    fn(aQ[:, i, :], ubank(U_AQ + i)[:, 0:S], ACT.Copy, scale=HD ** -0.5).then_inc(unit_act, 1)
                elif stage in ("kt", "st"):
                    u = nth(stage, 0)
                    aux_wait(u, l)
                    fn(kend if stage == "kt" else state[:], xbank(u)[:], ACT.Copy).then_inc(aux_act, 1)
                elif stage == "softmax":
                    act.wait_ge(max_ready, l + 1)
                    for b in range(2):
                        for h in range(QH):
                            s = sc[:, h, 0:P] if b == 0 else sc[:, h, P:P + S]
                            j = b * QH + h
                            fn(s, s, ACT.Exp, bias=smax[:, 1, j:j + 1], accum_out=smax[:, 2, j:j + 1])
                    fn(smax[:, 3, :], smax[:, 3, :], ACT.Exp).then_inc(exp_done, 1)
                elif stage == "hg":
                    unit_wait(U_HG + i, l)
                    fn(hG[:, i, :], ubank(U_HG + i)[:, 0:S], ACT.Silu).then_inc(unit_act, 1)
                elif stage in ("ga", "gb"):
                    u, dst = (U_GA + i, gA) if stage == "ga" else (U_GB + i, gB)
                    unit_wait(u, l)
                    fn(dst[:, i, :], ubank(u)[:, 0:S], ACT.Sigmoid).then_inc(unit_act, 1)
                elif stage == "pt":
                    u = nth("pt", i)
                    aux_wait(u, l)
                    if i >= 2:
                        aux_wait(nth("pv", i // 2 - 1), l)
                    fn(pT[:, i % 2, :], xbank(u)[:, 0:384], ACT.Copy).then_inc(aux_act, 1)
                elif stage == "o":
                    u = nth("o", i)
                    aux_wait(u, l)
                    fn(hK[:, i, :], xbank(u)[:, 0:S], ACT.Square).then_inc(osq_ready, 1)
                    fn(hO[:, i, :], xbank(u)[:, 0:S], ACT.Copy).then_inc(aux_act, 1)
                elif stage == "osq":
                    u = nth("osq", i)
                    aux_wait(u, l)
                    r = hE[:, 2 * i:2 * i + 2, :].rearrange("p h s -> p (h s)")
                    fn(r, xbank(u)[:], ACT.Ln, scale=1.0 / P, bias=eps[:]).then_inc(aux_act, 1)
                    act.drain()
                    fn(r, r, ACT.Exp, scale=-0.5).then_inc(orms_ready, 1)

                elif stage in ("ak", "swap"):
                    n = UNIT_OF[stage]
                    unit_wait(n, l)
                    fn(aK[:, int(stage == "swap"), :], ubank(n)[:, 0:S], ACT.Copy).then_inc(unit_act, 1)
                elif stage == "wo":
                    await_unit_read(act, U_WO + i, l)
                    square(i)
                elif stage == "branch":
                    if i == 0:
                        await_aux_read(act, nth("pv", 3), l)
                        fn(br_hi[:, 0:4, :], aO[:], ACT.Copy).then_inc(branch_hi, 1)
                    else:
                        act.wait_ge(yb_ready, l + 1)
                        fn(br_hi[:, 4:8, :], hO[:], ACT.Copy).then_inc(branch_hi, 1)
                elif stage == "merge":
                    unit_wait(U_YB + 2 * i + 1, l)
                    act.wait_ge(merged, 8 * l + 2 * i + 2)
                    fn(u_hi[:, 2 * i:2 * i + 2, :], gA[:, 2 * i:2 * i + 2, :], ACT.Copy).then_inc(merge_hi, 1)

            def swiglu_all(order, n0, turns, pairs0, chunks0, used, silu_sem, mul_sem, hi_sem, act_ready, result=None):
                for i, (m, j) in enumerate(order):
                    if result and i == len(order) - 1:
                        for q in range(4):
                            act.wait_ge(h_ffn, q + 1)
                            square(2 * q, 2)
                        act.wait_ge(result, 4)
                    else:
                        act.wait_ge(used, chunks0 + i + 1)
                    if m == "w1":
                        if j >= 2:
                            act.wait_ge(act_ready, pairs0 + j - 1)
                        fn(act2[:, j % 2], bank[2 * (j % 2)][:].rearrange("p (a s) -> p a s", a=2), ACT.Silu).then_inc(silu_sem, 1)
                    if not (result and i == len(order) - 1):
                        split_hi(n0 + i + SPLIT, turns)
                    if m == "w3":
                        act.wait_ge(mul_sem, pairs0 + j + 1)
                        fn(act_hi[:, j % 2], act2[:, j % 2], ACT.Copy).then_inc(hi_sem, 1)

            def expert(e):
                def hi_of_turned(j):
                    act.wait_ge(act_turned, PAIRS * e + j + 1)
                    fn(act_hi[:, j % 2, :, 0:P], bank[j % 2][:, 0:2 * P].rearrange("p (a s) -> p a s", a=2),
                       ACT.Copy).then_inc(m_hi, 1)

                for i, (m, j) in enumerate(EXPERT):
                    act.wait_ge(m_used, NX_E * e + i + 1)
                    if m == "w1":
                        fn(slot_act[:, j % 2], bank[j % 2][:, 0:2 * P], ACT.Silu).then_inc(m_silu, 1)
                    if m == "w3" and j == PAIRS - 1:
                        act.wait_ge(us_copied, e + 2)
                        fn(us_hi[:], us[:], ACT.Copy).then_inc(us_hi_ready, 1)
                    if m == "w2" and j == PAIRS - 1:
                        fn(y_tok[:, 0:512], bank[6][:], ACT.Copy).then_inc(y_act, 1)
                    split_hi(K_EXPERTS + i + SPLIT, NX_E // SPLIT * e)
                    if m == "w1" and j >= 1:
                        hi_of_turned(j - 1)
                    if m == "w3" and j == PAIRS - 1:
                        hi_of_turned(j)

            def moe():
                for t in range(TT):
                    for half in range(2):
                        act.wait_ge(r_tok, 1 + 2 * t + half)
                        fn(u_tok[:, t, 512 * half:512 * half + 512], bank[2 * t + half][:], ACT.Copy).then_inc(r_act, 1)
                act.wait_ge(r_dve, 2)
                fn(ex, ex, ACT.Exp).then_inc(r_act, 1)
                act.wait_ge(route_ready, 1)
                fullest = act.value_load(flag[0:1, 0:1], min_val=0, max_val=S)
                with act.If(fullest <= CAP):
                    act.wait_ge(us_copied, 1)
                    fn(us_hi[:], us[:], ACT.Copy).then_inc(us_hi_ready, 1)
                    fn(y_tok[:, 0:512], consts_sb[:, 0:512], ACT.Copy, scale=0.0).then_inc(y_act, 1)
                    with act.Fori(0, NE) as e:
                        expert(e)
                with act.Else():
                    with act.Fori(0, NE) as e:
                        swiglu_all(EXPERT, K_EXPERTS, NX_E // SPLIT * e, PAIRS * e, NX_E * e, m_used, m_silu, m_mul, m_hi, m_act)
                act.drain()

            for q in range(4):
                act.wait_ge(h_ready, 2 * q + 2)
                square(2 * q, 2)
            split_hi(0, 0)
            rms(X_SSQ, 0)
            with act.Fori(0, DEPTH) as l:
                for j in range(4):
                    u_part(0, l, j)
                with act.If(l < 1):
                    split_hi(1, 0)
                split_hi(2, mixer_turns(l))
                mixer(l)
                rms(X_FFN, l)
                for j in range(4):
                    u_part(1, l, j)
                split_hi(NM - 1 + SPLIT, mixer_turns(l))
                fn(p_hi[:], p_T[:, bass.ds(l, 1)].rearrange("p a k s -> p (a k) s"), ACT.Copy).then_inc(p_hi_ready, 1)
                with act.If(l < 1):
                    swiglu_all(DENSE, K_DENSE, 0, 0, 0, d_used, d_silu, d_mul, d_hi, d_act, d_result)
                with act.Else():
                    moe()
                    for q in range(4):
                        act.wait_ge(h_ffn, 4 * NE + 4 + q + 1)
                        square(2 * q, 2)
                with act.If(l < 1):
                    split_hi(K_DENSE + ND - 1 + SPLIT, 0)
                def embed_input(units):
                    for i in units:
                        unit_wait(U_PP + i, l)
                        fn(pp_out[:, i, :], ubank(U_PP + i)[:, 0:S], ACT.Copy).then_inc(unit_act, 1)

                embed_input((0, 1, 2))
                rms(X_PLE, l)
                for j, units in enumerate(((3, 4), (5,), (6,), (7,))):
                    u_part(2, l, j)
                    embed_input(units)
                for c in (0, 1):
                    unit_wait(U_PP + 4 * c + 3, l)
                    split_hi(K_EMBED + SPLIT + c, embed_turns(l))
                for i in range(DT):
                    unit_wait(U_PG + i, l)
                    fn(gA[:, i, :], ubank(U_PG + i)[:, 0:S], ACT.Sigmoid).then_inc(unit_act, 1)
                    if i == 1:
                        split_hi(K_EMBED + 5, embed_turns(l))
                    if i in (3, 5):
                        with act.If(l < 1):
                            split_hi((i - 3) // 2, mixer_turns(1))
                    if i >= 1:
                        act.wait_ge(h_ready, 8 * l + 8 + i)
                        square(i - 1)
                act.wait_ge(h_ready, 8 * l + 8 + DT)
                square(DT - 1)
                rms(0, l + 1)
            act.wait_ge(row_ready, 4)
            act.dma_start(out.rearrange("(t p) n -> p t n", p=P), out_rows).then_inc(out_done, 16)
            act.wait_ge(out_done, 16)

        @block.gpsimd
        def _(pool):
            pool.memset(eps[:], EPS).then_inc(set_const, 1)
            for factor in q_factor + k_factor:
                last = pool.memset(factor[:], 1.0)
            last.then_inc(set_const, 1)

            def add_squares(norm, l):
                for k in range(1, POOLED):
                    pool.wait_ge(sq_ready, 24 * l + 8 * norm + k + 1)
                    last = pool.tensor_tensor(gA[:, 0, :], gA[:, 0, :], gA[:, k, :], ALU.add)
                    if k < POOLED - 1:
                        pool.drain()
                last.then_inc(pooled, 1)

            add_squares(0, 0)
            pool.wait_ge(bias_row_ready, 1)
            pool.dma_start(bias_rows_dram, bias_out.unsqueeze(1).to_broadcast([QH, P, 384])).then_inc(bias_rows_out, 16)
            pool.wait_ge(bias_rows_out, 16)
            both = bass.AP(tensor=bias_rows_dram.tensor, offset=P - 1, ap=[[383, P], [384 * P, QH], [1, 2 * P]])
            pool.dma_start(bias[:], both).then_inc(bias_in, 16)
            with pool.Fori(0, DEPTH) as l:
                pool.wait_ge(consts_in, 16)
                pool.wait_ge(setup_pe, 4 + DT // 2)
                pool.wait_ge(h_ready, 8 * l + 8)
                starts = scan_mask.unsqueeze(1).to_broadcast([P, HH * NCH, CHUNK])
                pool.tensor_tensor(chunk_starts.rearrange("p (c t) -> p c t", t=CHUNK), starts, starts,
                                   ALU.mult).then_inc(starts_ready, 1)
                for g in range(LEVELS):
                    if g == 0:
                        pool.wait_ge(factors_ready, l + 1)
                    else:
                        pool.drain()
                    earlier, size = (hF if g == 0 else k_level[g - 1]), CHUNK << g
                    keys = earlier[:] if g < 2 else earlier[:, :, 0:P]
                    factor = k_factor[g][:].rearrange("p (h b) -> p h b", h=HH)
                    if g == 2:
                        factor = factor[:, :, 0:2]
                    for h in range(HH):
                        last = pool.tensor_tensor(k_level[g][:, h, :].rearrange("p (b t) -> p b t", t=size),
                                                  keys[:, h, :].rearrange("p (b t) -> p b t", t=size),
                                                  factor[:, h, :].unsqueeze(2).to_broadcast([P, factor.shape[2], size]), ALU.mult)
                    last.then_inc(k_ready, 1)
                for i in range(DT):
                    await_unit_read(pool, U_YB + i, l)
                    pool.tensor_tensor(gA[:, i, :], gA[:, i, :], gB[:, i, :], ALU.add).then_inc(merged, 1)
                for norm in (1, 2, 3):
                    pool.drain()
                    add_squares(norm, l)

        @block.vector
        def _(dve):
            v = nc.vector

            dve.wait_ge(setup_pe, 1)
            raw = bank[0]
            v.tensor_copy(params[:, :, 0:VROWS], raw[:, 0:R_LB].rearrange("p (l n) -> p l n", l=DEPTH))
            v.tensor_copy(fin_gain[:], raw[:, R_FIN:R_FIN + DT])
            v.tensor_copy(lbt[:, 0:2, :], raw[:, R_LB:R_FIN].rearrange("p (l n) -> p l n", l=DEPTH))
            dve.drain()
            v.tensor_tensor(lbt[:, 2, :], lbt[:, 0, :], lbt[:, 1, :], ALU.max)
            dve.drain()
            for l in range(DEPTH):
                last = v.tensor_tensor(lbt[:, l, :], lbt[:, l, :], lbt[:, 2, :], ALU.subtract)
            last.then_inc(setup_dve, 1)
            for j in range(DT // 2):
                dve.wait_ge(setup_pe, 2 + j)
                v.tensor_copy(hT[:, 2 * j:2 * j + 2, :], bank[X_BANKS[j]][:].rearrange("p (k s) -> p k s", k=2)).then_inc(h_ready, 2)
            dve.wait_ge(setup_pe, 2 + DT // 2)
            dve.wait_ge(sc_in, 48)
            v.tensor_tensor(bias_out, bank[4][0:QH, 0:384], mask_row, ALU.add).then_inc(bias_row_ready, 1)
            dve.wait_ge(lb_exp, 1)
            v.tensor_tensor(lbt[:, 2, :], lbt[:, 0, :], lbt[:, 1, :], ALU.add)
            dve.drain()
            v.reciprocal(lbt[:, 2, :], lbt[:, 2, :])
            dve.drain()
            for l in range(DEPTH):
                v.tensor_tensor(lbt[:, l, :], lbt[:, l, :], lbt[:, 2, :], ALU.mult)
            dve.drain()
            v.tensor_tensor(lbt[:, 2, :], lbt[:, 0, :], lbt[:, 1, :], ALU.add)
            v.tensor_tensor(params[:, 0, LB:LB + HH], lbt[:, 0, :], lbt[:, 0, :], ALU.subtract)
            dve.drain()
            v.tensor_tensor(params[:, 1, LB:LB + HH], lbt[:, 2, :], lbt[:, 0, :], ALU.subtract)
            dve.drain()
            v.tensor_scalar(params[:, :, OMLB:OMLB + HH], params[:, :, LB:LB + HH], -1.0, 1.0, ALU.mult, ALU.add)
            dve.drain()

            def norm_tile(k, gains):
                return v.scalar_tensor_tensor(gB[:, k, :], hT[:, k, :], gains[:, k:k + 1], rstd[:], ALU.mult, ALU.mult)

            def norm_tiles(norm, l, gains):
                dve.wait_ge(rms_ready, 3 * l + norm + 1)
                for j in range(4):
                    norm_tile(2 * j, gains)
                    norm_tile(2 * j + 1, gains).then_inc(u_normed, 1)

            def stream_lo(norm, l):
                for j in range(4):
                    dve.wait_ge(u_hi_ready, 12 * l + 4 * norm + j + 1)
                    two = slice(2 * j, 2 * j + 2)
                    v.tensor_tensor(u_lo[:, two, :], gB[:, two, :], u_hi[:, two, :].bitcast(F32),
                                    ALU.subtract).then_inc(u_ready, 1)

            def normed(norm, l, gains):
                norm_tiles(norm, l, gains)
                stream_lo(norm, l)

            def split_lo(n, turns, size=HALF):
                for half in range(2):
                    raw, hi, lo = half_views(n, half, size)
                    dve.wait_ge(hi_done, 2 * n + half + 1 + RAW * turns)
                    v.tensor_tensor(lo, raw, hi.bitcast(F32), ALU.subtract).then_inc(lo_done, 1)

            def unit_wait(u, l):
                dve.wait_ge(unit_done, NU * l + u + 1)

            def aux_wait(u, l):
                dve.wait_ge(aux_done, NX * l + u + 1)

            def mixer(l):
                for stage, i in STEPS:
                    stage_work(stage, i, l)
                    used = chunk_used(stage, i)
                    if used is not None:
                        split_lo(used + SPLIT, mixer_turns(l))

            def stage_work(stage, i, l):
                if stage == "hq":
                    unit_wait(U_HQ + i, l)
                    v.tensor_copy(hQ[:, i, :], ubank(U_HQ + i)[:, 0:S]).then_inc(unit_dve, 1)
                elif stage == "gates":
                    await_unit_read(dve, U_HF + 3, l)
                    for h in range(HH):
                        v.tensor_scalar(hF[:, h, :], hF[:, h, :], gain[:, OMLB + h:OMLB + h + 1],
                                        gain[:, LB + h:LB + h + 1], ALU.mult, ALU.add)
                    dve.drain()
                    v.tensor_scalar(hK[:], hF[:], -1.0, 1.0, ALU.mult, ALU.add).then_inc(f_ready, 1)
                elif stage == "hi":
                    unit_wait(U_HI + i, l)
                    half, t = i // 2, i % 2
                    v.tensor_copy(hV[:, t, half * 256:half * 256 + 256], ubank(U_HI + i)[:, 0:S]).then_inc(unit_dve, 1)
                elif stage == "scan":
                    dve.wait_ge(logf_ready, l + 1)
                    dve.wait_ge(starts_ready, l + 1)
                    v.tensor_tensor_scan(hA[:].rearrange("p h s -> p (h s)"), chunk_starts,
                                         hF[:].rearrange("p h s -> p (h s)"), 0.0, ALU.mult, ALU.add).then_inc(scan_ready, 1)
                    dve.drain()
                    a = hA[:].rearrange("p h (c t) -> p (h c) t", t=CHUNK)
                    v.tensor_tensor(hF[:].rearrange("p h (c t) -> p (h c) t", t=CHUNK),
                                    a[:, :, CHUNK - 1:CHUNK].to_broadcast([P, HH * NCH, CHUNK]), a,
                                    ALU.subtract).then_inc(diff_ready, 1)
                elif stage == "decay":
                    dve.wait_ge(exp_ready, 3 * l + 3)
                    v.tensor_tensor(hF[:], hF[:], hK[:], ALU.mult)
                    v.tensor_copy(dec[0][:], hE[:].rearrange("p h (c t) -> p (h c) t", t=CHUNK)[:, :, CHUNK - 1])
                    dve.wait_ge(set_const, 2)
                    dve.drain()
                    for g in range(LEVELS):
                        by_two = lambda a: a[:].rearrange("p (b two) -> p b two", two=2)
                        d2, q2, k2 = by_two(dec[g]), by_two(q_factor[g]), by_two(k_factor[g])
                        v.tensor_copy(q2[:, :, 1], d2[:, :, 0])
                        last = v.tensor_copy(k2[:, :, 0], d2[:, :, 1])
                        if g < LEVELS - 1:
                            v.tensor_tensor(dec[g + 1][:], d2[:, :, 0], d2[:, :, 1], ALU.mult)
                            dve.drain()
                    last.then_inc(factors_ready, 1)
                    v.tensor_tensor(hKi[:], hKi[:], hK[:], ALU.mult)
                    v.tensor_tensor(hQ[:], hQ[:], hE[:], ALU.mult).then_inc(hgrn_ready, 1)
                elif stage == "levels":
                    for g in range(LEVELS):
                        dve.drain()
                        size = CHUNK << g
                        if g < 2:
                            out_, in_ = q_level[g][:].rearrange("p h s -> p (h s)"), (hQ if g == 0 else q_level[0])[:].rearrange("p h s -> p (h s)")
                            v.tensor_tensor(out_.rearrange("p (b t) -> p b t", t=size), in_.rearrange("p (b t) -> p b t", t=size),
                                            q_factor[g][:].unsqueeze(2).to_broadcast([P, HH * NCH >> g, size]),
                                            ALU.mult).then_inc(q_ready, 1)
                        else:
                            for h in range(HH):
                                factor = q_factor[g][:, 4 * h + 2:4 * h + 4].unsqueeze(2).to_broadcast([P, 2, size])
                                last = v.tensor_tensor(q_level[g][:, h, :].rearrange("p (b t) -> p b t", t=size),
                                                       q_level[1][:, h, P:S].rearrange("p (b t) -> p b t", t=size),
                                                       factor, ALU.mult)
                            last.then_inc(q_ready, 1)
                elif stage == "av":
                    unit_wait(U_AV + i, l)
                    v.tensor_copy(aV[:, i // 2, :], ubank(U_AV + i)[:, P:2 * P]).then_inc(unit_dve, 1)
                elif stage == "p":
                    h, part = i // 2, i % 2
                    u = nth("p", i)
                    dve.drain()
                    aux_wait(u, l)
                    got = xbank(u)[:].rearrange("p (g t n) -> p g t n", g=2, t=TT)
                    if part == 0:
                        v.tensor_copy(rstd[:].rearrange("p (t n) -> p t n", t=TT), got[:, 0])
                        v.tensor_tensor(pm[:, h], got[:, 1], pair_masks[:, 0:1, :].to_broadcast([P, TT, P]),
                                        ALU.mult).then_inc(aux_dve, 1)
                    else:
                        for g in range(2):
                            last = v.tensor_tensor(pm_part[:, g], got[:, g],
                                                   pair_masks[:, g + 1:g + 2, :].to_broadcast([P, TT, P]), ALU.mult)
                        last.then_inc(aux_dve, 1)
                        for g in range(2):
                            dve.drain()
                            v.tensor_tensor(pm[:, h], pm[:, h], pm_part[:, g], ALU.add)
                        dve.drain()
                        v.copy_predicated(pm[:, h], hg_mask.bitcast(U32).unsqueeze(1).to_broadcast([P, TT, P]),
                                          rstd[:].rearrange("p (t n) -> p t n", t=TT)).then_inc(pm_ready, 1)
                elif stage == "sc":
                    u = nth("sc", i)
                    dve.wait_ge(bias_in, 16)
                    aux_wait(u, l)
                    v.tensor_tensor(sc[:, i, 0:P], xbank(u)[:, 0:P], bias[:, i, P:2 * P], ALU.add)
                    v.tensor_tensor(sc[:, i, P:P + S], xbank(u)[:, P:P + S], bias[:, i, :], ALU.add).then_inc(aux_dve, 1)
                elif stage == "softmax":
                    dve.wait_ge(small_in, 32)
                    dve.drain()
                    v.tensor_reduce(smax[:, 0, 0:QH], sc[:, :, 0:P], AX.X, ALU.max)
                    v.tensor_reduce(smax[:, 0, QH:2 * QH], sc[:, :, P:P + S], AX.X, ALU.max)
                    dve.drain()
                    own_sink = sink[:, bass.ds(l, 1), :].to_broadcast([P, 2, QH])
                    top = smax[:, 0, :].rearrange("p (b h) -> p b h", b=2)
                    v.tensor_tensor(top, top, own_sink, ALU.max)
                    dve.drain()
                    v.tensor_scalar(smax[:, 1, :], smax[:, 0, :], -1.0, None, ALU.mult)
                    v.tensor_tensor(smax[:, 3, :].rearrange("p (b h) -> p b h", b=2), own_sink, top, ALU.subtract)
                    dve.drain()
                    v.tensor_copy(smax[:, 5, :], smax[:, 1, :]).then_inc(max_ready, 1)
                elif stage == "probs":
                    dve.wait_ge(exp_done, l + 1)
                    v.tensor_tensor(smax[:, 4, :], smax[:, 2, :], smax[:, 3, :], ALU.add)
                    dve.drain()
                    v.reciprocal(smax[:, 4, :], smax[:, 4, :])
                    dve.drain()
                    v.tensor_tensor(sc[:, :, 0:P], sc[:, :, 0:P],
                                    smax[:, 4, 0:QH].unsqueeze(2).to_broadcast([P, QH, P]), ALU.mult)
                    v.tensor_tensor(sc[:, :, P:P + S], sc[:, :, P:P + S],
                                    smax[:, 4, QH:2 * QH].unsqueeze(2).to_broadcast([P, QH, S]),
                                    ALU.mult).then_inc(prob_ready, 1)
                elif stage == "pv":
                    u = nth("pv", i)
                    aux_wait(u, l)
                    v.tensor_copy(aO[:, i, :], xbank(u)[:, 0:S]).then_inc(aux_dve, 1)
                elif stage == "ynorm":
                    dve.wait_ge(orms_ready, 2 * l + 2)
                    v.tensor_tensor(hO[:], hO[:], hE[:], ALU.mult)
                    dve.drain()
                    v.scalar_tensor_tensor(hO[:], hO[:], gain[:, G_HN:G_HN + 1], hG[:], ALU.mult,
                                           ALU.mult).then_inc(yb_ready, 1)
                elif stage == "ya":
                    await_unit_read(dve, U_GA + i, l)
                    unit_wait(U_YA + i, l)
                    v.tensor_tensor(gA[:, i, :], gA[:, i, :], ubank(U_YA + i)[:, 0:S], ALU.mult).then_inc(unit_dve, 1)
                elif stage == "yb":
                    await_unit_read(dve, U_GB + i, l)
                    unit_wait(U_YB + i, l)
                    v.tensor_tensor(gB[:, i, :], gB[:, i, :], ubank(U_YB + i)[:, 0:S], ALU.mult).then_inc(unit_dve, 1)
                elif stage == "branch":
                    dve.wait_ge(branch_hi, 2 * l + i + 1)
                    part = slice(4 * i, 4 * i + 4)
                    v.tensor_tensor(br_lo[:, part, :], (aO if i == 0 else hO)[:], br_hi[:, part, :].bitcast(F32),
                                    ALU.subtract).then_inc(branch_ready, 1)
                elif stage == "merge":
                    dve.wait_ge(merge_hi, 4 * l + i + 1)
                    part = slice(2 * i, 2 * i + 2)
                    v.tensor_tensor(u_lo[:, part, :], gA[:, part, :], u_hi[:, part, :].bitcast(F32),
                                    ALU.subtract).then_inc(merge_ready, 1)
                elif stage == "wo":
                    unit_wait(U_WO + i, l)
                    v.tensor_tensor(hT[:, i, :], hT[:, i, :], ubank(U_WO + i)[:, 0:S], ALU.add).then_inc(unit_dve, 1)

            def swiglu_all(order, n0, turns, pairs0, chunks0, used, silu_sem, mul_sem, hi_sem, act_ready, by_gate, result=None):
                for i, (m, j) in enumerate(order):
                    if result and i == len(order) - 1:
                        for q in range(4):
                            dve.wait_ge(result, q + 1)
                            add_to_h(q)
                    if m == "w3":
                        dve.wait_ge(used, chunks0 + i + 1)
                        dve.wait_ge(silu_sem, pairs0 + j + 1)
                        w3u = bank[2 * (j % 2) + 1][:].rearrange("p (a s) -> p a s", a=2)
                        last = v.tensor_tensor(act2[:, j % 2], act2[:, j % 2], w3u, ALU.mult)
                        if by_gate:
                            dve.drain()
                            last = v.tensor_tensor(act2[:, j % 2], act2[:, j % 2],
                                                   gate_row[:].unsqueeze(1).to_broadcast([P, 2, S]), ALU.mult)
                        last.then_inc(mul_sem, 1)
                    if not (result and i == len(order) - 1):
                        split_lo(n0 + i + SPLIT, turns)
                    if m == "w3":
                        dve.wait_ge(hi_sem, pairs0 + j + 1)
                        v.tensor_tensor(act_lo[:, j % 2], act2[:, j % 2], act_hi[:, j % 2].bitcast(F32),
                                        ALU.subtract).then_inc(act_ready, 1)

            def gate_slots(e):
                for t in range(TT):
                    last = v.tensor_scalar(gate_slot[:, t, :], slot_iota, pos[:, t, bass.ds(e, 1)],
                                           gate[:, t, bass.ds(e, 1)], ALU.is_equal, ALU.mult)
                last.then_inc(slots_ready, 1)

            def sel_slots(at):
                for t in range(TT):
                    last = v.tensor_scalar(sel_slot[:, t, :], slot_iota, pos_wide[:, t, at], picked_wide[:, t, at],
                                           ALU.is_equal, ALU.mult)
                last.then_inc(slots_ready, 1)

            def copy_slots(n):
                for half in range(2):
                    dve.wait_ge(gathered, 2 * n + half + 1)
                    last = v.tensor_copy(us[:, 4 * half:4 * half + 4, :], bank[4 + half][:].rearrange("p (d n) -> p d n", d=4))
                last.then_inc(us_copied, 1)

            def slots_lo(n):
                dve.wait_ge(us_hi_ready, n + 1)
                v.tensor_tensor(us_lo[:], us[:], us_hi[:].bitcast(F32), ALU.subtract).then_inc(us_ready, 1)

            def combined(e, part):
                for j in (2 * part, 2 * part + 1):
                    dve.wait_ge(comb_done, 4 * e + j + 1)
                    v.tensor_tensor(hT[:, 2 * j:2 * j + 2, :], hT[:, 2 * j:2 * j + 2, :],
                                    bank[4 + j % 2][:].rearrange("p (k s) -> p k s", k=2), ALU.add).then_inc(h_ffn, 1)

            def expert(e):
                def lo_of_turned(j):
                    dve.wait_ge(m_hi, PAIRS * e + j + 1)
                    v.tensor_tensor(act_lo[:, j % 2, :, 0:P], bank[j % 2][:, 0:2 * P].rearrange("p (a s) -> p a s", a=2),
                                    act_hi[:, j % 2, :, 0:P].bitcast(F32), ALU.subtract).then_inc(m_act, 1)

                for i, (m, j) in enumerate(EXPERT):
                    if m == "w3":
                        dve.wait_ge(m_used, NX_E * e + i + 1)
                        dve.wait_ge(m_silu, PAIRS * e + j + 1)
                        v.tensor_tensor(slot_act[:, j % 2], slot_act[:, j % 2], bank[2 + j % 2][:, 0:2 * P],
                                        ALU.mult).then_inc(m_mul, 1)
                    if m == "w3" and j == PAIRS - 1:
                        slots_lo(e + 1)
                    if m == "w2" and j == PAIRS - 1:
                        dve.wait_ge(m_used, NX_E * e + i + 1)
                        v.tensor_copy(y_tok[:, 512:1024], bank[7][:]).then_inc(y_dve, 1)
                    split_lo(K_EXPERTS + i + SPLIT, NX_E // SPLIT * e)
                    if m == "w1" and j in (2, 3):
                        combined(e, j - 2)
                    if m == "w1" and j == 4:
                        gate_slots(e)
                    if m == "w1" and j == 5:
                        dve.wait_ge(comb_tr, e + 1)
                        v.tensor_copy(comb[:], bank[4][:, 0:S]).then_inc(comb_ready, 1)
                    if m == "w1" and j == 6:
                        sel_slots(bass.ds(e + 1, 1))
                    if m == "w1" and j == 8:
                        copy_slots(e + 1)
                    if m == "w1" and j >= 1:
                        lo_of_turned(j - 1)
                    if m == "w3" and j == PAIRS - 1:
                        lo_of_turned(j)

            def add_to_h(j):
                v.tensor_tensor(hT[:, 2 * j:2 * j + 2, :], hT[:, 2 * j:2 * j + 2, :],
                                bank[4 + j][:].rearrange("p (k s) -> p k s", k=2), ALU.add).then_inc(h_ffn, 1)

            def moe(remainders):
                v.memset(rt[:], 0.0)
                dve.drain()
                dve.wait_ge(r_pe, 1)
                v.tensor_copy(logit_T[:], bank[4][0:NE, 0:S]).then_inc(logits_copied, 1)
                dve.wait_ge(r_pe, 2)
                v.tensor_copy(logit, bank[5][:, 32:32 + TT * NE].rearrange("p (t e) -> p t e", t=TT))
                dve.drain()
                for t in range(TT):
                    v.max(top8[:, t, :], logit[:, t, :])
                dve.drain()
                for t in range(TT):
                    v.max_index(idx8[:, t, :], top8[:, t, :], logit[:, t, :])
                dve.drain()
                v.tensor_copy(idxf, idx8[:])
                dve.drain()
                for t in range(TT):
                    v.tensor_scalar(tmp8[:, t, :], expert_iota, idxf[:, t, 0:1], None, ALU.is_equal)
                    v.tensor_scalar(picked[:, t, :], expert_iota, idxf[:, t, 1:2], None, ALU.is_equal)
                    v.tensor_scalar(ex[:, t, :], logit[:, t, :], top8[:, t, 0:1], None, ALU.subtract)
                dve.drain()
                v.tensor_tensor(picked, picked, tmp8, ALU.add).then_inc(r_dve, 1)
                dve.drain()
                v.tensor_tensor(ex, ex, picked, ALU.mult).then_inc(r_dve, 1)
                dve.wait_ge(r_act, 5)
                v.tensor_tensor(gate, ex, picked, ALU.mult)
                dve.drain()
                v.tensor_reduce(den[:], gate, AX.X, ALU.add)
                dve.drain()
                v.reciprocal(den[:], den[:])
                dve.drain()
                for t in range(TT):
                    v.tensor_scalar(gate[:, t, :], gate[:, t, :], den[:, t:t + 1], None, ALU.mult)
                dve.wait_ge(r_pe, 3)
                v.tensor_copy(pos, bank[5][:, 0:16].rearrange("p (t e) -> p t e", t=TT))
                v.tensor_copy(cnt[:], bank[5][:, 16:24])
                dve.drain()
                v.tensor_reduce(flag[:], cnt[:], AX.X, ALU.max).then_inc(route_ready, 1)
                dve.wait_ge(route_ready, 1)
                fullest = dve.value_load(flag[0:1, 0:1], min_val=0, max_val=S)
                with dve.If(fullest <= CAP):
                    v.memset(y_tok[:, 512:1024], 0.0).then_inc(y_dve, 1)
                    v.memset(comb[:], 0.0).then_inc(comb_ready, 1)
                    v.memset(slot_act[:, 0], 0.0).then_inc(m_mul, 2)
                    v.memset(slot_act[:, 1], 0.0).then_inc(m_act, 2)
                    sel_slots(slice(0, 1))
                    copy_slots(0)
                    slots_lo(0)
                    remainders()
                    with dve.Fori(0, NE) as e:
                        expert(e)
                    for part in range(2):
                        combined(NE, part)
                with dve.Else():
                    remainders()
                    with dve.Fori(0, NE) as e:
                        for t in range(TT):
                            last = v.tensor_scalar(gate_cols[:, t, :], ones, gate[:, t, bass.ds(e, 1)], None, ALU.mult)
                        last.then_inc(slots_ready, 1)
                        dve.wait_ge(gathered, e + 1)
                        v.tensor_copy(gate_row[:], bank[0][:, 0:S]).then_inc(us_copied, 1)
                        dve.drain()
                        swiglu_all(EXPERT, K_EXPERTS, NX_E // SPLIT * e, PAIRS * e, NX_E * e, m_used, m_silu, m_mul, m_hi,
                                   m_act, True)
                        dve.wait_ge(m_used, NX_E * e + NX_E)
                        for j in range(4):
                            add_to_h(j)
                        dve.drain()
                    v.memset(y_tok[:, 0:1], 0.0).then_inc(h_ffn, 4)
                dve.drain()

            split_lo(0, 0)
            with dve.Fori(0, DEPTH) as l:
                v.tensor_copy(gain[:], params[:, bass.ds(l, 1), :].rearrange("p a n -> p (a n)"))
                dve.drain()
                normed(0, l, gain[:, G_MIX:G_MIX + DT])
                with dve.If(l < 1):
                    for n in range(DEPTH):
                        dve.wait_ge(setup_pe, 3 + DT // 2 + n)
                        v.tensor_copy(p_T[:, n], bank[P_BANKS[n]][:].rearrange("p (k s) -> p k s", k=KP)).then_inc(p_turned, 1)
                    split_lo(1, 0)
                split_lo(2, mixer_turns(l))
                mixer(l)
                norm_tiles(1, l, gain[:, G_FFN:G_FFN + DT])

                def remainders():
                    stream_lo(1, l)
                    split_lo(NM - 1 + SPLIT, mixer_turns(l))
                    dve.wait_ge(p_hi_ready, l + 1)
                    v.tensor_tensor(p_lo[:], p_T[:, bass.ds(l, 1)].rearrange("p a k s -> p (a k) s"), p_hi[:].bitcast(F32),
                                    ALU.subtract).then_inc(p_split, 1)

                with dve.If(l < 1):
                    remainders()
                    swiglu_all(DENSE, K_DENSE, 0, 0, 0, d_used, d_silu, d_mul, d_hi, d_act, False, d_result)
                with dve.Else():
                    moe(remainders)
                with dve.If(l < 1):
                    split_lo(K_DENSE + ND - 1 + SPLIT, 0)
                normed(2, l, gain[:, G_PLE:G_PLE + DT])
                for c in (0, 1):
                    split_lo(K_EMBED + SPLIT + c, embed_turns(l))
                for i in range(DT):
                    await_unit_read(dve, U_PG + i, l)
                    v.tensor_tensor(gA[:, i, :], gA[:, i, :], pp_out[:, i, :], ALU.mult)
                    dve.drain()
                    v.tensor_tensor(hT[:, i, :], hT[:, i, :], gA[:, i, :], ALU.add).then_inc(h_ready, 1)
                    if i == 1:
                        split_lo(K_EMBED + 5, embed_turns(l))
                    if i in (3, 5):
                        with dve.If(l < 1):
                            split_lo((i - 3) // 2, mixer_turns(1))
                dve.drain()
            dve.wait_ge(rms_ready, 3 * DEPTH + 1)
            for k in range(DT):
                norm_tile(k, fin_gain[:]).then_inc(fin_ready, 1)
            dve.wait_ge(fin_tr, 1)
            for t in range(TT):
                for half in range(2):
                    b = bank[4 + half] if t == 0 else bank[6 + half]
                    v.tensor_copy(out_rows[:, t, 512 * half:512 * half + 512], b[:]).then_inc(row_ready, 1)


def constants():
    c = np.zeros((P, C_N), np.float32)
    i = np.arange(P)
    c[:, C_ID:C_ID + P] = np.eye(P)
    c[:, C_ONE:C_ONE + P] = 1
    c[:, C_LT:C_LT + P] = i[:, None] < i[None, :]
    c[:, C_HM:C_HM + P] = (i[:, None] // CHUNK == i[None, :] // CHUNK) & (i[:, None] <= i[None, :])
    for g in range(LEVELS):
        b = i // (CHUNK << g)
        c[:, C_PM + g * P:C_PM + (g + 1) * P] = (b[None, :] % 2 == 1) & (b[:, None] == b[None, :] - 1)
    c[:, C_IO:C_IO + CAP] = np.arange(CAP)
    c[:, C_SC:C_SC + CHUNK] = np.arange(CHUNK) != 0
    c[:, C_I8:C_I8 + NE] = np.arange(NE)
    return c


def bias_tables():
    dist = 2 * P - 1 - np.arange(384)
    exact = BUCKETS // 2
    d = np.maximum(dist, 0)
    large = exact + (np.log(np.maximum(d, 1).astype(np.float32) / np.float32(exact)) / np.float32(np.log(MAX_DIST / exact))
                     * np.float32(BUCKETS - exact)).astype(np.int32)
    bucket = np.where(d < exact, d, np.minimum(large, BUCKETS - 1))
    inside = (dist >= 0) & (dist < P)
    onehot = ((np.arange(BUCKETS)[:, None] == bucket) & inside).astype(np.float32)
    outside = np.broadcast_to(np.where(inside, 0, NEG).astype(np.float32), (QH, 384))
    return onehot, np.ascontiguousarray(outside)


def kernel(**inputs):
    import concourse.bacc as bacc
    from concourse.bass_utils import run_bass_kernel_spmd

    a = {k: np.asarray(v) for k, v in inputs.items()}
    rows = []
    for l in range(DEPTH):
        for n in ("norm_mix", "norm_ffn", "norm_ple", "hgrn_norm"):
            rows.append(a[n][l].reshape(-1, P))
    rows += [a["lb_logits"].reshape(-1, P), a["final_norm"].reshape(-1, P)]
    onehot, outside = bias_tables()
    arrays = {
        "x": a["x"][0], "p": a["p"][:, 0], "w_in": a["w_in"], "sinks": a["sinks"], "rel_bias": a["rel_bias"],
        "vectors": np.concatenate(rows), "w_branch_a": a["w_branch_a"], "w_branch_b": a["w_branch_b"],
        "w_out": a["w_out"], "dense_w1": a["dense_w1"], "dense_w3": a["dense_w3"], "dense_w2": a["dense_w2"],
        "router_w": a["router_w"], "moe_w1": a["moe_w1"], "moe_w3": a["moe_w3"], "moe_w2": a["moe_w2"],
        "ple_proj": a["ple_proj"], "ple_gate": a["ple_gate"], "consts": constants(), "buckets": onehot,
        "outside": outside,
    }
    nc = bacc.Bacc("TRN2", target_bir_lowering=False, num_devices=1)
    handles = {n: nc.dram_tensor(n, v.shape, F32, kind="ExternalInput").ap() for n, v in arrays.items()}
    out = nc.dram_tensor("out", (S, D), F32, kind="ExternalOutput").ap()
    trunk(nc, *handles.values(), out)
    r = run_bass_kernel_spmd(nc, [{n: np.ascontiguousarray(v) for n, v in arrays.items()}], core_ids=[0])
    return r.results[0]["out"].reshape(1, S, D)
```
